# Optimizing a Trainium2 kernel written in Bass

```python
import jax, jax.numpy as jnp
from jax import lax
import numpy as np

D_MODEL = 1024
BATCH = 1
SEQ = 1024
DEPTH = 1
DEC_BATCH = 8
DEC_SEQ = 4
PAST_LEN = 8192
PAGE_SIZE = 128

BRANCH_WIDTH = D_MODEL // 2
N_BRANCHES = 3
CONV_A_WIDTH = 31
CONV_A_GROUPS = 8
SGU_CHUNK = 128
SGU_HEADS = 8
CONV_C_WIDTH = 3
N_GROUPS = 4
EXPERTS_PER_GROUP = 8
N_EXPERTS = N_GROUPS * EXPERTS_PER_GROUP
TOP_K = 2
D_FF_EXPERT = D_MODEL // 2
MOE_BLOCK = 128
IN_COLS = 7 * BRANCH_WIDTH + N_BRANCHES * D_MODEL
EPS = 1e-6

kernel_name = "hybrid_conv_sgu_shortconv_hmoe_step"

def rms_norm(x, g):
    xf = x.astype(jnp.float32)
    y = xf * lax.rsqrt(jnp.mean(xf * xf, axis=-1, keepdims=True) + EPS)
    return (y * g.astype(jnp.float32)).astype(x.dtype)

def layer_norm(x, g, b, n_groups=1):
    shp = x.shape
    xf = x.astype(jnp.float32).reshape(shp[:-1] + (n_groups, shp[-1] // n_groups))
    mu = jnp.mean(xf, axis=-1, keepdims=True)
    xc = xf - mu
    var = jnp.mean(xc * xc, axis=-1, keepdims=True)
    y = (xc * lax.rsqrt(var + EPS)).reshape(shp)
    return (y * g.astype(jnp.float32) + b.astype(jnp.float32)).astype(x.dtype)

def causal_dwconv(x, hist, w):
    k = w.shape[0]
    xp = jnp.concatenate([hist.astype(x.dtype), x], axis=1)
    y = lax.conv_general_dilated(xp, w[:, None, :].astype(x.dtype), window_strides=(1,),
                                 padding='VALID', dimension_numbers=('NWC', 'WIO', 'NWC'),
                                 feature_group_count=x.shape[-1])
    return y, xp[:, -(k - 1):]

def chunk_spatial_mix(v, w_s, b_s):
    n, t, c = v.shape
    n_chunks = -(-t // SGU_CHUNK)
    pad = n_chunks * SGU_CHUNK - t
    vp = jnp.pad(v, ((0, 0), (0, pad), (0, 0))).reshape(n, n_chunks, SGU_CHUNK, SGU_HEADS, c // SGU_HEADS)
    mask = jnp.tril(jnp.ones((SGU_CHUNK, SGU_CHUNK), dtype=bool))
    w = jnp.where(mask[None], w_s, 0).astype(v.dtype)
    s = jnp.einsum('hts,bnshd->bnthd', w, vp) + b_s.T.astype(v.dtype)[None, None, :, :, None]
    return s.reshape(n, n_chunks * SGU_CHUNK, c)[:, :t]

def hier_moe(h, w_rg, b_rg, w_re, b_re, w1, w3, w2):
    t, d = h.shape
    hf = h.astype(jnp.float32)
    tok = jnp.arange(t, dtype=jnp.int32)
    g_logits = hf @ w_rg.astype(jnp.float32) + b_rg.astype(jnp.float32)
    g_prob = jax.nn.softmax(g_logits, axis=-1)
    g_sel = jnp.argmax(g_logits, axis=-1).astype(jnp.int32)
    e_logits = (hf @ w_re.astype(jnp.float32) + b_re.astype(jnp.float32)).reshape(t, N_GROUPS, EXPERTS_PER_GROUP)
    e_in = e_logits[tok, g_sel]
    top_v, top_i = lax.top_k(e_in, TOP_K)
    gate = jax.nn.softmax(top_v, axis=-1) * g_prob[tok, g_sel][:, None]
    expert = g_sel[:, None] * EXPERTS_PER_GROUP + top_i.astype(jnp.int32)

    a = t * TOP_K
    e_flat = expert.reshape(a)
    tok_flat = jnp.repeat(tok, TOP_K)
    order = jnp.argsort(e_flat)
    e_sorted = e_flat[order]
    tok_sorted = tok_flat[order]
    w_sorted = gate.reshape(a)[order]
    counts = jnp.zeros((N_EXPERTS,), jnp.int32).at[e_flat].add(1)
    starts = jnp.cumsum(counts) - counts
    padded = (counts + MOE_BLOCK - 1) // MOE_BLOCK * MOE_BLOCK
    pends = jnp.cumsum(padded)
    pstarts = pends - padded
    dest = pstarts[e_sorted] + (jnp.arange(a, dtype=jnp.int32) - starts[e_sorted])
    n_blocks = -(-a // MOE_BLOCK) + N_EXPERTS
    rows = jnp.zeros((n_blocks * MOE_BLOCK, d), h.dtype).at[dest].set(h[tok_sorted])
    block_e = jnp.minimum(jnp.searchsorted(pends, jnp.arange(n_blocks, dtype=jnp.int32) * MOE_BLOCK,
                                           side='right'), N_EXPERTS - 1)

    def expert_block(args):
        xb, e = args
        return (jax.nn.silu(xb @ w1[e]) * (xb @ w3[e])) @ w2[e]

    y_rows = lax.map(expert_block, (rows.reshape(n_blocks, MOE_BLOCK, d), block_e)).reshape(n_blocks * MOE_BLOCK, d)
    contrib = y_rows[dest] * w_sorted[:, None].astype(y_rows.dtype)
    return jnp.zeros((t, d), y_rows.dtype).at[tok_sorted].add(contrib)

def trunk_layer(x, c, hist_a, hist_c, norm1_g, norm2_g, w_ada, b_ada, w_in, a_dw_w, a_dw_b,
                a_norm_g, a_norm_b, b_norm_g, b_norm_b, b_spatial_w, b_spatial_b, c_conv_w,
                w_branch, w_out, w_router_g, b_router_g, w_router_e, b_router_e, w1, w3, w2):
    n, t, d = x.shape
    wd = BRANCH_WIDTH
    mod = (jax.nn.silu(c) @ w_ada + b_ada)[:, None, :]
    sh1, sc1, g1, sh2, sc2, g2 = jnp.split(mod, 6, axis=-1)

    h = rms_norm(x, norm1_g) * (1 + sc1) + sh1
    z = h @ w_in
    a_val, a_gt, b_u, b_v, c_b, c_c, c_h, gates = jnp.split(z, [wd * i for i in range(1, 8)], axis=-1)

    a = a_val * jax.nn.sigmoid(a_gt)
    a, new_hist_a = causal_dwconv(a, hist_a, a_dw_w)
    a = jax.nn.silu(layer_norm(a + a_dw_b, a_norm_g, a_norm_b, CONV_A_GROUPS))

    u = jax.nn.gelu(b_u)
    v = layer_norm(jax.nn.gelu(b_v), b_norm_g, b_norm_b)
    bb = u * chunk_spatial_mix(v, b_spatial_w, b_spatial_b)

    ch, new_hist_c = causal_dwconv(c_c * c_h, hist_c, c_conv_w)
    cc = c_b * ch

    br = jnp.einsum('ntgc,gcd->ntgd', jnp.stack([a, bb, cc], axis=2), w_branch)
    gsig = jax.nn.sigmoid(gates.reshape(n, t, N_BRANCHES, d))
    mixed = jnp.sum(gsig * br, axis=2) @ w_out
    x = x + g1 * mixed

    h2 = rms_norm(x, norm2_g) * (1 + sc2) + sh2
    y = hier_moe(h2.reshape(n * t, d), w_router_g, b_router_g, w_router_e, b_router_e, w1, w3, w2)
    x = x + g2 * y.reshape(n, t, d).astype(x.dtype)
    return x, new_hist_a, new_hist_c, v

def setup_inputs(seed: int = 0) -> dict:
    key = jax.random.key(seed)
    k = jax.random.split(key, 30)
    L, D, W, E, F = DEPTH, D_MODEL, BRANCH_WIDTH, N_EXPERTS, D_FF_EXPERT
    f32 = jnp.float32

    def nrm(i, shape, s):
        return jax.random.normal(k[i], shape, f32) * s

    return {
        "x_prompt": nrm(0, (BATCH, SEQ, D), 1.0),
        "x_sample": nrm(1, (DEC_BATCH, DEC_SEQ, D), 1.0),
        "c_prompt": nrm(2, (BATCH, D), 1.0),
        "c_sample": nrm(3, (DEC_BATCH, D), 1.0),
        "state_conv_a": nrm(4, (L, DEC_BATCH, CONV_A_WIDTH - 1, W), 0.5),
        "state_conv_c": nrm(5, (L, DEC_BATCH, CONV_C_WIDTH - 1, W), 1.0),
        "norm1_g": 1.0 + nrm(6, (L, D), 0.02),
        "norm2_g": 1.0 + nrm(7, (L, D), 0.02),
        "w_ada": nrm(8, (L, D, 6 * D), 0.3 * D ** -0.5),
        "b_ada": nrm(9, (L, 6 * D), 0.02),
        "w_in": nrm(10, (L, D, IN_COLS), D ** -0.5),
        "a_dw_w": nrm(11, (L, CONV_A_WIDTH, W), CONV_A_WIDTH ** -0.5),
        "a_dw_b": nrm(12, (L, W), 0.02),
        "a_norm_g": 1.0 + nrm(13, (L, W), 0.02),
        "a_norm_b": nrm(14, (L, W), 0.02),
        "b_norm_g": 1.0 + nrm(15, (L, W), 0.02),
        "b_norm_b": nrm(16, (L, W), 0.02),
        "b_spatial_w": nrm(17, (L, SGU_HEADS, SGU_CHUNK, SGU_CHUNK), SGU_CHUNK ** -0.5),
        "b_spatial_b": 1.0 + nrm(18, (L, SGU_HEADS, SGU_CHUNK), 0.02),
        "c_conv_w": nrm(19, (L, CONV_C_WIDTH, W), CONV_C_WIDTH ** -0.5),
        "w_branch": nrm(20, (L, N_BRANCHES, W, D), W ** -0.5),
        "w_out": nrm(21, (L, D, D), D ** -0.5),
        "w_router_g": nrm(22, (L, D, N_GROUPS), D ** -0.5),
        "b_router_g": nrm(23, (L, N_GROUPS), 0.01),
        "w_router_e": nrm(24, (L, D, E), D ** -0.5),
        "b_router_e": nrm(25, (L, E), 0.01),
        "w1": nrm(26, (L, E, D, F), D ** -0.5),
        "w3": nrm(27, (L, E, D, F), D ** -0.5),
        "w2": nrm(28, (L, E, F, D), F ** -0.5),
        "final_norm_g": 1.0 + nrm(29, (D,), 0.02),
    }

def reference(x_prompt, x_sample, c_prompt, c_sample, state_conv_a, state_conv_c,
              norm1_g, norm2_g, w_ada, b_ada, w_in, a_dw_w, a_dw_b, a_norm_g, a_norm_b,
              b_norm_g, b_norm_b, b_spatial_w, b_spatial_b, c_conv_w, w_branch, w_out,
              w_router_g, b_router_g, w_router_e, b_router_e, w1, w3, w2, final_norm_g):
    xp, xs = x_prompt, x_sample
    pa, pc, sa, sc, sv = [], [], [], [], []
    for l in range(DEPTH):
        lp = [p[l] for p in (norm1_g, norm2_g, w_ada, b_ada, w_in, a_dw_w, a_dw_b, a_norm_g, a_norm_b,
                             b_norm_g, b_norm_b, b_spatial_w, b_spatial_b, c_conv_w, w_branch, w_out,
                             w_router_g, b_router_g, w_router_e, b_router_e, w1, w3, w2)]
        hza = jnp.zeros((xp.shape[0], CONV_A_WIDTH - 1, BRANCH_WIDTH), xp.dtype)
        hzc = jnp.zeros((xp.shape[0], CONV_C_WIDTH - 1, BRANCH_WIDTH), xp.dtype)
        xp, ha, hc, _ = trunk_layer(xp, c_prompt, hza, hzc, *lp)
        pa.append(ha)
        pc.append(hc)
        xs, ha_s, hc_s, v_s = trunk_layer(xs, c_sample, state_conv_a[l], state_conv_c[l], *lp)
        sa.append(ha_s)
        sc.append(hc_s)
        sv.append(v_s)
    y_prompt = rms_norm(xp, final_norm_g)
    y_sample = rms_norm(xs, final_norm_g)
    new_conv_a_prompt = jnp.stack(pa)
    new_conv_c_prompt = jnp.stack(pc)
    new_conv_a_sample = jnp.stack(sa)
    new_conv_c_sample = jnp.stack(sc)
    new_sgu_v_sample = jnp.stack(sv)
    return (y_prompt, y_sample, new_conv_a_prompt, new_conv_c_prompt, new_conv_a_sample, new_conv_c_sample, new_sgu_v_sample)


_drawn_inputs = setup_inputs


def setup_inputs(seed=0):
    import zlib

    import numpy as np

    out = dict(_drawn_inputs(seed))
    spreads = {}
    factors = {'norm2_g': 6.913,
     'a_dw_b': 8.0,
     'a_norm_g': 8.0,
     'a_norm_b': 8.0,
     'b_norm_g': 2.907,
     'b_norm_b': 2.8,
     'b_spatial_b': 8.0,
     'b_router_g': 8.0,
     'b_router_e': 8.0,
     'final_norm_g': 2.92}
    for name, (base, spread) in spreads.items():
        noise = np.random.default_rng([zlib.crc32(name.encode()), seed]).standard_normal(out[name].shape)
        drawn = base * np.exp(spread * noise) if base else spread * noise
        out[name] = __import__('jax').numpy.asarray(drawn.astype(out[name].dtype))
    for name, factor in factors.items():
        out[name] = (out[name] * factor).astype(out[name].dtype)
    return out
```

```python
import numpy as np

import concourse.bass as bass
from concourse import mybir
from contextlib import ExitStack

F32 = mybir.dt.float32
F32R = mybir.dt.float32r
BF16 = mybir.dt.bfloat16
I32 = mybir.dt.int32
U32 = mybir.dt.uint32
ALU = mybir.AluOpType
ACT = mybir.ActivationFunctionType
AX = mybir.AxisListType

P = 128
D = 1024
KD = D // P
W = D // 2
CW = W // P
SEQ, NS, TS = 1024, 8, 4
SMP = NS * TS
HALF = SEQ // 2
PT = HALF // P
TOK = SEQ + SMP
NT = 2 * PT + 1
KA, KC = 31, 3
HA, HC = KA - 1, KC - 1
HEADS = 8
NE, NG, EG, FF = 32, 4, 8, 512
NR = NG + NE
KF = FF // P
EPS = 1e-6
NB_A, NB_C, NB_B = 0, 2, 1
GELU0 = 1.5957691216057308
GELU1 = GELU0 * 0.044715
MAGIC = 0x5F375A86
BIG = 3.0e38
TPAD = 2048
NBLK = 9
OOB = 4 * TPAD - 1
MAXX = 16

A0, C0, B0 = 0, 2 * CW, 5 * CW
GC0 = B0 + 2 * CW
GB0 = GC0 + 2 * KD
GA0 = GB0 + 2 * KD
O0 = GA0 + 2 * KD
NI = O0 + KD
NSPLIT = O0
AS, CS = HA + TS, HC + TS
NPAR = KA + KC + 3 + NS * HC
PAR_B, PAR_G, PAR_S, PAR_H = KA + KC, KA + KC + 1, KA + KC + 2, KA + KC + 3
N_PAR = 25
N_RT = 12
N_CONST = 17
COL = dict(a_val=0, a_gt=W, b_u=2 * W, b_v=3 * W, c_b=4 * W, c_c=5 * W, c_h=6 * W, gates=7 * W)


def build(nc, x_prompt, x_sample, c_prompt, c_sample, state_conv_a, state_conv_c, norm1_g, norm2_g,
          w_ada, b_ada, w_in, a_dw_w, a_dw_b, a_norm_g, a_norm_b, b_norm_g, b_norm_b, b_spatial_w,
          b_spatial_b, c_conv_w, w_branch, w_out, w_router_g, b_router_g, w_router_e, b_router_e,
          w1, w3, w2, final_norm_g, y_prompt, y_sample, new_a_prompt, new_c_prompt, new_a_sample,
          new_c_sample, new_v_sample):
    ctx = ExitStack()
    with ctx:
        def sem(name):
            return ctx.enter_context(nc.semaphore(name))

        mod_dram = nc.dram_tensor("mod_rows", (9, 6 * D), F32, kind="Internal").ap()
        h2_dram = nc.dram_tensor("h2_rows", (TOK, D), F32, kind="Internal").ap()
        x1_dram = nc.dram_tensor("x1_rows", (TOK, D), F32, kind="Internal").ap()
        y_dram = nc.dram_tensor("y_rows", (2 * TPAD, D), F32, kind="Internal").ap()
        table = nc.dram_tensor("slot_table", (NBLK * P * NE, 1), I32, kind="Internal").ap()
        table_rows = table.rearrange("(r e) o -> r (e o)", e=NE)

        base = (nc.sbuf_base + 31) // 32 * 32
        top = [base]
        size_of = {F32: 4, F32R: 4, BF16: 2, I32: 4, U32: 4}

        def at(name, shape, dt, offset):
            n = int(np.prod(shape[1:])) * size_of[dt]
            return nc.alloc_sbuf_tensor_at(name, shape, dt, offset=offset), offset + (n + 31) // 32 * 32

        def sb(name, shape, dt=F32):
            t, top[0] = at(name, shape, dt, top[0])
            return t

        TG = [HALF, HALF + SMP]
        TM = TG[1]
        ident = sb("ident", [P, P])
        logit = sb("logit", [P, NT, NR])
        tri = sb("tri", [P, P], BF16)
        oneb = sb("oneb", [P, P], BF16)
        io32 = sb("io32", [P, NE])
        vali = sb("vali", [P, 2, NT], I32)
        tinit = sb("tinit", [P, NBLK * NE], I32)
        thr = sb("thr", [NE, NBLK - 1])
        bval = sb("bval", [NE, NBLK - 1])
        io16 = sb("io16", [NE, MAXX])
        trif = sb("trif", [NE, NE])
        onef = sb("onef", [NE, P])
        h_at = top[0]
        h_hi = sb("h_hi", [P, KD, TM], F32R)
        h_lo = sb("h_lo", [P, KD, TM], F32R)
        act0_at = top[0]
        act0_hi = sb("act0_hi", [P, CW, TM], F32R)
        act0_lo = sb("act0_lo", [P, CW, TM], F32R)
        macc = sb("macc", [P, KD, TM])
        act1_at = top[0]
        act1_hi = sb("act1_hi", [P, CW, TM], F32R)
        act1_lo = sb("act1_lo", [P, CW, TM], F32R)
        act1_end = top[0]
        ures_at = top[0]
        u_sb = sb("u_sb", [P, CW, TM])
        v_tok = sb("v_tok", [P, PT + 1, W])
        xres, xres_end = at("xres", [P, PT + 1, D], F32, ures_at)
        top[0] = max(top[0], xres_end)
        w_raw = [sb(f"w_raw{s}", [P, KD, P]) for s in range(2)]
        w_hi = [sb(f"w_hi{s}", [P, KD, P], F32R) for s in range(2)]
        w_lo = [sb(f"w_lo{s}", [P, KD, P], F32R) for s in range(2)]
        a_in = sb("a_in", [P, CW, HA + HALF + NS * AS])
        conv = sb("conv", [P, CW, TM])
        xs = sb("xs", [P, 2, D])
        sig = sb("sig", [P, TM])
        chb = sb("chb", [P, TM])
        vT = sb("vT", [P, TM])
        g_at = top[0]
        gq = sb("gq", [P, TM])
        gt = sb("gt", [P, TM])
        htmp, _ = at("htmp", [P, KD, P], F32, g_at)
        ot = [sb(f"ot{s}", [P, TM]) for s in range(2)]
        p_in = sb("p_in", [P, HC + HALF + NS * CS])
        cv = sb("cv", [P, TM])
        a_tail = sb("a_tail", [P, CW, HA + SMP])
        p_tail = sb("p_tail", [P, CW, HC + SMP])
        p_hist = sb("p_hist", [P, CW, NS * HC])
        wsT = sb("wsT", [P, HEADS, P])
        wsS = sb("wsS", [SMP, HEADS, SMP])
        s_bias = sb("s_bias", [P, CW, P])
        bn_g = sb("bn_g", [P, W])
        bn_b = sb("bn_b", [P, W])
        parT = sb("parT", [P, CW, NPAR])
        n1T = sb("n1T", [P, KD])
        modT = sb("modT", [P, 3 * KD, 9])
        blk64 = sb("blk64", [P, P])
        blk2 = sb("blk2", [P, 2])
        rs_v = sb("rs_v", [P, CW, PT + 1, 2])
        rs_y = sb("rs_y", [P, CW, PT + 1, 2])
        rs_t = sb("rs_t", [P, CW, PT + 1, 2])
        bn6 = sb("bn6", [P, 6])
        mv = sb("mv", [P, 2])
        ssq = sb("ssq", [P, NT])
        ssq2 = sb("ssq2", [P, NT])
        nv = sb("nv", [P, NT])
        ny = sb("ny", [P, NT])
        nt_ = sb("nt_", [P, NT])
        r2y = sb("r2y", [P, NT])
        rw = sb("rw", [P, KD, NR])
        rb = sb("rb", [P, NR])
        n2_b = sb("n2_b", [P, D])
        assert top[0] <= nc.sbuf_usable_end, top[0] - nc.sbuf_usable_end
        h2s, o = at("h2s", [P, D], F32, act1_at)
        h2T, o = at("h2T", [P, KD, P], F32, o)
        A2, o = at("A2", [P, D], F32, o)
        B2, o = at("B2", [P, D], F32, o)
        assert o <= act1_end, o - act1_end
        junk, _ = at("junk", [P, D], F32, act0_at)
        ada, o = at("ada", [P, 2, KD, 512], F32, act0_at)
        assert o <= act1_at
        crow, o = at("crow", [9, D], F32, act1_at)
        sicT, o = at("sicT", [P, KD, 9], F32, o)
        badar, o = at("badar", [9, 2, 512], F32, o)
        modr, o = at("modr", [9, 2, 512], F32, o)
        assert o <= act1_end
        csig, o = at("csig", [9, D], F32, ures_at)
        parr, o = at("parr", [NPAR, W], F32, o)
        n1r, o = at("n1r", [KD, P], F32, o)
        hist, o = at("hist", [HA * TS, 2, W], F32, o)
        wsr, o = at("wsr", [P, HEADS, P], F32, o)
        assert o <= xres_end

        w13, w2s, xg, xT, ysb = [None] * 2, [None] * 2, [None] * 2, [None] * 2, [None] * 2
        o = h_at
        w13[0], o = at("w13_0", [P, 2, KD, FF], F32, o)
        w2s[0], o = at("w2_0", [P, KF, D], F32, o)
        w13[1], o = at("w13_1", [P, 2, KD, FF], F32, o)
        w2s[1], o = at("w2_1", [P, KF, D], F32, o)
        xg[0], o = at("xg0", [P, D], F32, o)
        xg[1], o = at("xg1", [P, D], F32, o)
        xT[0], o = at("xT0", [P, KD, P], F32, o)
        xT[1], o = at("xT1", [P, KD, P], F32, o)
        hsg, o = at("hsg", [P, FF], F32, o)
        gs, o = at("gs", [P, FF], F32, o)
        gT, o = at("gT", [P, KF, P], F32, o)
        ysb[0], o = at("ysb0", [P, D], F32, o)
        ysb[1], o = at("ysb1", [P, D], F32, o)
        x1a, o = at("x1a", [P, 2, D], F32, o)
        g2b, o = at("g2b", [P, 2, D], F32, o)
        fgb, o = at("fgb", [P, D], F32, o)
        yacc, o = at("yacc", [P, 2, D], F32, o)
        top[0] = o
        yin, _ = at("yin", [P, 2, 2, D], F32, h_at)
        gpad = sb("gpad", [P, NT, 8])
        m8g = sb("m8g", [P, NT, 8])
        i8g = sb("i8g", [P, NT, 8], U32)
        m8 = sb("m8", [P, NT, 8])
        i8 = sb("i8", [P, NT, 8], U32)
        gif = sb("gif", [P, NT])
        ohg = sb("ohg", [P, NT, NG])
        em = sb("em", [P, NT, NE])
        ef = sb("ef", [P, NT, 2])
        oh = sb("oh", [P, 2, NT, NE])
        ohs = sb("ohs", [P, NT, NE], BF16)
        rk = sb("rk", [P, 2, NT])
        dsti = sb("dsti", [P, 2, NT], I32)
        wk = sb("wk", [P, 2, NT])
        gd = sb("gd", [P, NT, NG])
        gsum = sb("gsum", [P, NT])
        tb0 = sb("tb0", [P, NE], I32)
        tok0 = sb("tok0", [P, NE], I32)
        gcol = [sb(f"gcol{s}", [P, 1], I32) for s in range(2)]
        scol = [sb(f"scol{s}", [P, 1], I32) for s in range(2)]
        xcol = sb("xcol", [P, 1], I32)
        xtok = sb("xtok", [P, 1], I32)
        cnt = sb("cnt", [NE, 1])
        need = sb("need", [NE, NBLK - 1])
        posn = sb("posn", [NE, NBLK - 1])
        rowc = sb("rowc", [NE, 1])
        xeq = sb("xeq", [NE, MAXX, NBLK - 1])
        xls = sb("xls", [NE, MAXX + 1])
        xrow = sb("xrow", [1, 3, MAXX + 1], I32)
        fss = sb("fss", [P, 2])
        fv = sb("fv", [P, 1])
        fy = sb("fy", [P, 1])
        ft = sb("ft", [P, 1])
        assert top[0] <= nc.sbuf_usable_end, top[0] - nc.sbuf_usable_end

        z = [ctx.enter_context(nc.psum_tensor(f"z{s}", [P, 2, 512], F32)) for s in range(2)]
        q = [ctx.enter_context(nc.psum_tensor(f"q{s}", [P, 2, 512], F32)) for s in range(2)]

        par_in, c_in = sem("par_in"), sem("c_in")
        ada_in = [sem(f"ada_in{s}") for s in range(2)]
        bada_in = [sem(f"bada_in{s}") for s in range(2)]
        x_in = [sem(f"x_in{s}") for s in range(2)]
        w_in_sem = [sem(f"w_in{s}") for s in range(2)]
        consts = sem("consts")
        csig_ok, sic_ok = sem("csig_ok"), sem("sic_ok")
        modr_ok = sem("modr_ok")
        modt_ok = sem("modt_ok")
        mod_out = [sem(f"mod_out{s}") for s in range(2)]
        aux_ok = sem("aux_ok")
        bd_in = sem("bd_in")
        q_ready = [sem(f"q_ready{s}") for s in range(2)]
        q_free = [sem(f"q_free{s}") for s in range(2)]
        z_free = [sem(f"z_free{s}") for s in range(2)]
        whi_ok, wlo_ok = sem("whi_ok"), sem("wlo_ok")
        item_mm = sem("item_mm")
        x_sq, x_n = sem("x_sq"), sem("x_n")
        hhi_ok, hlo_ok = sem("hhi_ok"), sem("hlo_ok")
        chi_ok, clo_ok = sem("chi_ok"), sem("clo_ok")
        gt_ok, gs_ok, gq_ok = sem("gt_ok"), sem("gs_ok"), sem("gq_ok")
        vT_ok, vn_ok, v_out = sem("vT_ok"), sem("vn_ok"), sem("v_out")
        bb_ok, bhi_ok, blo_ok = sem("bb_ok"), sem("bhi_ok"), sem("blo_ok")
        cnv_ok = sem("cnv_ok")
        asq_ok, rs_ok, ay_ok, af_ok, ahi_ok, alo_ok = (
            sem(n) for n in ("asq_ok", "rs_ok", "ay_ok", "af_ok", "ahi_ok", "alo_ok"))
        macc_ok = sem("macc_ok")
        ot_ok = sem("ot_ok")
        xres_in = sem("xres_in")
        x1_sq = sem("x1_sq")
        ab_in = sem("ab_in")
        h2_ok, h2_out, x1_out = sem("h2_ok"), sem("h2_out"), sem("x1_out")
        st_out = sem("st_out")

        block = ctx.enter_context(nc.Block())

        H2 = TM // 2

        def zv(s, g):
            return z[s][:, 0, 0:HALF] if g == 0 else z[s][:, :, 0:H2]

        def tv(ap, g):
            return ap[:, 0:HALF] if g == 0 else ap[:, 0:TM].rearrange("p (b t) -> p b t", b=2)

        def chunk(t, i):
            return t[:, i, :] if isinstance(i, int) else \
                t[:, bass.ds(i, 1), :].rearrange("p o t -> p (o t)")

        def zparts(s, g):
            return [(z[s][:, 0, 0:HALF], 0, HALF)] if g == 0 else \
                [(z[s][:, 0, 0:H2], 0, H2), (z[s][:, 1, 0:HALF - H2], H2, HALF)]

        def zsample(s):
            return z[s][:, 1, HALF - H2:H2]

        def halves(g):
            return [(0, 0, HALF)] if g == 0 else [(0, 0, H2), (1, H2, TM)]

        def seqs(ap):
            return ap.rearrange("p (n t) -> p n t", n=NS)

        def item_no(g, u, s):
            return NI * g + 2 * u + s

        def split_no(g, u, s):
            return NSPLIT * g + 2 * u + s

        def slot_use(g, u):
            return NI // 2 * g + u

        def first(u):
            return u if isinstance(u, int) else u.min_val

        QFILL, QUSE, qn, qf = {}, {}, [0, 0], [0, 0]

        def use(s, *name):
            QFILL[name], QUSE[name] = (s, qn[s]), (s, qf[s])
            qn[s] += 1
            qf[s] += name[0] != "ada"

        use(0, "par"), use(1, "n1"), use(0, "hist"), use(1, "ws"), use(0, "sic")

        def use_ada(js):
            for j in js:
                use(0, "ada", j)
                if j < 6:
                    use(1, "modT", j)

        use_ada(range(4))
        for t in range(PT):
            use(t % 2, "xT", 0, t)
        for g in range(2):
            if g:
                for i in range(PT):
                    use(0, "h2T", 0, i), use(1, "lg", 0, i)
            else:
                use_ada(range(4, 12))
            for i in range(CW):
                use(0, "vT", g, i)
            for t in range(PT + g):
                use(t % 2, "sp", g, t)
            if g:
                use(0, "stA"), use(1, "stC")
            for c in range(3):
                use(c % 2, "mu", g, c)
            use(1, "var", g, 0)
            for c in range(3):
                use(c % 2, "bc", g, c)
            use(0, "mu", g, 3), use(1, "var", g, 3), use(0, "bc", g, 3)
            if g == 0:
                for t in range(PT):
                    use(t % 2, "xT", 1, t)
            use(0, "oT", g, 0), use(1, "oT", g, 1)
            if g == 0:
                use(0, "xT", 1, PT)
            for n in range(2, KD):
                use(n % 2, "oT", g, n)
        for i in range(PT + 1):
            use(0, "h2T", 1, i), use(1, "lg", 1, i)
        use(0, "rank"), use(1, "cnt"), use(1, "pos"), use(1, "list")

        def q_wait_free(pe, *name, more=0):
            s, n = QUSE[name]
            if n:
                pe.wait_ge(q_free[s], n + more)
            return s

        def q_wait_ready(eng, *name, more=0):
            s, n = QFILL[name]
            eng.wait_ge(q_ready[s], n + 1 + more)
            return s

        def q_wait_read(eng, *name, more=0):
            s, n = QUSE[name]
            eng.wait_ge(q_free[s], n + 1 + more)

        def before_wait(eng, n):
            n = n if isinstance(n, int) else eng.to_reg(n)
            eng.wait_ge(c_in, 32)
            return n

        def tiles(g):
            return [(t, P) for t in range(PT)] + ([(PT, SMP)] if g else [])

        def x_rows(g, t):
            return x_sample.rearrange("n t d -> (n t) d") if t == PT else \
                x_prompt[0, (g * PT + t) * P:(g * PT + t + 1) * P, :]

        XT = [(g, t, rows) for g in range(2) for t, rows in tiles(g)]
        XN = {(g, t): n for n, (g, t, _) in enumerate(XT)}
        XUSE = {(g, t): sum(1 for gg, tt, _ in XT[:n] if tt % 2 == t % 2) for n, (g, t, _) in enumerate(XT)}


        rt_const, tab_out = sem("rt_const"), sem("tab_out")
        rt_m = sem("rt_m")
        rt_e = sem("rt_e")
        oh_ok, wk_ok = sem("oh_ok"), sem("wk_ok")
        dst_ok, tab_sc = sem("dst_ok"), sem("tab_sc")
        tb_in, tok_ok = sem("tb_in"), sem("tok_ok")
        row_ok, xls_ok, xrow_ok = sem("row_ok"), sem("xls_ok"), sem("xrow_ok")
        xg0_ok, gcol_ok, scol_ok = sem("xg0_ok"), sem("gcol_ok"), sem("scol_ok")
        m_w13, m_w2, m_xg, m_sc = ([sem(f"{n}{s}") for s in range(2)] for n in ("m_w13", "m_w2", "m_xg", "m_sc"))
        m_T, m_xT, m_H, m_sg, m_g, m_G, m_gT, m_Y, m_y = (
            sem(n) for n in ("m_T", "m_xT", "m_H", "m_sg", "m_g", "m_G", "m_gT", "m_Y", "m_y"))
        o_w, o_c, o_x, o_sc = (sem(n) for n in ("o_w", "o_c", "o_x", "o_sc"))
        f_in = [sem(f"f_in{s}") for s in range(2)]
        f_par, f_a, f_sum, f_sq, f_y = (sem(n) for n in ("f_par", "f_a", "f_sum", "f_sq", "f_y"))
        f_out = [sem(f"f_out{s}") for s in range(2)]

        def dense_done(eng):
            eng.wait_ge(item_mm, 2 * NI)
            eng.wait_ge(h2_out, 16 * NT)
            eng.wait_ge(x1_out, 16 * NT)
            eng.wait_ge(x1_sq, NT)
            q_wait_read(eng, "lg", 1, PT)

        def expert_rows(w, e):
            return w[0, bass.ds(e, 1)].rearrange("o (p k) f -> p (o k) f", p=P)

        def moe_sync(sp):
            def load13(e, s):
                for j, w in enumerate((w1, w3)):
                    sp.dma_start(w13[s][:, j], expert_rows(w, e)).then_inc(m_w13[s], 16)

            def load2(e, s):
                sp.dma_start(w2s[s][:], expert_rows(w2, e)).then_inc(m_w2[s], 16)

            sp.wait_ge(item_mm, item_no(1, O0 // 2, 0))
            load13(0, 0)
            dense_done(sp)
            load2(0, 0)
            load13(1, 1)
            load2(1, 1)
            with sp.Fori(0, NE // 2 - 1) as r:
                for s in range(2):
                    sp.wait_ge(m_H, r * 2 + (s + 1))
                    load13(r * 2 + (s + 2), s)
                    sp.wait_ge(m_Y, r * 2 + (s + 1))
                    load2(r * 2 + (s + 2), s)
            sp.wait_ge(xrow_ok, 1)
            sp.wait_ge(m_Y, NE)
            n = sp.value_load(xrow[0:1, 0, MAXX:MAXX + 1], min_val=0, max_val=MAXX)
            with sp.If(n > 0):
                with sp.Fori(0, n) as i:
                    e = sp.value_load(xrow[0:1, 1, bass.ds(i, 1)], min_val=0, max_val=NE - 1)
                    b = sp.value_load(xrow[0:1, 2, bass.ds(i, 1)], min_val=1, max_val=NBLK - 1)
                    for j, w in enumerate((w1, w3)):
                        sp.dma_start(w13[0][:, j], expert_rows(w, e)).then_inc(o_w, 16)
                    sp.dma_start(w2s[0][:], expert_rows(w2, e)).then_inc(o_w, 16)
                    sp.dma_start(xcol[:], table[bass.ds(b * (P * NE), P * NE), :].rearrange(
                        "(r e) o -> r e o", e=NE)[:, bass.ds(e, 1), :].rearrange("r e o -> r (e o)"), allow_slow_non_contiguous=True).then_inc(o_w, 16)
                    n_ = before_wait(sp, i * 16 + 16)
                    sp.wait_ge(o_sc, n_)
            for s in range(2):
                sp.wait_ge(m_sc[s], 16 * (NE // 2))

            def final_load(r, s, rows):
                r0 = r * (2 * P) + s * P
                sp.dma_start(x1a[0:rows, s, :], x1_dram[bass.ds(r0, rows), :]).then_inc(f_in[s], 16)
                for k in range(2):
                    sp.dma_start(yin[0:rows, s, k, :], y_dram[bass.ds(r0 + k * TPAD, rows), :]).then_inc(f_in[s], 16)

            final_load(0, 0, P)
            final_load(0, 1, P)
            with sp.Fori(1, PT) as r:
                for s in range(2):
                    sp.wait_ge(f_sum, r * 2 + (s - 1))
                    final_load(r, s, P)
            sp.wait_ge(f_sum, NT - 2)
            final_load(PT, 0, SMP)

        def moe_gpsimd(pool):
            dense_done(pool)
            pool.memset(xg[0][:], 0.0).then_inc(xg0_ok, 1)
            pool.drain()
            pool.memset(xg[1][:], 0.0).then_inc(xg0_ok, 1)
            pool.wait_ge(dst_ok, 1)
            pool.wait_ge(tab_out, 16)
            for t in range(NT):
                rows = P if t < NT - 1 else SMP
                for k in range(2):
                    pool.indirect_dma_start(table, bass.IndirectOffsetOnAxis(ap=dsti[0:rows, k, t:t + 1], axis=0),
                                            vali[0:rows, k, t:t + 1], None, bounds_check=NBLK * P * NE - 1,
                                            oob_is_err=False).then_inc(tab_sc, 16)
            pool.wait_ge(tab_sc, 16 * 2 * NT)
            pool.dma_start(tb0[:], table_rows[0:P, :]).then_inc(tb_in, 16)
            pool.wait_ge(tok_ok, 1)

            def gather_dma(s, col, done):
                pool.indirect_dma_start(xg[s][:], None, h2_dram, bass.IndirectOffsetOnAxis(ap=col[:, 0:1], axis=0),
                                        bounds_check=TOK - 1, oob_is_err=False).then_inc(done, 16)

            def scatter_dma(s, col, done):
                pool.indirect_dma_start(y_dram, bass.IndirectOffsetOnAxis(ap=col[:, 0:1], axis=0), ysb[s][:], None,
                                        bounds_check=2 * TPAD - 1, oob_is_err=False).then_inc(done, 16)

            def gather(e, s):
                if first(e) >= 2:
                    pool.wait_ge(m_T, e - 1)
                pool.tensor_copy(gcol[s][:], tok0[:, bass.ds(e, 1)]).then_inc(gcol_ok, 1)
                n_ = before_wait(pool, e + 1)
                pool.wait_ge(gcol_ok, n_)
                gather_dma(s, gcol[s], m_xg[s])

            def scatter(e, s, r):
                if first(r):
                    pool.wait_ge(m_sc[s], r * 16)
                pool.tensor_copy(scol[s][:], tb0[:, bass.ds(e, 1)]).then_inc(scol_ok, 1)
                n_ = before_wait(pool, e + 1)
                pool.wait_ge(scol_ok, n_)
                pool.wait_ge(m_y, e + 1)
                scatter_dma(s, scol[s], m_sc[s])

            pool.wait_ge(xg0_ok, 2)
            for s in range(2):
                gather(s, s)
            for s in range(2):
                gather(s + 2, s)
                scatter(s, s, 0)
            with pool.Fori(1, NE // 2 - 1) as r:
                for s in range(2):
                    gather(r * 2 + (s + 2), s)
                    scatter(r * 2 + s, s, r)
            for s in range(2):
                scatter(NE - 2 + s, s, NE // 2 - 1)
            pool.wait_ge(xrow_ok, 1)
            for s in range(2):
                pool.wait_ge(m_sc[s], 16 * (NE // 2))
            n = pool.value_load(xrow[0:1, 0, MAXX:MAXX + 1], min_val=0, max_val=MAXX)
            with pool.If(n > 0):
                with pool.Fori(0, n) as i:
                    n_ = before_wait(pool, i + 1)
                    pool.wait_ge(o_c, n_)
                    gather_dma(0, xtok, o_x)
                    n_ = before_wait(pool, i + (NE + 1))
                    pool.wait_ge(m_y, n_)
                    scatter_dma(0, xcol, o_sc)

            def final_store(r, s, rows, dst):
                pool.wait_ge(f_y, r * 2 + (s + 1))
                pool.dma_start(dst, yacc[0:rows, s, :]).then_inc(f_out[s], 16)

            with pool.Fori(0, PT) as r:
                for s in range(2):
                    final_store(r, s, P, y_prompt[0, bass.ds(r * (2 * P) + s * P, P), :])
            final_store(PT, 0, SMP, y_sample.rearrange("n t d -> (n t) d"))
            pool.wait_ge(f_out[0], 16 * (PT + 1))
            pool.wait_ge(f_out[1], 16 * PT)
            pool.wait_ge(st_out, 16 * (3 + 2 * NS))

        def step_T(pe, e, s):
            if first(e):
                pe.wait_ge(m_xT, e)
            for k in range(KD):
                last = pe.transpose(q[0][:, k // 4, (k % 4) * P:(k % 4 + 1) * P],
                                    xg[s][:, :].rearrange("p (c k) -> p k c", k=KD)[:, k, :], ident[:])
            last.then_inc(m_T, 1)

        def step_H(pe, e, s):
            pe.wait_ge(m_xT, e + 1)
            if first(e):
                pe.wait_ge(m_g, e)
            for k in range(KD):
                for j in range(2):
                    last = pe.matmul(z[0][:, j, :], xT[s][:, k, :], w13[s][:, j, k, :], start=(k == 0), stop=(k == KD - 1))
            last.then_inc(m_H, 1)

        def step_G(pe, e):
            pe.wait_ge(m_g, e + 1)
            if first(e):
                pe.wait_ge(m_gT, e)
            for k in range(KF):
                last = pe.transpose(q[1][:, 0, k * P:(k + 1) * P], gs[:, :].rearrange("p (c k) -> p k c", k=KF)[:, k, :], ident[:])
            last.then_inc(m_G, 1)

        def step_Y(pe, e, s):
            pe.wait_ge(m_gT, e + 1)
            if first(e):
                pe.wait_ge(m_y, e)
            for k in range(KF):
                for j in range(2):
                    last = pe.matmul(z[1][:, j, :], gT[:, k, :], w2s[s][:, k, j * 512:(j + 1) * 512],
                                     start=(k == 0), stop=(k == KF - 1))
            last.then_inc(m_Y, 1)

        def moe_tensor(pe):
            s = q_wait_free(pe, "rank")
            pe.wait_ge(oh_ok, 1)
            pe.wait_ge(rt_const, N_RT)
            for t in range(NT):
                out = q[s][:, 0, t * NE:(t + 1) * NE]
                for j in range(t):
                    pe.matmul(out, oneb[:], ohs[:, j, :], start=(j == 0), stop=False)
                last = pe.matmul(out, tri[:], ohs[:, t, :], start=(t == 0), stop=True)
            last.then_inc(q_ready[s], 1)
            s = q_wait_free(pe, "cnt")
            for t in range(NT):
                last = pe.matmul(q[s][0:NE, 0, 0:1], ohs[:, t, :], oneb[:, 0:1], start=(t == 0), stop=(t == NT - 1))
            last.then_inc(q_ready[s], 1)
            s = q_wait_free(pe, "pos")
            pe.wait_ge(row_ok, 1)
            pe.matmul(q[s][0:NE, 0, 0:1], trif[:], rowc[:], start=True, stop=True).then_inc(q_ready[s], 1)
            s = q_wait_free(pe, "list")
            pe.wait_ge(xls_ok, 1)
            pe.matmul(q[s][0:1, 0, 0:MAXX + 1], onef[:, 0:1], xls[:], start=True, stop=True).then_inc(q_ready[s], 1)
            q_wait_read(pe, "rank")
            q_wait_read(pe, "list")
            for s in range(2):
                pe.wait_ge(z_free[s], NI)

            def T(r, s):
                pe.wait_ge(m_xg[s], r * 16 + 16)
                step_T(pe, r * 2 + s, s)

            def H(r, s):
                pe.wait_ge(m_w13[s], r * 32 + 32)
                step_H(pe, r * 2 + s, s)

            def Y(r, s):
                pe.wait_ge(m_w2[s], r * 16 + 16)
                step_Y(pe, r * 2 + s, s)

            T(0, 0)
            H(0, 0)
            T(0, 1)
            step_G(pe, 0)
            H(0, 1)
            T(1, 0)
            Y(0, 0)
            step_G(pe, 1)
            with pe.Fori(1, NE // 2) as r:
                H(r, 0)
                T(r, 1)
                Y(r - 1, 1)
                step_G(pe, r * 2)
                H(r, 1)
                with pe.If(r < NE // 2 - 1):
                    T(r + 1, 0)
                Y(r, 0)
                step_G(pe, r * 2 + 1)
            Y(NE // 2 - 1, 1)
            pe.wait_ge(xrow_ok, 1)
            n = pe.value_load(xrow[0:1, 0, MAXX:MAXX + 1], min_val=0, max_val=MAXX)
            with pe.If(n > 0):
                with pe.Fori(0, n) as i:
                    pe.wait_ge(o_x, i * 16 + 16)
                    step_T(pe, i + NE, 0)
                    pe.wait_ge(o_w, i * 64 + 64)
                    step_H(pe, i + NE, 0)
                    step_G(pe, i + NE)
                    step_Y(pe, i + NE, 0)

        def moe_scalar(act):
            act.wait_ge(rt_m, 1)
            act.activation(wk[:, 0, :], gif[:], ACT.Sigmoid)
            act.activation(wk[:, 1, :], gif[:], ACT.Sigmoid, scale=-1.0)
            act.activation(gd[:], gd[:], ACT.Exp).then_inc(rt_e, 1)

            def rows_T(e, s):
                act.wait_ge(m_T, e + 1)
                act.activation(xT[s][:], q[0][:, :, :].rearrange("p b (k t) -> p (b k) t", t=P), ACT.Copy).then_inc(m_xT, 1)

            def sigm(e):
                act.wait_ge(m_H, e + 1)
                if first(e):
                    act.wait_ge(m_g, e)
                act.activation(hsg[:], z[0][:, 0, :], ACT.Sigmoid).then_inc(m_sg, 1)

            def hidden_T(e):
                act.wait_ge(m_G, e + 1)
                if first(e):
                    act.wait_ge(m_Y, e)
                act.activation(gT[:], q[1][:, 0, :].rearrange("p (k t) -> p k t", t=P), ACT.Copy).then_inc(m_gT, 1)

            rows_T(0, 0)
            sigm(0)
            rows_T(1, 1)
            hidden_T(0)
            sigm(1)
            rows_T(2, 0)
            hidden_T(1)
            with act.Fori(1, NE // 2 - 1) as r:
                for s in range(2):
                    sigm(r * 2 + s)
                    rows_T(r * 2 + (s + 1), 1 - s)
                    hidden_T(r * 2 + s)
            sigm(NE - 2)
            rows_T(NE - 1, 1)
            hidden_T(NE - 2)
            sigm(NE - 1)
            hidden_T(NE - 1)
            act.wait_ge(xrow_ok, 1)
            n = act.value_load(xrow[0:1, 0, MAXX:MAXX + 1], min_val=0, max_val=MAXX)
            with act.If(n > 0):
                with act.Fori(0, n) as i:
                    rows_T(i + NE, 0)
                    sigm(i + NE)
                    hidden_T(i + NE)
            act.dma_start(fgb[:], final_norm_g.rearrange("(o d) -> o d", o=1).to_broadcast([P, D])).then_inc(f_par, 16)
            act.dma_start(g2b[:, 0, :], mod_dram[0:1, 5 * D:6 * D].to_broadcast([P, D])).then_inc(f_par, 16)
            for n_ in range(NS):
                act.dma_start(g2b[n_ * TS:(n_ + 1) * TS, 1, :],
                              mod_dram[1 + n_:2 + n_, 5 * D:6 * D].to_broadcast([TS, D])).then_inc(f_par, 16)

            def final_tile(r, s, rows):
                t = r * 2 + s
                act.wait_ge(f_in[s], r * 48 + 48)
                if first(r):
                    act.wait_ge(f_out[s], r * 16)
                w0 = wk[0:rows, 0, t:t + 1] if isinstance(t, int) else wk[0:rows, 0, bass.ds(t, 1)]
                act.activation(yacc[0:rows, s, :], yin[0:rows, s, 0, :], ACT.Copy, scale=w0).then_inc(f_a, 1)
                act.wait_ge(f_sum, t + 1)
                if first(t):
                    act.wait_ge(f_y, t)
                act.activation(ysb[0][0:rows, :], yacc[0:rows, s, :], ACT.Square, accum_out=fss[0:rows, s:s + 1]).then_inc(f_sq, 1)

            for s in range(2):
                act.wait_ge(m_sc[s], 16 * (NE // 2))
            final_tile(0, 0, P)
            final_tile(0, 1, P)
            with act.Fori(1, PT) as r:
                final_tile(r, 0, P)
                final_tile(r, 1, P)
            final_tile(PT, 0, SMP)

        def moe_vector(dve):
            def tt(out, a, b, op):
                return dve.tensor_tensor(out, a, b, op)

            def rsqrt(y, v, t):
                dve.drain()
                dve.tensor_scalar(y.bitcast(I32), v.bitcast(I32), 1, None, ALU.logical_shift_right)
                dve.drain()
                dve.tensor_scalar(y.bitcast(I32), y.bitcast(I32), -1, MAGIC, ALU.mult, ALU.add)
                for _ in range(3):
                    dve.drain()
                    tt(t, y, y, ALU.mult)
                    dve.drain()
                    dve.scalar_tensor_tensor(t, v, -0.5, t, ALU.mult, ALU.mult)
                    dve.drain()
                    last = dve.scalar_tensor_tensor(y, t, 1.5, y, ALU.add, ALU.mult)
                return last

            dense_done(dve)
            dve.wait_ge(rt_const, N_RT)
            dve.memset(gpad[:], -BIG)
            dve.drain()
            dve.tensor_copy(gpad[:, :, 0:NG], logit[:, :, 0:NG])
            dve.drain()
            for t in range(NT):
                dve.max(m8g[:, t, :], gpad[:, t, :])
            dve.drain()
            for t in range(NT):
                dve.max_index(i8g[:, t, :], m8g[:, t, :], gpad[:, t, :])
            dve.drain()
            dve.tensor_copy(gif[:], i8g[:, :, 0])
            dve.drain()
            tt(ohg[:], io32[:, 0:NG].unsqueeze(1).to_broadcast([P, NT, NG]), gif[:].unsqueeze(2).to_broadcast([P, NT, NG]), ALU.is_equal)
            tt(gd[:], logit[:, :, 0:NG], m8g[:, :, 0:1].to_broadcast([P, NT, NG]), ALU.subtract)
            dve.drain()
            em4 = em[:, :, :].rearrange("p t (g e) -> p (t g) e", e=EG)
            oh4 = ohg[:, :, :].rearrange("p t g -> p (t g)")
            for t in range(NT):
                tt(em[:, t, :].rearrange("p (g e) -> p g e", e=EG), logit[:, t, NG:NR].rearrange("p (g e) -> p g e", e=EG),
                   ohg[:, t, :].unsqueeze(2).to_broadcast([P, NG, EG]), ALU.mult)
            dve.drain()
            dve.tensor_scalar(ohg[:], ohg[:], 1.0, BIG, ALU.subtract, ALU.mult)
            dve.drain()
            tt(em4, em4, oh4.unsqueeze(2).to_broadcast([P, NT * NG, EG]), ALU.add)
            dve.drain()
            for t in range(NT):
                dve.max(m8[:, t, :], em[:, t, :])
            dve.drain()
            for t in range(NT):
                dve.max_index(i8[:, t, :], m8[:, t, :], em[:, t, :])
            tt(gif[:], m8[:, :, 0], m8[:, :, 1], ALU.subtract).then_inc(rt_m, 1)
            dve.drain()
            dve.tensor_copy(ef[:], i8[:, :, 0:2])
            dve.drain()
            for k in range(2):
                tt(oh[:, k], io32[:].unsqueeze(1).to_broadcast([P, NT, NE]), ef[:, :, k:k + 1].to_broadcast([P, NT, NE]), ALU.is_equal)
            dve.drain()
            tt(ohs[:], oh[:, 0], oh[:, 1], ALU.add)
            dve.drain()
            for p0 in range(SMP, P, 32):
                last = dve.memset(ohs[p0:p0 + 32, NT - 1, :], 0.0)
            last.then_inc(oh_ok, 1)
            s = q_wait_ready(dve, "rank")
            rank = q[s][:, 0, 0:NT * NE].rearrange("p (t e) -> p t e", e=NE)
            for k in range(2):
                tt(oh[:, k], oh[:, k], rank, ALU.mult)
            dve.drain()
            for k in range(2):
                last = dve.tensor_reduce(rk[:, k, :], oh[:, k], axis=AX.X, op=ALU.add)
            last.then_inc(q_free[s], 1)
            dve.drain()
            for k in range(2):
                last = dve.scalar_tensor_tensor(dsti[:, k, :], rk[:, k, :], float(NE), ef[:, :, k], ALU.mult, ALU.add)
            last.then_inc(dst_ok, 1)
            s = q_wait_ready(dve, "cnt")
            dve.tensor_copy(cnt[:], q[s][0:NE, 0, 0:1]).then_inc(q_free[s], 1)
            dve.drain()
            dve.tensor_scalar(need[:], thr[:], cnt[:, 0:1], None, ALU.is_lt)
            dve.drain()
            dve.tensor_reduce(rowc[:], need[:], axis=AX.X, op=ALU.add).then_inc(row_ok, 1)
            tt(bval[:], bval[:], need[:], ALU.mult)
            s = q_wait_ready(dve, "pos")
            dve.tensor_scalar(posn[:], thr[:], 1.0 / P, q[s][0:NE, 0, 0:1], ALU.mult, ALU.add).then_inc(q_free[s], 1)
            dve.drain()
            dve.tensor_scalar(posn[:], posn[:], 1.0, None, ALU.subtract)
            dve.drain()
            shape = [NE, MAXX, NBLK - 1]
            tt(xeq[:], io16[:].unsqueeze(2).to_broadcast(shape), posn[:].unsqueeze(1).to_broadcast(shape), ALU.is_equal)
            dve.drain()
            tt(xeq[:], xeq[:], bval[:].unsqueeze(1).to_broadcast(shape), ALU.mult)
            dve.drain()
            dve.tensor_reduce(xls[:, 0:MAXX], xeq[:], axis=AX.X, op=ALU.add)
            dve.tensor_copy(xls[:, MAXX:MAXX + 1], rowc[:]).then_inc(xls_ok, 1)
            s = q_wait_ready(dve, "list")
            dve.tensor_copy(xrow[:, 0, :], q[s][0:1, 0, 0:MAXX + 1]).then_inc(q_free[s], 1)
            dve.drain()
            dve.tensor_scalar(xrow[:, 1, :], xrow[:, 0, :], NE - 1, None, ALU.bitwise_and)
            dve.tensor_scalar(xrow[:, 2, :], xrow[:, 0, :], 5, None, ALU.logical_shift_right).then_inc(xrow_ok, 1)
            dve.wait_ge(rt_e, 1)
            dve.tensor_reduce(gsum[:], gd[:], axis=AX.X, op=ALU.add)
            dve.drain()
            dve.reciprocal(gsum[:], gsum[:])
            dve.drain()
            for k in range(2):
                last = tt(wk[:, k, :], wk[:, k, :], gsum[:], ALU.mult)
            last.then_inc(wk_ok, 1)
            dve.wait_ge(tb_in, 16)
            dve.tensor_scalar(tok0[:], tb0[:], TPAD - 1, None, ALU.bitwise_and).then_inc(tok_ok, 1)

            def hidden(e):
                dve.wait_ge(m_sg, e + 1)
                if first(e):
                    dve.wait_ge(m_G, e)
                tt(gs[:], hsg[:], z[0][:, 0, :], ALU.mult)
                dve.drain()
                tt(gs[:], gs[:], z[0][:, 1, :], ALU.mult).then_inc(m_g, 1)

            def result(e, s, r=None):
                dve.wait_ge(m_Y, e + 1)
                if r is not None and first(r):
                    dve.wait_ge(m_sc[s], r * 16)
                dve.tensor_copy(ysb[s][:], z[1][:, :, :].rearrange("p b c -> p (b c)")).then_inc(m_y, 1)

            hidden(0)
            hidden(1)
            result(0, 0, 0)
            hidden(2)
            result(1, 1, 0)
            hidden(3)
            result(2, 0, 1)
            with dve.Fori(2, NE // 2) as r:
                hidden(r * 2)
                result(r * 2 - 1, 1, r - 1)
                hidden(r * 2 + 1)
                result(r * 2, 0, r)
            result(NE - 1, 1, NE // 2 - 1)
            for s in range(2):
                dve.wait_ge(m_sc[s], 16 * (NE // 2))
            n = dve.value_load(xrow[0:1, 0, MAXX:MAXX + 1], min_val=0, max_val=MAXX)
            with dve.If(n > 0):
                with dve.Fori(0, n) as i:
                    dve.wait_ge(o_w, i * 64 + 64)
                    dve.tensor_scalar(xtok[:], xcol[:], TPAD - 1, None, ALU.bitwise_and).then_inc(o_c, 1)
                    hidden(i + NE)
                    result(i + NE, 0)

            def final_tile(r, s, rows):
                t = r * 2 + s
                acc, xr = yacc[0:rows, s, :], x1a[0:rows, s, :]
                w1_ = wk[0:rows, 1, t:t + 1] if isinstance(t, int) else wk[0:rows, 1, bass.ds(t, 1)]
                dve.wait_ge(f_a, t + 1)
                dve.scalar_tensor_tensor(acc, yin[0:rows, s, 1, :], w1_, acc, ALU.mult, ALU.add)
                dve.drain()
                tt(acc, acc, g2b[0:rows, 1 if rows == SMP else 0, :], ALU.mult)
                dve.drain()
                tt(acc, acc, xr, ALU.add).then_inc(f_sum, 1)
                dve.wait_ge(f_sq, t + 1)
                dve.tensor_scalar(fv[0:rows, :], fss[0:rows, s:s + 1], 1.0 / D, EPS, ALU.mult, ALU.add)
                rsqrt(fy[0:rows, :], fv[0:rows, :], ft[0:rows, :])
                dve.drain()
                dve.scalar_tensor_tensor(acc, acc, fy[0:rows, 0:1], fgb[0:rows, :], ALU.mult, ALU.mult).then_inc(f_y, 1)

            dve.wait_ge(f_par, 16 * (2 + NS))
            final_tile(0, 0, P)
            final_tile(0, 1, P)
            with dve.Fori(1, PT) as r:
                final_tile(r, 0, P)
                final_tile(r, 1, P)
            final_tile(PT, 0, SMP)

        w_in_v = w_in[0].rearrange("(k p) c -> p k c", p=P)
        w_br_v = w_branch[0].rearrange("b (k p) c -> p b k c", p=P)
        w_out_v = w_out[0].rearrange("(k p) c -> p k c", p=P)
        ada_v = w_ada[0].rearrange("(k p) c -> p k c", p=P)

        @block.sync
        def _(sp):
            def load(g, u, s, src, kn=KD):
                if first(u) == 0 or first(u) > O0 // 2:
                    if g or first(u):
                        sp.wait_ge(item_mm, item_no(g, u, s) - 1)
                else:
                    n_ = before_wait(sp, split_no(g, u, s) - 1)
                    sp.wait_ge(wlo_ok, n_)
                sp.dma_start(w_raw[s][:, 0:kn, :], src).then_inc(w_in_sem[s], 16)

            def cols_of(name, i):
                return w_in_v[:, :, bass.ds(i * P + COL[name], P)]

            def load_ada(j):
                s = j % 2
                if j >= 2:
                    q_wait_ready(sp, "ada", j - 2)
                sp.dma_start(ada[:, s, :, :], ada_v[:, :, j * 512:(j + 1) * 512]).then_inc(ada_in[s], 16)
                if j >= 2:
                    sp.wait_ge(modr_ok, j - 1)
                sp.dma_start(badar[:, s, :], b_ada[0:1, j * 512:(j + 1) * 512].to_broadcast([9, 512])
                             ).then_inc(bada_in[s], 16)

            for j in range(4):
                load_ada(j)
            for g in range(2):
                load(g, 0, 0, cols_of("a_gt", 0))
                load(g, 0, 1, cols_of("a_val", 0))
                with sp.Fori(1, CW) as i:
                    load(g, i, 0, cols_of("a_gt", i))
                    load(g, i, 1, cols_of("a_val", i))
                for n in range(3 * CW):
                    if g == 0 and n == 2:
                        for j in range(4, 12):
                            load_ada(j)
                    load(g, (C0 + n) // 2, n % 2, cols_of(("c_h", "c_c", "c_b")[n % 3], n // 3))
                with sp.Fori(0, CW) as i:
                    load(g, i + B0 // 2, 0, cols_of("b_v", i))
                    load(g, i + B0 // 2, 1, cols_of("b_u", i))
                for b, n0 in ((NB_C, GC0), (NB_B, GB0), (NB_A, GA0)):
                    with sp.Fori(0, KD) as i:
                        load(g, i + n0 // 2, 0, cols_of("gates", i + b * KD))
                        load(g, i + n0 // 2, 1, w_br_v[:, b, :, bass.ds(i * P, P)], CW)
                load(g, O0 // 2, 0, w_out_v[:, :, 0:P])
                load(g, O0 // 2, 1, w_out_v[:, :, P:2 * P])
                with sp.Fori(1, KD // 2) as i:
                    for s in range(2):
                        load(g, i + O0 // 2, s, w_out_v[:, :, bass.ds(i * (2 * P) + s * P, P)])
            moe_sync(sp)

        @block.gpsimd
        def _(pool):
            def x_load(g, t):
                s, rows = t % 2, dict(tiles(g))[t]
                if XUSE[g, t]:
                    gl, tl, _ = [k for k in XT if k[1] % 2 == s][XUSE[g, t] - 1]
                    q_wait_ready(pool, "xT", gl, tl)
                pool.dma_start(xs[0:rows, s, :], x_rows(g, t)).then_inc(x_in[s], 16)

            x_load(0, 0)
            x_load(0, 1)
            pool.memset(ident[:], 0.0).then_inc(consts, 1)
            pool.drain()
            pool.memset(blk64[:], 0.0).then_inc(consts, 1)
            pool.drain()
            pool.memset(blk2[:], 0.0).then_inc(consts, 1)
            pool.drain()
            pool.wait_ge(consts, 3)
            pool.affine_select(out=ident[:], in_=ident[:], compare_op=ALU.not_equal, fill=1.0, base=0,
                               pattern=[[-1, P]], channel_multiplier=1).then_inc(consts, 1)
            pool.drain()
            for h in range(2):
                pool.memset(blk64[64 * h:64 * h + 64, 64 * h:64 * h + 64], 1.0 / 64).then_inc(consts, 1)
                pool.drain()
                pool.memset(blk2[64 * h:64 * h + 64, h:h + 1], 1.0 / 64).then_inc(consts, 1)
                pool.drain()
            pool.memset(a_in[:, :, 0:HA], 0.0).then_inc(consts, 1)
            pool.drain()
            pool.memset(p_in[:, 0:HC], 0.0).then_inc(consts, 1)
            pool.drain()
            pool.memset(wsS[:], 0.0).then_inc(consts, 1)
            pool.drain()
            for t_ in (rs_v, ssq, ssq2, mv, logit):
                pool.memset(t_[:], 1.0).then_inc(consts, 1)
                pool.drain()
            pool.wait_ge(par_in, 16 * N_PAR)
            pool.affine_select(out=wsr[:], in_=wsr[:], compare_op=ALU.is_ge, fill=0.0, base=0,
                               pattern=[[0, HEADS], [-1, P]], channel_multiplier=1).then_inc(consts, 1)
            pool.drain()
            pool.memset(tinit[:], OOB).then_inc(rt_const, 1)
            pool.drain()
            pool.memset(tri[:], 1.0).then_inc(rt_const, 1)
            pool.drain()
            pool.memset(oneb[:], 1.0).then_inc(rt_const, 1)
            pool.drain()
            pool.memset(trif[:], 1.0).then_inc(rt_const, 1)
            pool.drain()
            pool.memset(onef[:], 1.0).then_inc(rt_const, 1)
            pool.drain()
            pool.wait_ge(rt_const, 5)
            pool.dma_start(table.rearrange("(p n) o -> p (n o)", p=P), tinit[:]).then_inc(tab_out, 16)
            for m, n in ((tri, P), (trif, NE)):
                pool.affine_select(out=m[:], in_=m[:], compare_op=ALU.is_gt, fill=0.0, base=0,
                                   pattern=[[1, n]], channel_multiplier=-1).then_inc(rt_const, 1)
                pool.drain()
            pool.iota(io32[:], pattern=[[1, NE]], base=0, channel_multiplier=0,
                      allow_small_or_imprecise_dtypes=True).then_inc(rt_const, 1)
            pool.drain()
            pool.iota(io16[:], pattern=[[1, MAXX]], base=0, channel_multiplier=0,
                      allow_small_or_imprecise_dtypes=True).then_inc(rt_const, 1)
            pool.drain()
            pool.iota(thr[:], pattern=[[P, NBLK - 1]], base=P, channel_multiplier=0,
                      allow_small_or_imprecise_dtypes=True).then_inc(rt_const, 1)
            pool.drain()
            pool.iota(bval[:], pattern=[[NE, NBLK - 1]], base=NE, channel_multiplier=1,
                      allow_small_or_imprecise_dtypes=True).then_inc(rt_const, 1)
            pool.drain()
            pool.iota(vali[:], pattern=[[TPAD, 2], [P, NT]], base=0, channel_multiplier=1).then_inc(rt_const, 1)
            pool.drain()
            for j in range(12):
                pool.wait_ge(modr_ok, j + 1)
                pool.dma_start(mod_dram[:, j * 512:(j + 1) * 512], modr[:, j % 2, :]).then_inc(mod_out[j % 2], 16)
                if j == 3:
                    for t in range(2, PT):
                        x_load(0, t)
                    pool.wait_ge(aux_ok, 1)
                    pool.wait_ge(consts, N_CONST)
                    for n in range(NS):
                        pool.dma_start(wsS[n * TS:(n + 1) * TS, :, n * TS:(n + 1) * TS],
                                       wsT[0:TS, :, 0:TS]).then_inc(bd_in, 16)

            def tail_out(g, t, rows):
                r0 = t * P + g * PT * P
                pool.dma_start(x1_dram[bass.ds(r0, rows), :], chunk(xres, t)[0:rows, :]).then_inc(x1_out, 16)
                n_ = before_wait(pool, PT * g + t + 1)
                pool.wait_ge(h2_ok, n_)
                pool.dma_start(h2_dram[bass.ds(r0, rows), :], h2s[0:rows, :]).then_inc(h2_out, 16)

            for g in range(2):
                if g == 1:
                    pool.wait_ge(vn_ok, 2 * PT + 1)
                    pool.dma_start(new_v_sample[0].rearrange("n t c -> (n t) c"), v_tok[0:SMP, PT, :]).then_inc(v_out, 16)
                    pool.dma_start(new_a_sample[0, :, 0:HA - TS, :], state_conv_a[0, :, TS:HA, :]).then_inc(st_out, 16)
                    q_wait_read(pool, "stA")
                    q_wait_read(pool, "stC")
                    pool.dma_start(new_a_prompt[0, 0], xs[0:HA, 0, 0:W]).then_inc(st_out, 16)
                    pool.dma_start(new_c_prompt[0, 0], xs[0:HC, 1, 0:W]).then_inc(st_out, 16)
                    for n in range(NS):
                        pool.dma_start(new_a_sample[0, n, HA - TS:HA, :], xs[n * TS:(n + 1) * TS, 0, W:D]).then_inc(st_out, 16)
                        pool.dma_start(new_c_sample[0, n], xs[n * TS + TS - HC:(n + 1) * TS, 1, W:D]).then_inc(st_out, 16)
                    pool.wait_ge(v_out, 16)
                pool.wait_ge(blo_ok, CW * (g + 1))
                for t, rows in tiles(g):
                    pool.dma_start(xres[0:rows, t, :], x_rows(g, t)).then_inc(xres_in, 16)
                if g == 0:
                    for t, _ in tiles(1):
                        x_load(1, t)
                    for s in range(2):
                        pool.wait_ge(mod_out[s], 16 * 6)
                pool.wait_ge(item_mm, item_no(g, GA0 // 2, 0))
                pool.dma_start(B2[:], mod_dram[0:1, 3 * D:4 * D].to_broadcast([P, D])).then_inc(ab_in, 16)
                pool.dma_start(A2[:], mod_dram[0:1, 4 * D:5 * D].to_broadcast([P, D])).then_inc(ab_in, 16)
                q_wait_read(pool, "oT", g, KD - 1)
                if g == 0:
                    with pool.Fori(0, PT) as t:
                        tail_out(0, t, P)
            for t in range(PT):
                tail_out(1, t, P)
            for off, buf in ((3, B2), (4, A2)):
                for n in range(NS):
                    pool.dma_start(buf[n * TS:(n + 1) * TS, :],
                                   mod_dram[1 + n:2 + n, off * D:(off + 1) * D].to_broadcast([TS, D])).then_inc(ab_in, 16)
            tail_out(1, PT, SMP)
            moe_gpsimd(pool)

        @block.scalar
        def _(act):
            act.dma_start(crow[0:1, :], c_prompt).then_inc(c_in, 16)
            act.dma_start(crow[1:9, :], c_sample).then_inc(c_in, 16)

            def par(dst, src):
                act.dma_start(dst, src).then_inc(par_in, 16)

            par(parr[0:KA, :], a_dw_w[0])
            par(parr[KA:PAR_B, :], c_conv_w[0])
            for r, v in ((PAR_B, a_dw_b), (PAR_G, a_norm_g), (PAR_S, a_norm_b)):
                par(parr[r:r + 1, :], v)
            par(parr[PAR_H:NPAR, :], state_conv_c[0].rearrange("n h c -> (n h) c"))
            par(n1r[:], norm1_g[0].rearrange("(k p) -> k p", p=P))
            for a in range(2):
                par(hist[:, a, :], state_conv_a[0, a * TS:(a + 1) * TS].rearrange("n h c -> (n h) c"))
            par(wsr[:], b_spatial_w[0].rearrange("h t s -> t h s"))
            for h in range(HEADS):
                par(s_bias[64 * (h % 2):64 * (h % 2) + 64, h // 2, :], b_spatial_b[0, h:h + 1, :].to_broadcast([64, P]))
            par(bn_g[:], b_norm_g.to_broadcast([P, W]))
            par(bn_b[:], b_norm_b.to_broadcast([P, W]))
            par(n2_b[:], norm2_g.to_broadcast([P, D]))
            par(rb[:, 0:NG], b_router_g.to_broadcast([P, NG]))
            par(rb[:, NG:NR], b_router_e.to_broadcast([P, NE]))
            par(rw[:, :, 0:NG], w_router_g[0].rearrange("(k p) c -> p k c", p=P))
            par(rw[:, :, NG:NR], w_router_e[0].rearrange("(k p) c -> p k c", p=P))

            act.wait_ge(c_in, 32)
            act.activation(csig[:], crow[:], ACT.Sigmoid).then_inc(csig_ok, 1)
            conv_flat = conv[:, :, :].rearrange("p c t -> p (c t)")

            def x_square(g, t):
                n, rows = XN[g, t], dict(tiles(g))[t]
                act.wait_ge(x_in[t % 2], 16 * (XUSE[g, t] + 1))
                if n == 0:
                    act.wait_ge(consts, N_CONST)
                if n:
                    act.wait_ge(x_sq, n)
                act.activation(conv_flat[0:rows, 0:D], xs[0:rows, t % 2, :], ACT.Square,
                               accum_out=ssq[0:rows, n:n + 1]).then_inc(x_sq, 1)

            def h_round(g, t):
                rows = dict(tiles(g))[t]
                q_wait_read(act, "xT", g, t)
                if g and t == 0:
                    act.wait_ge(item_mm, item_no(0, O0 // 2, 0))
                act.activation(h_hi[:, :, t * P:t * P + rows], htmp[:, :, 0:rows], ACT.Copy).then_inc(hhi_ok, 1)

            def w_round(g, u, s, kn=KD):
                act.wait_ge(w_in_sem[s], slot_use(g, u) * 16 + 16)
                if g or first(u):
                    act.wait_ge(item_mm, item_no(g, u, s) - 1)
                act.activation(w_hi[s][:, 0:kn, :], w_raw[s][:, 0:kn, :], ACT.Copy).then_inc(whi_ok, 1)

            x_square(0, 0)
            x_square(0, 1)
            s = q_wait_ready(act, "par")
            act.activation(parT[:], q[s][:, 0, 0:CW * 64].rearrange("p (c n) -> p c n", n=64)[:, :, 0:NPAR],
                           ACT.Copy).then_inc(q_free[s], 1)
            s = q_wait_ready(act, "n1")
            act.activation(n1T[:], q[s][:, 0, 0:KD], ACT.Copy).then_inc(q_free[s], 1)
            s = q_wait_ready(act, "hist")
            for c in range(CW):
                last = act.activation(
                    a_in[:, c, HA + HALF:].rearrange("p (n t) -> p n t", t=AS)[:, :, 0:HA],
                    q[s][:, c // 2, (c % 2) * 240:(c % 2) * 240 + 240].rearrange("p (n h) -> p n h", h=HA), ACT.Copy)
            last.then_inc(q_free[s], 1)
            s = q_wait_ready(act, "ws")
            act.activation(wsT[:], q[s][:, :, :].rearrange("p b (h t) -> p (b h) t", t=P), ACT.Copy).then_inc(q_free[s], 1)
            q_wait_read(act, "par")
            q_wait_read(act, "ws")
            act.activation(p_hist[:], parT[:, :, PAR_H:NPAR], ACT.Copy).then_inc(aux_ok, 1)
            for t in range(2, PT):
                x_square(0, t)
            w_round(0, 0, 0)
            w_round(0, 0, 1)
            for t in range(PT):
                h_round(0, t)

            def tail_squares(g):
                q_wait_read(act, "oT", g, KD - 1)
                if g:
                    q_wait_read(act, "lg", 0, PT - 1)
                for t, rows in tiles(g):
                    if t:
                        act.wait_ge(x1_sq, PT * g + t)
                    act.activation(junk[0:rows, :], xres[0:rows, t, :], ACT.Square,
                                   accum_out=ssq2[0:rows, t:t + 1]).then_inc(x1_sq, 1)

            def tail_tile(g, t, rows=P):
                s = q_wait_ready(act, "h2T", g, 0, more=t)
                act.activation(h2T[:, :, 0:rows], q[s][:, :, :].rearrange("p b (k t) -> p (b k) t", t=P)[:, :, 0:rows],
                               ACT.Copy).then_inc(q_free[s], 1)

            for g in range(2):
                T = TG[g]

                def a_chunk(i):
                    act.wait_ge(item_mm, item_no(g, i, 0) + 1)
                    if g or first(i):
                        act.wait_ge(z_free[1], slot_use(g, i))
                    act.activation(tv(sig, g), zv(0, g), ACT.Sigmoid).then_inc(z_free[0], 1)
                    w_round(g, i + 1, 0)
                    if g:
                        tail_tile(0, i)
                    w_round(g, i + 1, 1)

                if g:
                    tail_squares(0)
                a_chunk(0)
                with act.Fori(1, CW) as i:
                    a_chunk(i)

                def c_chunk(i, u, s0):
                    for k in range(3):
                        uk, s = u + (s0 + k) // 2, (s0 + k) % 2
                        if k == 0:
                            act.wait_ge(item_mm, item_no(g, uk, s) + 1)
                            act.activation(tv(chb, g), zv(s, g), ACT.Copy).then_inc(z_free[s], 1)
                        w_round(g, uk + 1, s)
                        if k == 2:
                            act.wait_ge(z_free[s], slot_use(g, uk) + 1)
                            act.activation(chunk(act0_hi, i)[:, 0:T], cv[:, 0:T], ACT.Copy).then_inc(chi_ok, 1)

                if g == 0:
                    q_wait_ready(act, "ada", 11)
                else:
                    act.wait_ge(x1_sq, PT)
                with act.Fori(0, CW // 2) as i:
                    c_chunk(i * 2, i * 3 + C0 // 2, 0)
                    c_chunk(i * 2 + 1, i * 3 + (C0 // 2 + 1), 1)

                def b_item(i, s):
                    n = i * 2 + (2 * CW * g + s)
                    u = i + B0 // 2
                    act.wait_ge(item_mm, item_no(g, u, s) + 1)
                    act.wait_ge(z_free[1 - s], slot_use(g, u) + s)
                    act.activation(tv(gq, g), zv(s, g), ACT.Square).then_inc(gq_ok, 1)
                    act.wait_ge(gt_ok, n + 1)
                    act.activation(gq[:, 0:T], gt[:, 0:T], ACT.Sigmoid).then_inc(gs_ok, 1)

                def b_chunk(i, kn=KD):
                    b_item(i, 0)
                    w_round(g, i + (B0 // 2 + 1), 0)
                    b_item(i, 1)
                    w_round(g, i + (B0 // 2 + 1), 1, kn)
                    s = q_wait_ready(act, "vT", g, 0, more=i)
                    if g:
                        act.activation(v_tok[0:SMP, PT, bass.ds(i * P, P)], q[s][0:SMP, 1, 0:P], ACT.Copy)
                    act.activation(v_tok[:, 0:PT, bass.ds(i * P, P)],
                                   q[s][:, 0, :].rearrange("p (t c) -> p t c", c=P), ACT.Copy).then_inc(q_free[s], 1)

                if g:
                    act.wait_ge(x1_out, 16 * PT)
                with act.Fori(0, CW - 1) as i:
                    b_chunk(i)
                b_chunk(CW - 1, CW)

                def gate(n0, i, k0=KD, k1=CW):
                    u = i + n0 // 2
                    act.wait_ge(item_mm, item_no(g, u, 0) + 1)
                    act.wait_ge(z_free[1], slot_use(g, u))
                    act.activation(tv(sig, g), zv(0, g), ACT.Sigmoid).then_inc(z_free[0], 1)
                    if k0:
                        w_round(g, u + 1, 0, k0)
                        w_round(g, u + 1, 1, k1)

                with act.Fori(0, KD) as i:
                    gate(GC0, i)
                if g == 0:
                    for s in range(2):
                        act.wait_ge(mod_out[s], 16 * 6)
                else:
                    act.wait_ge(h2_out, 16 * PT)
                    q_wait_read(act, "lg", 0, PT - 1)
                act.wait_ge(bb_ok, PT + g * (PT + 1))
                for c in range(CW):
                    act.activation(act1_hi[:, c, 0:T], u_sb[:, c, 0:T], ACT.Copy).then_inc(bhi_ok, 1)
                if g:
                    for k, rows in ((0, HA), (1, HC)):
                        s = q_wait_ready(act, ("stA", "stC")[k])
                        act.activation(xs[0:rows, k, 0:W], q[s][0:rows, 0, :], ACT.Copy)
                        act.activation(xs[0:SMP, k, W:D], q[s][0:SMP, 1, :], ACT.Copy).then_inc(q_free[s], 1)

                def squares(cs):
                    for c in cs:
                        q_wait_read(act, "mu", g, c)
                        act.activation(a_in[:, c, 0:T], conv[:, c, 0:T], ACT.Square).then_inc(asq_ok, 1)

                def silus(cs):
                    for c in cs:
                        n = CW * g + c
                        q_wait_read(act, "bc", g, c)
                        if n:
                            act.wait_ge(af_ok, n)
                        gain, shift = parT[:, c, PAR_G:PAR_G + 1], parT[:, c, PAR_S:PAR_S + 1]
                        act.activation(gq[:, 0:T], conv[:, c, 0:T], ACT.Sigmoid, bias=shift, scale=gain)
                        act.activation(gt[:, 0:T], conv[:, c, 0:T], ACT.Identity, bias=shift, scale=gain).then_inc(ay_ok, 1)
                        act.wait_ge(af_ok, n + 1)
                        act.activation(act0_hi[:, c, 0:T], conv[:, c, 0:T], ACT.Copy).then_inc(ahi_ok, 1)

                squares(range(3))
                gate(GB0, 0)
                silus(range(3))
                with act.Fori(1, KD - 1) as i:
                    gate(GB0, i)
                squares([3])
                gate(GB0, KD - 1)
                silus([3])
                with act.Fori(0, KD - 1) as i:
                    gate(GA0, i)
                if g == 0:
                    act.wait_ge(alo_ok, CW)
                    x_square(1, 0)
                    x_square(1, 1)
                gate(GA0, KD - 1, None)

                def out_item(j, s, ready=None):
                    u = j + O0 // 2
                    act.wait_ge(item_mm, item_no(g, u, s) + 1)
                    if first(j) or g:
                        if isinstance(j, int):
                            q_wait_ready(act, "oT", g if j else 0, 2 * j - 2 + s if j else KD - 2 + s)
                        else:
                            q_wait_ready(act, "oT", g, 2 + s, more=j - 2)
                    n = j * 2 + (2 * KD + s)
                    g1 = modT[:, n, 0:1] if isinstance(n, int) else \
                        modT[:, bass.ds(n, 1), 0:1].rearrange("p a b -> p (a b)")
                    for src, t0, t1 in zparts(s, g):
                        last = act.activation(ot[s][:, t0:t1], src, ACT.Copy, scale=g1)
                    last.then_inc(ot_ok if g else z_free[s], 1)

                if g == 0:
                    h_round(1, 0)
                    h_round(1, 1)
                    x_square(1, 2)
                    x_square(1, 3)
                out_item(0, 0)
                out_item(0, 1)
                if g == 0:
                    h_round(1, 2)
                    h_round(1, 3)
                    x_square(1, 4)
                out_item(1, 0)
                out_item(1, 1)
                if g == 0:
                    h_round(1, 4)
                with act.Fori(2, KD // 2) as j:
                    out_item(j, 0)
                    out_item(j, 1)
                if g == 0:
                    w_round(1, 0, 0)
                    w_round(1, 0, 1)
            tail_squares(1)
            for t, rows in tiles(1):
                tail_tile(1, t, rows)
            moe_scalar(act)

        @block.vector
        def _(dve):
            def tt(out, a, b, op):
                return dve.tensor_tensor(out, a, b, op)

            def rsqrt(y, v, t):
                dve.drain()
                dve.tensor_scalar(y.bitcast(I32), v.bitcast(I32), 1, None, ALU.logical_shift_right)
                dve.drain()
                dve.tensor_scalar(y.bitcast(I32), y.bitcast(I32), -1, MAGIC, ALU.mult, ALU.add)
                for _ in range(3):
                    dve.drain()
                    tt(t, y, y, ALU.mult)
                    dve.drain()
                    dve.scalar_tensor_tensor(t, v, -0.5, t, ALU.mult, ALU.mult)
                    dve.drain()
                    last = dve.scalar_tensor_tensor(y, t, 1.5, y, ALU.add, ALU.mult)
                return last

            def w_low(g, u, s, kn=KD):
                dve.wait_ge(whi_ok, split_no(g, u, s) + 1)
                tt(w_lo[s][:, 0:kn, :], w_raw[s][:, 0:kn, :], w_hi[s][:, 0:kn, :].bitcast(F32),
                   ALU.subtract).then_inc(wlo_ok, 1)

            def x_norm(g, t):
                n, rows = XN[g, t], dict(tiles(g))[t]
                dve.wait_ge(x_sq, n + 1)
                v, y, tm = (a[0:rows, n:n + 1] for a in (nv, ny, nt_))
                dve.tensor_scalar(v, ssq[0:rows, n:n + 1], 1.0 / D, EPS, ALU.mult, ALU.add)
                rsqrt(y, v, tm)
                dve.drain()
                x = xs[0:rows, t % 2, :]
                dve.tensor_scalar(x, x, y, None, ALU.mult).then_inc(x_n, 1)

            def x_mod(g, t):
                rows = dict(tiles(g))[t]
                dve.drain()
                s = q_wait_ready(dve, "xT", g, t)
                ps = q[s][:, :, :].rearrange("p b (k t) -> p (b k) t", t=P)
                if t < PT:
                    for k in range(KD):
                        last = dve.tensor_scalar(htmp[:, k, :], ps[:, k, :], modT[:, KD + k, 0:1], modT[:, k, 0:1],
                                                 ALU.mult, ALU.add)
                else:
                    for k in range(KD):
                        dve.tensor_tensor(seqs(htmp[:, k, 0:SMP]), seqs(ps[:, k, 0:SMP]),
                                          modT[:, KD + k, 1:9].unsqueeze(2).to_broadcast([P, NS, TS]), ALU.mult)
                    dve.drain()
                    for k in range(KD):
                        last = dve.tensor_tensor(seqs(htmp[:, k, 0:SMP]), seqs(htmp[:, k, 0:SMP]),
                                                 modT[:, k, 1:9].unsqueeze(2).to_broadcast([P, NS, TS]), ALU.add)
                last.then_inc(q_free[s], 1)
                dve.wait_ge(hhi_ok, XN[g, t] + 1)
                if g and t == 0:
                    dve.wait_ge(item_mm, item_no(0, O0 // 2, 0))
                tt(h_lo[:, :, t * P:t * P + rows], htmp[:, :, 0:rows],
                   h_hi[:, :, t * P:t * P + rows].bitcast(F32), ALU.subtract).then_inc(hlo_ok, 1)

            dve.wait_ge(csig_ok, 1)
            tt(crow[:], crow[:], csig[:], ALU.mult).then_inc(sic_ok, 1)
            s = q_wait_ready(dve, "sic")
            dve.tensor_copy(sicT[:], q[s][:, 0, 0:KD * 9].rearrange("p (k n) -> p k n", n=9)).then_inc(q_free[s], 1)

            def ada_piece(j):
                dve.wait_ge(bada_in[j % 2], 16 * (j // 2 + 1))
                if j >= 2:
                    dve.wait_ge(mod_out[j % 2], 16 * (j // 2))
                    if j - 2 < 6:
                        q_wait_ready(dve, "modT", j - 2)
                s = q_wait_ready(dve, "ada", j)
                tt(modr[:, j % 2, :], q[s][0:9, 0, :], badar[:, j % 2, :], ALU.add).then_inc(modr_ok, 1)
                if j < 6:
                    s = q_wait_ready(dve, "modT", j)
                    dve.tensor_copy(modT[:, 4 * j:4 * j + 4, :], q[s][:, 0, 0:36].rearrange("p (k n) -> p k n", n=9)
                                    ).then_inc(q_free[s], 1)

            x_norm(0, 0)
            x_norm(0, 1)
            for j in range(4):
                ada_piece(j)
            q_wait_read(dve, "n1")
            dve.drain()
            for k in range(KD):
                dve.tensor_scalar(modT[:, KD + k, :], modT[:, KD + k, :], 1.0, n1T[:, k:k + 1], ALU.add, ALU.mult)
            dve.drain()
            x_mod(0, 0)
            x_norm(0, 2)
            x_mod(0, 1)
            x_norm(0, 3)
            w_low(0, 0, 0)
            w_low(0, 0, 1)
            x_mod(0, 2)
            x_mod(0, 3)

            def smp_in(ap, seq, h):
                return ap.rearrange("p (n t) -> p n t", t=seq)[:, :, h:seq]

            def conv_taps(g, c, k, first_tap=False):
                src = chunk(a_in, c)
                wt = parT[:, c, k:k + 1] if isinstance(k, int) else parT[:, c, bass.ds(k, 1)]
                parts = [(conv[:, c, 0:HALF], src[:, bass.ds(k, HALF)])]
                if g:
                    parts.append((seqs(conv[:, c, HALF:TM]),
                                  src[:, HA + HALF:].rearrange("p (n t) -> p n t", t=AS)[:, :, bass.ds(k, TS)]))
                dve.drain()
                for out, x in parts:
                    if first_tap:
                        last = dve.tensor_scalar(out, x, wt, parT[:, c, PAR_B:PAR_B + 1], ALU.mult, ALU.add)
                    else:
                        last = dve.scalar_tensor_tensor(out, x, wt, out, ALU.mult, ALU.add)
                return last

            def tail_h2(g, t, rows=P):
                n = PT * g + t
                if first(n):
                    dve.wait_ge(h2_out, n * 16)
                    q_wait_ready(dve, "h2T", g, 0, more=t - 1) if first(t) else q_wait_ready(dve, "h2T", 0, PT - 1)
                y = r2y[0:rows, t:t + 1] if isinstance(t, int) else r2y[0:rows, bass.ds(t, 1)]
                dve.scalar_tensor_tensor(h2s[0:rows, :], chunk(xres, t)[0:rows, :], y, A2[0:rows, :], ALU.mult, ALU.mult)
                dve.drain()
                tt(h2s[0:rows, :], h2s[0:rows, :], B2[0:rows, :], ALU.add).then_inc(h2_ok, 1)

            def tail_logits(g, t, rows=P):
                s = q_wait_ready(dve, "lg", g, 0, more=t)
                dst = logit[0:rows, t + PT * g, :] if isinstance(t, int) else \
                    logit[0:rows, bass.ds(t, 1), :].rearrange("p o r -> p (o r)")
                tt(dst, q[s][0:rows, 0, 0:NR], rb[0:rows, :], ALU.add).then_inc(q_free[s], 1)

            def tail_start(g):
                nt = PT + g
                dve.wait_ge(x1_sq, PT + g * (PT + 1))
                dve.tensor_scalar(nv[:, 0:nt], ssq2[:, 0:nt], 1.0 / D, EPS, ALU.mult, ALU.add)
                rsqrt(r2y[:, 0:nt], nv[:, 0:nt], nt_[:, 0:nt])
                dve.wait_ge(ab_in, 32 * (g + 1))
                dve.scalar_tensor_tensor(A2[:], A2[:], 1.0, n2_b[:], ALU.add, ALU.mult)
                dve.drain()

            for g in range(2):
                T = TG[g]

                def a_chunk(i):
                    w_low(g, i + 1, 0)
                    s = 1
                    dve.wait_ge(z_free[0], slot_use(g, i) + 1)
                    dve.wait_ge(item_mm, item_no(g, i, 1) + 1)
                    dst = chunk(a_in, i)
                    if g:
                        tt(smp_in(dst[:, HA + HALF:], AS, HA), seqs(zsample(s)), seqs(sig[:, HALF:TM]), ALU.mult)
                    for src, t0, t1 in zparts(s, g):
                        last = tt(dst[:, HA + t0:HA + t1], src, sig[:, t0:t1], ALU.mult)
                    last.then_inc(z_free[1], 1)
                    w_low(g, i + 1, 1)
                    dve.drain()
                    tail = chunk(a_tail, i)
                    dve.tensor_copy(tail[:, 0:HA], dst[:, HALF:HALF + HA])
                    if g:
                        dve.tensor_copy(seqs(tail[:, HA:]), smp_in(dst[:, HA + HALF:], AS, HA))

                if g == 0:
                    dve.wait_ge(consts, N_CONST)
                    q_wait_read(dve, "hist")
                    dve.wait_ge(aux_ok, 1)
                    a_chunk(0)
                    with dve.Fori(1, CW) as i:
                        a_chunk(i)
                    for j in range(4, 12):
                        ada_piece(j)
                else:
                    dve.tensor_copy(a_in[:, :, 0:HA], a_tail[:, :, 0:HA])
                    tail_start(0)
                    tail_h2(0, 0)
                    a_chunk(0)
                    tail_logits(0, 0)
                    with dve.Fori(1, CW) as i:
                        tail_h2(0, i)
                        a_chunk(i)
                        tail_logits(0, i)

                def c_chunk(i, u, s0, taps):
                    (uh, sh), (uc, sc), (ub, sb_) = ((u + (s0 + k) // 2, (s0 + k) % 2) for k in range(3))
                    w_low(g, uh + 1, sh)
                    if g:
                        dve.tensor_copy(p_in[:, 0:HC], chunk(p_tail, i)[:, 0:HC])
                        dve.tensor_copy(p_in[:, HC + HALF:].rearrange("p (n t) -> p n t", t=CS)[:, :, 0:HC],
                                        chunk(p_hist, i).rearrange("p (n h) -> p n h", h=HC))
                    for k in taps[:len(taps) // 2]:
                        conv_taps(g, 0, k)
                    dve.wait_ge(z_free[sh], slot_use(g, uh) + 1)
                    dve.wait_ge(item_mm, item_no(g, uc, sc) + 1)
                    if g:
                        tt(smp_in(p_in[:, HC + HALF:], CS, HC), seqs(zsample(sc)), seqs(chb[:, HALF:TM]), ALU.mult)
                    for src, t0, t1 in zparts(sc, g):
                        last = tt(p_in[:, HC + t0:HC + t1], src, chb[:, t0:t1], ALU.mult)
                    last.then_inc(z_free[sc], 1)
                    w_low(g, uc + 1, sc)
                    dve.drain()
                    tail = chunk(p_tail, i)
                    dve.tensor_copy(tail[:, 0:HC], p_in[:, HALF:HALF + HC])
                    if g:
                        dve.tensor_copy(seqs(tail[:, HC:]), smp_in(p_in[:, HC + HALF:], CS, HC))
                    for k in range(KC):
                        dve.drain()
                        wt = parT[:, i, KA + k:KA + k + 1] if isinstance(i, int) else \
                            parT[:, bass.ds(i, 1), KA + k:KA + k + 1].rearrange("p a b -> p (a b)")
                        parts = [(cv[:, 0:HALF], p_in[:, k:k + HALF])]
                        if g:
                            parts.append((seqs(cv[:, HALF:TM]),
                                          p_in[:, HC + HALF:].rearrange("p (n t) -> p n t", t=CS)[:, :, k:k + TS]))
                        for out, x in parts:
                            if k == 0:
                                dve.tensor_scalar(out, x, wt, None, ALU.mult)
                            else:
                                dve.scalar_tensor_tensor(out, x, wt, out, ALU.mult, ALU.add)
                    for k in taps[len(taps) // 2:]:
                        conv_taps(g, 0, k)
                    dve.drain()
                    dve.wait_ge(item_mm, item_no(g, ub, sb_) + 1)
                    tt(tv(cv, g), zv(sb_, g), tv(cv, g), ALU.mult).then_inc(z_free[sb_], 1)
                    w_low(g, ub + 1, sb_)
                    n = i + CW * g
                    dve.wait_ge(chi_ok, n + 1)
                    tt(chunk(act0_lo, i)[:, 0:T], cv[:, 0:T], chunk(act0_hi, i)[:, 0:T].bitcast(F32),
                       ALU.subtract).then_inc(clo_ok, 1)

                conv_taps(g, 0, 0, True)
                with dve.Fori(0, CW // 2) as i:
                    c_chunk(i * 2, i * 3 + C0 // 2, 0, [i * 15 + (1 + k) for k in range(8)])
                    c_chunk(i * 2 + 1, i * 3 + (C0 // 2 + 1), 1, [i * 15 + (9 + k) for k in range(7)])
                cnv = [CW * g]

                def b_item(i, s):
                    n = i * 2 + (2 * CW * g + s)
                    u = i + B0 // 2
                    dve.wait_ge(gq_ok, n + 1)
                    dve.tensor_scalar(gt[:, 0:T], gq[:, 0:T], GELU1, GELU0, ALU.mult, ALU.add)
                    dve.drain()
                    tt(tv(gt, g), tv(gt, g), zv(s, g), ALU.mult).then_inc(gt_ok, 1)
                    dst = vT
                    if s == 0:
                        if first(i):
                            q_wait_ready(dve, "vT", g, 0, more=i - 1)
                        out = tv(vT, g)
                    else:
                        out = tv(chunk(u_sb, i), g)
                    dve.wait_ge(gs_ok, n + 1)
                    tt(out, tv(gq, g), zv(s, g), ALU.mult).then_inc(z_free[s], 1)

                def b_chunk(i, taps, kn=KD):
                    b_item(i, 0)
                    w_low(g, i + (B0 // 2 + 1), 0)
                    for k in taps[:4]:
                        conv_taps(g, 1, k)
                    b_item(i, 1)
                    w_low(g, i + (B0 // 2 + 1), 1, kn)
                    for k in taps[4:]:
                        conv_taps(g, 1, k)

                if g:
                    dve.wait_ge(x1_out, 16 * PT)
                conv_taps(g, 1, 0, True)
                b_chunk(0, range(1, 9))
                with dve.Fori(1, CW - 1) as i:
                    b_chunk(i, [i * 8 + (k + 1) for k in range(8)])
                b_chunk(CW - 1, range(25, 31), CW)

                def gated(b, n0, i, k0=KD, k1=CW):
                    u = i + n0 // 2
                    if k0:
                        w_low(g, u + 1, 0, k0)
                    dve.wait_ge(z_free[0], slot_use(g, u) + 1)
                    dve.wait_ge(item_mm, item_no(g, u, 1) + 1)
                    m = chunk(macc, i)
                    if b == NB_C:
                        tt(tv(m, g), zv(1, g), tv(sig, g), ALU.mult).then_inc(z_free[1], 1)
                    else:
                        tt(tv(chb, g), zv(1, g), tv(sig, g), ALU.mult).then_inc(z_free[1], 1)
                        dve.drain()
                        last = tt(m[:, 0:T], m[:, 0:T], chb[:, 0:T], ALU.add)
                        if b == NB_A:
                            last.then_inc(macc_ok, 1)
                    if k0:
                        w_low(g, u + 1, 1, k1)

                def v_norm(t, rows=P):
                    v = chunk(v_tok, t)[0:rows, :]
                    dve.bn_stats(bn6[0:rows, :], v)
                    dve.drain()
                    dve.bn_aggr(mv[0:rows, :], bn6[0:rows, :])
                    dve.drain()
                    dve.tensor_scalar(nv[0:rows, 0:1], mv[0:rows, 1:2], EPS, None, ALU.add)
                    rsqrt(ny[0:rows, 0:1], nv[0:rows, 0:1], nt_[0:rows, 0:1])
                    dve.drain()
                    dve.tensor_scalar(v, v, mv[0:rows, 0:1], ny[0:rows, 0:1], ALU.subtract, ALU.mult)
                    dve.drain()
                    tt(v, v, bn_g[0:rows, :], ALU.mult)
                    dve.drain()
                    tt(v, v, bn_b[0:rows, :], ALU.add).then_inc(vn_ok, 1)

                def spatial(t, rows=P):
                    s = q_wait_ready(dve, "sp", g, t)
                    tmp = gt[:, 0:CW * rows].rearrange("p (c t) -> p c t", t=rows)
                    src = q[s][:, 0, 0:CW * rows].rearrange("p (c t) -> p c t", t=rows)
                    ut = u_sb[:, :, t * P:t * P + rows]
                    dve.drain()
                    if rows == P:
                        tt(tmp, src, s_bias[:], ALU.add).then_inc(q_free[s], 1)
                    else:
                        for c in range(CW):
                            last = tt(seqs(tmp[:, c, :]), seqs(src[:, c, :]),
                                      s_bias[:, c:c + 1, 0:TS].to_broadcast([P, NS, TS]), ALU.add)
                        last.then_inc(q_free[s], 1)
                    dve.drain()
                    tt(ut, tmp, ut, ALU.mult).then_inc(bb_ok, 1)

                conv_taps(g, 2, 0, True)
                q_wait_read(dve, "vT", g, CW - 1)
                if g:
                    v_norm(PT, SMP)
                with dve.Fori(0, PT) as i:
                    gated(NB_C, GC0, i)
                    v_norm(i)
                    for k in range(3):
                        conv_taps(g, 2, i * 3 + (1 + k))
                k = 1 + 3 * PT
                for i in range(PT, KD):
                    gated(NB_C, GC0, i)
                    spatial(i - PT)
                    for _ in range(4 if i < KD - 2 else 5):
                        last = conv_taps(g, 2, k)
                        k += 1
                assert k == KA
                last.then_inc(cnv_ok, 1)
                if g:
                    spatial(PT, SMP)
                for c in range(CW):
                    dve.wait_ge(bhi_ok, CW * g + c + 1)
                    tt(act1_lo[:, c, 0:T], u_sb[:, c, 0:T], act1_hi[:, c, 0:T].bitcast(F32), ALU.subtract).then_inc(blo_ok, 1)

                def parts_of(c, s):
                    p = [(conv[:, c, 0:HALF], q[s][:, 0, :])]
                    return p + [(conv[:, c, HALF:TM], q[s][:, 1, 0:SMP])] if g else p

                def centre(cs):
                    for c in cs:
                        s = q_wait_ready(dve, "mu", g, c)
                        for x, m in parts_of(c, s):
                            last = tt(x, x, m, ALU.subtract)
                        last.then_inc(q_free[s], 1)

                def inverse(cs):
                    c0, n = cs[0], len(cs)
                    s = q_wait_ready(dve, "var", g, c0)
                    src = q[s][:, 0, 0:CW * (PT + 1) * 2].rearrange("p (c t j) -> p c t j", c=CW, j=2)
                    cc = slice(c0, c0 + n)
                    for t, rows in tiles(g):
                        last = dve.tensor_scalar(rs_v[0:rows, cc, t, :], src[0:rows, cc, t, :], EPS, None, ALU.add)
                    last.then_inc(q_free[s], 1)
                    a, b, c = (x[:, cc, :, :].rearrange("p c t j -> p (c t j)") for x in (rs_y, rs_v, rs_t))
                    rsqrt(a, b, c).then_inc(rs_ok, 1)

                def normed(c):
                    s = q_wait_ready(dve, "bc", g, c)
                    for x, m in parts_of(c, s):
                        last = tt(x, x, m, ALU.mult)
                    last.then_inc(q_free[s], 1)

                def silus(cs):
                    normed(cs[0])
                    for c in cs:
                        n = CW * g + c
                        if c + 1 in cs:
                            normed(c + 1)
                        dve.wait_ge(ay_ok, n + 1)
                        tt(conv[:, c, 0:T], gq[:, 0:T], gt[:, 0:T], ALU.mult).then_inc(af_ok, 1)
                        dve.wait_ge(ahi_ok, n + 1)
                        tt(act0_lo[:, c, 0:T], conv[:, c, 0:T], act0_hi[:, c, 0:T].bitcast(F32), ALU.subtract).then_inc(alo_ok, 1)

                centre(range(3))
                conv_taps(g, 3, 0, True)
                gated(NB_B, GB0, 0)
                inverse(range(3))
                silus(range(3))
                with dve.Fori(1, KD - 2) as i:
                    gated(NB_B, GB0, i)
                    for k in range(5):
                        conv_taps(g, 3, i * 5 + (k - 4))
                gated(NB_B, GB0, KD - 2)
                for k in range(26, 31):
                    last = conv_taps(g, 3, k)
                last.then_inc(cnv_ok, 1)
                centre([3])
                gated(NB_B, GB0, KD - 1)
                inverse([3])
                silus([3])
                with dve.Fori(0, KD - 1) as i:
                    gated(NB_A, GA0, i)
                if g == 0:
                    x_norm(1, 0)
                    x_norm(1, 1)
                gated(NB_A, GA0, KD - 1, None)

                def out_smp(j, s):
                    if not g:
                        return
                    n = j * 2 + (2 * KD + s)
                    g1 = modT[:, n, 1:9] if isinstance(n, int) else modT[:, bass.ds(n, 1), 1:9].rearrange("p a b -> p (a b)")
                    dve.wait_ge(ot_ok, j * 2 + (s + 1))
                    tt(seqs(ot[s][:, HALF:TM]), seqs(zsample(s)), g1.unsqueeze(2).to_broadcast([P, NS, TS]),
                       ALU.mult).then_inc(z_free[s], 1)

                def out_add(j, s):
                    if isinstance(j, int):
                        q_wait_ready(dve, "oT", g, 2 * j + s)
                    else:
                        q_wait_ready(dve, "oT", g, 2 + s, more=j - 1)
                    lo = j * (2 * P) + s * P
                    x = xres[:, 0:PT, bass.ds(lo, P)]
                    if g:
                        xx = xres[0:SMP, PT, bass.ds(lo, P)]
                        tt(xx, q[s][0:SMP, 1, 0:P], xx, ALU.add)
                    tt(x, q[s][:, 0, :].rearrange("p (t c) -> p t c", c=P), x, ALU.add).then_inc(q_free[s], 1)

                if g == 0:
                    x_mod(1, 0)
                    x_mod(1, 1)
                    x_norm(1, 2)
                    x_norm(1, 3)
                    x_mod(1, 2)
                    x_mod(1, 3)
                    x_norm(1, 4)
                out_smp(0, 0)
                out_smp(0, 1)
                dve.wait_ge(xres_in, 16 * (PT + g * (PT + 1)))
                out_add(0, 0)
                out_smp(1, 0)
                out_add(0, 1)
                out_smp(1, 1)
                if g == 0:
                    x_mod(1, 4)
                with dve.Fori(2, KD // 2) as j:
                    out_add(j - 1, 0)
                    out_smp(j, 0)
                    out_add(j - 1, 1)
                    out_smp(j, 1)
                out_add(KD // 2 - 1, 0)
                out_add(KD // 2 - 1, 1)
                if g == 0:
                    w_low(1, 0, 0)
                    w_low(1, 0, 1)
            tail_start(1)
            for t in range(PT):
                tail_h2(1, t)
                if t:
                    tail_logits(1, t - 1)
            dve.wait_ge(ab_in, 16 * (4 + 2 * NS))
            dve.scalar_tensor_tensor(A2[0:SMP, :], A2[0:SMP, :], 1.0, n2_b[0:SMP, :], ALU.add, ALU.mult)
            dve.drain()
            tail_h2(1, PT, SMP)
            tail_logits(1, PT - 1)
            tail_logits(1, PT, SMP)
            moe_vector(dve)

        @block.tensor
        def _(pe):
            def transposed(out, src):
                n = src.shape[0]
                return pe.transpose(out, src, ident[0:n, 0:n])

            pe.wait_ge(par_in, 16 * N_PAR)
            pe.wait_ge(consts, N_CONST)
            for c in range(CW):
                last = transposed(q[0][:, 0, c * 64:c * 64 + NPAR], parr[:, c * P:(c + 1) * P])
            last.then_inc(q_ready[0], 1)
            transposed(q[1][:, 0, 0:KD], n1r[:]).then_inc(q_ready[1], 1)
            s = q_wait_free(pe, "hist")
            for c in range(CW):
                for a in range(2):
                    o = (c % 2) * 240 + a * HA * TS
                    last = transposed(q[s][:, c // 2, o:o + HA * TS], hist[:, a, c * P:(c + 1) * P])
            last.then_inc(q_ready[s], 1)
            s = q_wait_free(pe, "ws")
            for h in range(HEADS):
                last = transposed(q[s][:, h // 4, (h % 4) * P:(h % 4 + 1) * P], wsr[:, h, :])
            last.then_inc(q_ready[s], 1)
            s = q_wait_free(pe, "sic")
            pe.wait_ge(sic_ok, 1)
            for k in range(KD):
                last = transposed(q[s][:, 0, 9 * k:9 * k + 9], crow[:, k * P:(k + 1) * P])
            last.then_inc(q_ready[s], 1)
            q_wait_read(pe, "sic")

            def ada_piece(j):
                if j:
                    pe.wait_ge(modr_ok, j)
                pe.wait_ge(ada_in[j % 2], 16 * (j // 2 + 1))
                for k in range(KD):
                    last = pe.matmul(q[0][0:9, 0, :], sicT[:, k, :], ada[:, j % 2, k, :], start=(k == 0), stop=(k == KD - 1))
                last.then_inc(q_ready[0], 1)
                if j < 6:
                    s = q_wait_free(pe, "modT", j)
                    pe.wait_ge(modr_ok, j + 1)
                    for c in range(4):
                        last = transposed(q[s][:, 0, 9 * c:9 * c + 9], modr[:, j % 2, c * P:(c + 1) * P])
                    last.then_inc(q_ready[s], 1)

            for j in range(4):
                ada_piece(j)

            def x_transpose(g, t):
                s, rows = q_wait_free(pe, "xT", g, t), dict(tiles(g))[t]
                pe.wait_ge(x_n, XN[g, t] + 1)
                for k in range(KD):
                    last = transposed(q[s][:, k // 4, (k % 4) * P:(k % 4) * P + rows], xs[0:rows, t % 2, k * P:(k + 1) * P])
                last.then_inc(q_ready[s], 1)

            pe.wait_ge(modr_ok, 4)
            for t in range(PT):
                x_transpose(0, t)

            def item(g, u, s, hi, lo, kn=KD):
                pe.wait_ge(wlo_ok, split_no(g, u, s) + 1)
                if g or first(u):
                    pe.wait_ge(z_free[s], slot_use(g, u))
                for b, t0, t1 in halves(g):
                    for k in range(kn):
                        out = z[s][:, b, 0:t1 - t0]
                        pe.matmul(out, w_hi[s][:, k, :], hi[:, k, t0:t1], start=(k == 0), stop=False)
                        pe.matmul(out, w_hi[s][:, k, :], lo[:, k, t0:t1], start=False, stop=False)
                        last = pe.matmul(out, w_lo[s][:, k, :], hi[:, k, t0:t1], start=False, stop=(k == kn - 1))
                last.then_inc(item_mm, 1)

            def h2_transpose(g, t, rows=P):
                s, n0 = QUSE["h2T", g, 0]
                pe.wait_ge(q_free[s], n0 + t)
                pe.wait_ge(h2_ok, t + (PT * g + 1))
                for k in range(KD):
                    last = transposed(q[s][:, k // 4, (k % 4) * P:(k % 4) * P + rows], h2s[0:rows, k * P:(k + 1) * P])
                last.then_inc(q_ready[s], 1)

            def logits(g, t, rows=P):
                q_wait_read(pe, "h2T", g, 0, more=t)
                s, n0 = QUSE["lg", g, 0]
                pe.wait_ge(q_free[s], n0 + t)
                for k in range(KD):
                    last = pe.matmul(q[s][0:rows, 0, 0:NR], h2T[:, k, 0:rows], rw[:, k, :], start=(k == 0), stop=(k == KD - 1))
                last.then_inc(q_ready[s], 1)

            for g in range(2):
                T = TG[g]
                pe.wait_ge(hlo_ok, PT + g * (PT + 1))
                item(g, 0, 0, h_hi, h_lo)
                if g:
                    h2_transpose(0, 0)
                item(g, 0, 1, h_hi, h_lo)
                if g:
                    logits(0, 0)
                with pe.Fori(1, CW) as i:
                    item(g, i, 0, h_hi, h_lo)
                    if g:
                        h2_transpose(0, i)
                    item(g, i, 1, h_hi, h_lo)
                    if g:
                        logits(0, i)
                if g == 0:
                    for j in range(4, 12):
                        if j == 4:
                            q_wait_free(pe, "ada", 4)
                        ada_piece(j)
                    pe.wait_ge(modr_ok, 12)
                with pe.Fori(0, CW // 2) as i:
                    for k in range(6):
                        item(g, i * 3 + (C0 // 2 + k // 2), k % 2, h_hi, h_lo)

                def v_chunk(i):
                    item(g, i + B0 // 2, 0, h_hi, h_lo)
                    item(g, i + B0 // 2, 1, h_hi, h_lo)
                    s, n0 = QUSE["vT", g, 0]
                    pe.wait_ge(q_free[s], i + n0)
                    pe.wait_ge(z_free[0], slot_use(g, i + B0 // 2) + 1)
                    for t, rows in tiles(g):
                        last = transposed(q[s][0:rows, t // PT, (t % PT) * P:(t % PT) * P + P], vT[:, t * P:t * P + rows])
                    last.then_inc(q_ready[s], 1)

                with pe.Fori(0, CW) as i:
                    v_chunk(i)

                def pairs(n0, lo, hi_, xh, xl):
                    if hi_ == lo + 1:
                        item(g, lo + n0 // 2, 0, h_hi, h_lo)
                        item(g, lo + n0 // 2, 1, xh, xl, CW)
                        return
                    with pe.Fori(lo, hi_) as i:
                        item(g, i + n0 // 2, 0, h_hi, h_lo)
                        item(g, i + n0 // 2, 1, xh, xl, CW)

                pe.wait_ge(clo_ok, CW * (g + 1))
                pairs(GC0, 0, PT, act0_hi, act0_lo)
                def spatial(t, rows=P):
                    s = q_wait_free(pe, "sp", g, t)
                    pe.wait_ge(vn_ok, PT + g * (PT + 1))
                    if t == PT:
                        pe.wait_ge(bd_in, 16 * NS)
                    for h in range(HEADS):
                        ws = wsT[:, h, :] if t < PT else wsS[:, h, :]
                        last = pe.matmul(q[s][64 * (h % 2):64 * (h % 2) + 64, 0, (h // 2) * rows:(h // 2 + 1) * rows],
                                         v_tok[0:rows, t, 64 * h:64 * h + 64], ws, start=True, stop=True)
                    last.then_inc(q_ready[s], 1)

                spatial(0)
                for i in range(PT, KD):
                    if i - PT + 1 < PT:
                        spatial(i - PT + 1)
                    elif g:
                        spatial(PT, SMP)
                    pairs(GC0, i, i + 1, act0_hi, act0_lo)
                if g:
                    for name, src, n in (("stA", a_tail, HA), ("stC", p_tail, HC)):
                        s = q_wait_free(pe, name)
                        for c in range(CW):
                            transposed(q[s][0:n, 0, c * P:(c + 1) * P], src[:, c, 0:n])
                            last = transposed(q[s][0:SMP, 1, c * P:(c + 1) * P], src[:, c, n:n + SMP])
                        last.then_inc(q_ready[s], 1)

                def mean(c, n_cnv):
                    s = q_wait_free(pe, "mu", g, c)
                    pe.wait_ge(cnv_ok, n_cnv)
                    last = pe.matmul(q[s][:, 0, :], blk64[:], conv[:, c, 0:HALF], start=True, stop=True)
                    if g:
                        last = pe.matmul(q[s][:, 1, 0:SMP], blk64[:], conv[:, c, HALF:TM], start=True, stop=True)
                    last.then_inc(q_ready[s], 1)

                def variance(cs):
                    s = q_wait_free(pe, "var", g, cs[0])
                    for c in cs:
                        pe.wait_ge(asq_ok, CW * g + c + 1)
                        for t, rows in tiles(g):
                            o = (c * (PT + 1) + t) * 2
                            last = pe.matmul(q[s][0:rows, 0, o:o + 2], a_in[:, c, t * P:t * P + rows], blk2[:], start=True, stop=True)
                    last.then_inc(q_ready[s], 1)

                def spread(c, n_rs):
                    s = q_wait_free(pe, "bc", g, c)
                    pe.wait_ge(rs_ok, n_rs)
                    for t, rows in tiles(g):
                        for j in range(2):
                            last = pe.matmul(q[s][64 * j:64 * j + 64, t // PT, (t % PT) * P:(t % PT) * P + rows],
                                             rs_y[0:rows, c, t, j:j + 1].to_broadcast([rows, 64]),
                                             ident[0:rows, 0:rows], start=True, stop=True)
                    last.then_inc(q_ready[s], 1)

                for c in range(3):
                    mean(c, 2 * g + 1)
                pe.wait_ge(blo_ok, CW * (g + 1))
                item(g, GB0 // 2, 0, h_hi, h_lo)
                variance(range(3))
                item(g, GB0 // 2, 1, act1_hi, act1_lo, CW)
                for c in range(3):
                    spread(c, 2 * g + 1)
                pairs(GB0, 1, KD - 1, act1_hi, act1_lo)
                mean(3, 2 * g + 2)
                item(g, GB0 // 2 + KD - 1, 0, h_hi, h_lo)
                variance([3])
                item(g, GB0 // 2 + KD - 1, 1, act1_hi, act1_lo, CW)
                spread(3, 2 * g + 2)
                item(g, GA0 // 2, 0, h_hi, h_lo)
                pe.wait_ge(alo_ok, CW * (g + 1))
                item(g, GA0 // 2, 1, act0_hi, act0_lo, CW)
                pairs(GA0, 1, KD, act0_hi, act0_lo)

                def out_item(j, s):
                    u = j + O0 // 2
                    pe.wait_ge(w_in_sem[s], slot_use(g, u) * 16 + 16)
                    pe.wait_ge(z_free[s], slot_use(g, u))
                    for b, t0, t1 in halves(g):
                        for k in range(KD):
                            last = pe.matmul(z[s][:, b, 0:t1 - t0], w_raw[s][:, k, :], macc[:, k, t0:t1],
                                             start=(k == 0), stop=(k == KD - 1))
                    last.then_inc(item_mm, 1)

                def out_transpose(j, s):
                    if isinstance(j, int):
                        q_wait_free(pe, "oT", g, 2 * j + s)
                    else:
                        pe.wait_ge(q_free[s], QUSE["oT", g, 2 + s][1] + (j - 1))
                    pe.wait_ge(z_free[s], slot_use(g, j + O0 // 2) + 1)
                    for t, rows in tiles(g):
                        last = transposed(q[s][0:rows, t // PT, (t % PT) * P:(t % PT) * P + P], ot[s][:, t * P:t * P + rows])
                    last.then_inc(q_ready[s], 1)

                if g == 0:
                    x_transpose(1, 0)
                    x_transpose(1, 1)
                pe.wait_ge(macc_ok, KD * (g + 1))
                out_item(0, 0)
                out_item(0, 1)
                if g == 0:
                    x_transpose(1, 2)
                    x_transpose(1, 3)
                out_transpose(0, 0)
                out_item(1, 0)
                out_transpose(0, 1)
                out_item(1, 1)
                if g == 0:
                    x_transpose(1, 4)
                with pe.Fori(2, KD // 2) as j:
                    out_transpose(j - 1, 0)
                    out_item(j, 0)
                    out_transpose(j - 1, 1)
                    out_item(j, 1)
                out_transpose(KD // 2 - 1, 0)
                out_transpose(KD // 2 - 1, 1)
            for t, rows in tiles(1):
                h2_transpose(1, t, rows)
                logits(1, t, rows)
            moe_tensor(pe)


_INS = ["x_prompt", "x_sample", "c_prompt", "c_sample", "state_conv_a", "state_conv_c", "norm1_g", "norm2_g",
        "w_ada", "b_ada", "w_in", "a_dw_w", "a_dw_b", "a_norm_g", "a_norm_b", "b_norm_g", "b_norm_b",
        "b_spatial_w", "b_spatial_b", "c_conv_w", "w_branch", "w_out", "w_router_g", "b_router_g",
        "w_router_e", "b_router_e", "w1", "w3", "w2", "final_norm_g"]
_OUTS = [(1, SEQ, D), (NS, TS, D), (1, 1, HA, W), (1, 1, HC, W), (1, NS, HA, W), (1, NS, HC, W), (1, NS, TS, W)]


def kernel(**inputs):
    import concourse.bacc as _bacc
    from concourse.bass_utils import run_bass_kernel_spmd as _run

    nc = _bacc.Bacc("TRN2", target_bir_lowering=False, num_devices=1)
    arrays, args = {}, []
    for name in _INS:
        a = np.ascontiguousarray(inputs[name])
        arrays[f"in_{name}_dram"] = a
        args.append(nc.dram_tensor(f"in_{name}_dram", a.shape, mybir.dt.from_np(a.dtype), kind="ExternalInput").ap())
    for i, shape in enumerate(_OUTS):
        args.append(nc.dram_tensor(f"out_{i}_dram", shape, F32, kind="ExternalOutput").ap())
    build(nc, *args)
    r = _run(nc, [arrays], core_ids=[0])
    return tuple(r.results[0][f"out_{i}_dram"] for i in range(len(_OUTS)))
```

```python
import numpy as np

import concourse.bass as bass
from concourse import mybir
from contextlib import ExitStack

F32 = mybir.dt.float32
F32R = mybir.dt.float32r
BF16 = mybir.dt.bfloat16
I32 = mybir.dt.int32
U32 = mybir.dt.uint32
ALU = mybir.AluOpType
ACT = mybir.ActivationFunctionType
AX = mybir.AxisListType

P = 128
D = 1024
KD = D // P
W = D // 2
CW = W // P
SEQ, NS, TS = 1024, 8, 4
SMP = NS * TS
HALF = SEQ // 2
PT = HALF // P
TOK = SEQ + SMP
NT = 2 * PT + 1
KA, KC = 31, 3
HA, HC = KA - 1, KC - 1
HEADS = 8
NE, NG, EG, FF = 32, 4, 8, 512
NR = NG + NE
KF = FF // P
EPS = 1e-6
NB_A, NB_C, NB_B = 0, 2, 1
GELU0 = 1.5957691216057308
GELU1 = GELU0 * 0.044715
MAGIC = 0x5F375A86
BIG = 3.0e38
TPAD = 2048
NBLK = 9
OOB = 4 * TPAD - 1
MAXX = 16

A0, C0, B0 = 0, 2 * CW, 5 * CW
GC0 = B0 + 2 * CW
GB0 = GC0 + 2 * KD
GA0 = GB0 + 2 * KD
O0 = GA0 + 2 * KD
NI = O0 + KD
NSPLIT = O0
AS, CS = HA + TS, HC + TS
NPAR = KA + KC + 3 + NS * HC
PAR_B, PAR_G, PAR_S, PAR_H = KA + KC, KA + KC + 1, KA + KC + 2, KA + KC + 3
N_PAR = 25
N_RT = 14
N_CONST = 17
COL = dict(a_val=0, a_gt=W, b_u=2 * W, b_v=3 * W, c_b=4 * W, c_c=5 * W, c_h=6 * W, gates=7 * W)


def build(nc, x_prompt, x_sample, c_prompt, c_sample, state_conv_a, state_conv_c, norm1_g, norm2_g,
          w_ada, b_ada, w_in, a_dw_w, a_dw_b, a_norm_g, a_norm_b, b_norm_g, b_norm_b, b_spatial_w,
          b_spatial_b, c_conv_w, w_branch, w_out, w_router_g, b_router_g, w_router_e, b_router_e,
          w1, w3, w2, final_norm_g, y_prompt, y_sample, new_a_prompt, new_c_prompt, new_a_sample,
          new_c_sample, new_v_sample):
    ctx = ExitStack()
    with ctx:
        def sem(name):
            return ctx.enter_context(nc.semaphore(name))

        mod_dram = nc.dram_tensor("mod_rows", (9, 6 * D), F32, kind="Internal").ap()
        h2_dram = nc.dram_tensor("h2_rows", (TOK, D), F32, kind="Internal").ap()
        x1_dram = nc.dram_tensor("x1_rows", (TOK, D), F32, kind="Internal").ap()
        y_dram = nc.dram_tensor("y_rows", (2 * TPAD, D), F32, kind="Internal").ap()
        table = nc.dram_tensor("slot_table", (NBLK * P * NE, 1), I32, kind="Internal").ap()
        table_rows = table.rearrange("(r e) o -> r (e o)", e=NE)

        base = (nc.sbuf_base + 31) // 32 * 32
        top = [base]
        size_of = {F32: 4, F32R: 4, BF16: 2, I32: 4, U32: 4}

        def at(name, shape, dt, offset):
            n = int(np.prod(shape[1:])) * size_of[dt]
            return nc.alloc_sbuf_tensor_at(name, shape, dt, offset=offset), offset + (n + 31) // 32 * 32

        def sb(name, shape, dt=F32):
            t, top[0] = at(name, shape, dt, top[0])
            return t

        TG = [HALF, HALF + SMP]
        TM = TG[1]
        ident = sb("ident", [P, P])
        logit = sb("logit", [P, NT, NR])
        tri = sb("tri", [P, P], BF16)
        oneb = sb("oneb", [P, P], BF16)
        io32 = sb("io32", [P, NE])
        vali = sb("vali", [P, 2, NT], I32)
        valf = sb("valf", [P, 2, NT])
        io128 = sb("io128", [P, P])
        tinit = sb("tinit", [P, NBLK * NE], I32)
        thr = sb("thr", [NE, NBLK - 1])
        bval = sb("bval", [NE, NBLK - 1])
        io16 = sb("io16", [NE, MAXX])
        trif = sb("trif", [NE, NE])
        onef = sb("onef", [NE, P])
        h_at = top[0]
        h_hi = sb("h_hi", [P, KD, TM], F32R)
        h_lo = sb("h_lo", [P, KD, TM], F32R)
        act0_at = top[0]
        act0_hi = sb("act0_hi", [P, CW, TM], F32R)
        act0_lo = sb("act0_lo", [P, CW, TM], F32R)
        macc = sb("macc", [P, KD, TM])
        act1_at = top[0]
        act1_hi = sb("act1_hi", [P, CW, TM], F32R)
        act1_lo = sb("act1_lo", [P, CW, TM], F32R)
        act1_end = top[0]
        ures_at = top[0]
        u_sb = sb("u_sb", [P, CW, TM])
        v_tok = sb("v_tok", [P, PT + 1, W])
        xres, xres_end = at("xres", [P, PT + 1, D], F32, ures_at)
        top[0] = max(top[0], xres_end)
        w_raw = [sb(f"w_raw{s}", [P, KD, P]) for s in range(2)]
        w_hi = [sb(f"w_hi{s}", [P, KD, P], F32R) for s in range(2)]
        w_lo = [sb(f"w_lo{s}", [P, KD, P], F32R) for s in range(2)]
        a_in = sb("a_in", [P, CW, HA + HALF + NS * AS])
        conv = sb("conv", [P, CW, TM])
        xs = sb("xs", [P, 2, D])
        sig = sb("sig", [P, TM])
        chb = sb("chb", [P, TM])
        vT = sb("vT", [P, TM])
        g_at = top[0]
        gq = sb("gq", [P, TM])
        gt = sb("gt", [P, TM])
        ot = [sb(f"ot{s}", [P, TM]) for s in range(2)]
        p_in = sb("p_in", [P, HC + HALF + NS * CS])
        cv = sb("cv", [P, TM])
        a_tail = sb("a_tail", [P, CW, HA + SMP])
        p_tail = sb("p_tail", [P, CW, HC + SMP])
        p_hist = sb("p_hist", [P, CW, NS * HC])
        tap_s = sb("tap_s", [P, 2, 2, SMP])
        wsT = sb("wsT", [P, HEADS, P])
        wsS = sb("wsS", [SMP, HEADS, SMP])
        s_bias = sb("s_bias", [P, CW, P])
        bn_g = sb("bn_g", [P, W])
        bn_b = sb("bn_b", [P, W])
        parT = sb("parT", [P, CW, NPAR])
        n1T = sb("n1T", [P, KD])
        modT = sb("modT", [P, 3 * KD, 9])
        blk64 = sb("blk64", [P, P])
        blk2 = sb("blk2", [P, 2])
        rs_v = sb("rs_v", [P, CW, PT + 1, 2])
        rs_y = sb("rs_y", [P, CW, PT + 1, 2])
        rs_t = sb("rs_t", [P, CW, PT + 1, 2])
        bn6 = sb("bn6", [P, PT + 1, 6])
        mv = sb("mv", [P, PT + 1, 2])
        ssq = sb("ssq", [P, NT])
        ssq2 = sb("ssq2", [P, NT])
        nv = sb("nv", [P, NT])
        ny = sb("ny", [P, NT])
        nt_ = sb("nt_", [P, NT])
        r2y = sb("r2y", [P, NT])
        rw = sb("rw", [P, KD, NR])
        rb = sb("rb", [P, NR])
        n2_b = sb("n2_b", [P, D])
        assert top[0] <= nc.sbuf_usable_end, top[0] - nc.sbuf_usable_end
        h2s = [None, None]
        h2s[0], o = at("h2s0", [P, D], F32, act1_at)
        h2T, o = at("h2T", [P, KD, P], F32, o)
        A2, o = at("A2", [P, D], F32, o)
        B2, o = at("B2", [P, D], F32, o)
        assert o <= act1_end, o - act1_end
        junk, o = at("junk", [P, D], F32, act0_at)
        h2s[1], _ = at("h2s1", [P, D], F32, o)
        ada, o = at("ada", [P, 2, KD, 512], F32, act0_at)
        assert o <= act1_at
        crow, o = at("crow", [9, D], F32, act1_at)
        sicT, o = at("sicT", [P, KD, 9], F32, o)
        badar, o = at("badar", [9, 2, 512], F32, o)
        modr, o = at("modr", [9, 2, 512], F32, o)
        assert o <= act1_end
        csig, o = at("csig", [9, D], F32, ures_at)
        parr, o = at("parr", [NPAR, W], F32, o)
        n1r, o = at("n1r", [KD, P], F32, o)
        hist, o = at("hist", [HA * TS, 2, W], F32, o)
        wsr, o = at("wsr", [P, HEADS, P], F32, o)
        assert o <= xres_end

        w13, w2s, xg, xT, ysb = [None] * 2, [None] * 2, [None] * 2, [None] * 2, [None] * 2
        o = h_at
        w13[0], o = at("w13_0", [P, 2, KD, FF], F32, o)
        w2s[0], o = at("w2_0", [P, KF, D], F32, o)
        slot1_at = o
        w13[1], o = at("w13_1", [P, 2, KD, FF], F32, o)
        w2s[1], o = at("w2_1", [P, KF, D], F32, o)
        slot1_end = o
        xg[0], o = at("xg0", [P, D], F32, o)
        xg[1], o = at("xg1", [P, D], F32, o)
        xT[0], o = at("xT0", [P, KD, P], F32, o)
        xT[1], o = at("xT1", [P, KD, P], F32, o)
        hsg, o = at("hsg", [P, FF], F32, o)
        gs, o = at("gs", [P, FF], F32, o)
        gT, o = at("gT", [P, KF, P], F32, o)
        ohr_at = o
        ysb[0], o = at("ysb0", [P, D], F32, o)
        ysb[1], o = at("ysb1", [P, D], F32, o)
        x1a, o = at("x1a", [P, NT, D], F32, o)
        g2b, o = at("g2b", [P, 2, D], F32, o)
        fgb, o = at("fgb", [P, D], F32, o)
        top[0] = o
        YS = 5
        yin, yin_end = at("yin", [P, YS, 2, D], F32, h_at)
        yacc, yacc_end = at("yacc", [P, NT, D], F32, slot1_at)
        assert yin_end <= slot1_at and yacc_end <= slot1_end
        ohr, _ = at("ohr", [P, 2, NT, P], F32, ohr_at)
        gpad = sb("gpad", [P, NT, 8])
        m8g = sb("m8g", [P, NT, 8])
        i8g = sb("i8g", [P, NT, 8], U32)
        m8 = sb("m8", [P, NT, 8])
        i8 = sb("i8", [P, NT, 8], U32)
        gif = sb("gif", [P, NT])
        ohg = sb("ohg", [P, NT, NG])
        em = sb("em", [P, NT, NE])
        ef = sb("ef", [P, NT, 2])
        oh = sb("oh", [P, 2, NT, NE])
        ohs = sb("ohs", [P, NT, NE], BF16)
        rk = sb("rk", [P, 2, NT])
        dsti = sb("dsti", [P, 2, NT], I32)
        wk = sb("wk", [P, 2, NT])
        gd = sb("gd", [P, NT, NG])
        gsum = sb("gsum", [P, NT])
        tb0 = sb("tb0", [P, NE], I32)
        tok0 = sb("tok0", [P, NE], I32)
        gcol = [sb(f"gcol{s}", [P, 1], I32) for s in range(2)]
        scol = [sb(f"scol{s}", [P, 1], I32) for s in range(2)]
        xcol = sb("xcol", [P, 1], I32)
        xtok = sb("xtok", [P, 1], I32)
        cnt = sb("cnt", [NE, 1])
        need = sb("need", [NE, NBLK - 1])
        posn = sb("posn", [NE, NBLK - 1])
        rowc = sb("rowc", [NE, 1])
        xeq = sb("xeq", [NE, MAXX, NBLK - 1])
        xls = sb("xls", [NE, MAXX + 1])
        xrow = sb("xrow", [1, 3, MAXX + 1], I32)
        ohv = sb("ohv", [P, 2, NT, NE])
        fss = sb("fss", [P, NT])
        fv = sb("fv", [P, NT])
        fy = sb("fy", [P, NT])
        ft = sb("ft", [P, NT])
        assert top[0] <= nc.sbuf_usable_end, top[0] - nc.sbuf_usable_end

        z = [ctx.enter_context(nc.psum_tensor(f"z{s}", [P, 2, 512], F32)) for s in range(2)]
        q = [ctx.enter_context(nc.psum_tensor(f"q{s}", [P, 2, 512], F32)) for s in range(2)]

        par_in, c_in = sem("par_in"), sem("c_in")
        ada_in = [sem(f"ada_in{s}") for s in range(2)]
        bada_in = [sem(f"bada_in{s}") for s in range(2)]
        x_in = [sem(f"x_in{s}") for s in range(4)]
        w_in_sem = [sem(f"w_in{s}") for s in range(2)]
        consts = sem("consts")
        csig_ok, sic_ok = sem("csig_ok"), sem("sic_ok")
        modr_ok = sem("modr_ok")
        modt_ok = sem("modt_ok")
        mod_out = [sem(f"mod_out{s}") for s in range(2)]
        aux_ok = sem("aux_ok")
        bd_in = sem("bd_in")
        q_ready = [sem(f"q_ready{s}") for s in range(2)]
        q_free = [sem(f"q_free{s}") for s in range(2)]
        z_free = [sem(f"z_free{s}") for s in range(2)]
        whi_ok, wlo_ok = sem("whi_ok"), sem("wlo_ok")
        item_mm = sem("item_mm")
        x_sq, x_n = sem("x_sq"), sem("x_n")
        hhi_ok, hlo_ok = sem("hhi_ok"), sem("hlo_ok")
        chi_ok, clo_ok = sem("chi_ok"), sem("clo_ok")
        gt_ok, gs_ok, gq_ok = sem("gt_ok"), sem("gs_ok"), sem("gq_ok")
        vT_ok, vn_ok, v_out = sem("vT_ok"), sem("vn_ok"), sem("v_out")
        bb_ok, bhi_ok, blo_ok = sem("bb_ok"), sem("bhi_ok"), sem("blo_ok")
        cnv_ok, cnvp_ok = sem("cnv_ok"), sem("cnvp_ok")
        asq_ok, rs_ok, ay_ok, af_ok, ahi_ok, alo_ok = (
            sem(n) for n in ("asq_ok", "rs_ok", "ay_ok", "af_ok", "ahi_ok", "alo_ok"))
        macc_ok = sem("macc_ok")
        ot_ok = sem("ot_ok")
        xres_in = sem("xres_in")
        x1_sq = sem("x1_sq")
        h2_last = [sem(f"h2_last{s}") for s in range(2)]
        ab_in, abs_in = sem("ab_in"), sem("abs_in")
        h2_ok, h2_out, x1_out = sem("h2_ok"), sem("h2_out"), sem("x1_out")
        st_out = sem("st_out")

        block = ctx.enter_context(nc.Block())

        H2 = TM // 2

        def zv(s, g):
            return z[s][:, 0, 0:HALF] if g == 0 else z[s][:, :, 0:H2]

        def tv(ap, g):
            return ap[:, 0:HALF] if g == 0 else ap[:, 0:TM].rearrange("p (b t) -> p b t", b=2)

        def chunk(t, i):
            return t[:, i, :] if isinstance(i, int) else \
                t[:, bass.ds(i, 1), :].rearrange("p o t -> p (o t)")

        def zparts(s, g):
            return [(z[s][:, 0, 0:HALF], 0, HALF)] if g == 0 else \
                [(z[s][:, 0, 0:H2], 0, H2), (z[s][:, 1, 0:HALF - H2], H2, HALF)]

        def zsample(s):
            return z[s][:, 1, HALF - H2:H2]

        def halves(g):
            return [(0, 0, HALF)] if g == 0 else [(0, 0, H2), (1, H2, TM)]

        def seqs(ap):
            return ap.rearrange("p (n t) -> p n t", n=NS)

        def item_no(g, u, s):
            return NI * g + 2 * u + s

        def split_no(g, u, s):
            return NSPLIT * g + 2 * u + s

        def slot_use(g, u):
            return NI // 2 * g + u

        def first(u):
            return u if isinstance(u, int) else u.min_val

        QFILL, QUSE, qn, qf = {}, {}, [0, 0], [0, 0]

        def use(s, *name):
            QFILL[name], QUSE[name] = (s, qn[s]), (s, qf[s])
            qn[s] += 1
            qf[s] += name[0] != "ada"

        use(0, "sic")

        def use_ada(js):
            for j in js:
                use(0, "ada", j)
                if j < 6:
                    use(1, "modT", j)

        use_ada(range(4))
        use(0, "par"), use(1, "n1"), use(0, "hist"), use(1, "ws")
        for t in range(PT):
            use(t % 2, "xT", 0, t)
        for g in range(2):
            if g:
                for i in range(PT):
                    use(0, "h2T", 0, i), use(1, "lg", 0, i)
            else:
                use_ada(range(4, 12))
            for i in range(CW):
                use(0, "vT", g, i)
            for t in range(PT + g):
                use(t % 2, "sp", g, t)
            if g:
                use(0, "stA"), use(1, "stC")
            for c in range(CW):
                use(c % 2, "mu", g, c)
            use(1, "var", g)
            for c in range(CW):
                use(c % 2, "bc", g, c)
            if g == 0:
                for t in range(PT):
                    use(t % 2, "xT", 1, t)
            use(0, "oT", g, 0), use(1, "oT", g, 1)
            if g == 0:
                use(0, "xT", 1, PT)
            for n in range(2, KD):
                use(n % 2, "oT", g, n)
        for i in range(PT + 1):
            use(0, "h2T", 1, i), use(1, "lg", 1, i)
        use(0, "rank"), use(1, "cnt"), use(0, "tb"), use(1, "pos"), use(1, "list")

        def q_wait_free(pe, *name, more=0):
            s, n = QUSE[name]
            if n:
                pe.wait_ge(q_free[s], n + more)
            return s

        def q_wait_ready(eng, *name, more=0):
            s, n = QFILL[name]
            eng.wait_ge(q_ready[s], n + 1 + more)
            return s

        def q_wait_read(eng, *name, more=0):
            s, n = QUSE[name]
            eng.wait_ge(q_free[s], n + 1 + more)

        def before_wait(eng, n):
            n = n if isinstance(n, int) else eng.to_reg(n)
            eng.wait_ge(c_in, 32)
            return n

        def tiles(g):
            return [(t, P) for t in range(PT)] + ([(PT, SMP)] if g else [])

        def x_rows(g, t):
            return x_sample.rearrange("n t d -> (n t) d") if t == PT else \
                x_prompt[0, (g * PT + t) * P:(g * PT + t + 1) * P, :]

        XT = [(g, t, rows) for g in range(2) for t, rows in tiles(g)]
        XN = {(g, t): n for n, (g, t, _) in enumerate(XT)}
        conv_flat = conv[:, :, :].rearrange("p c t -> p (c t)")

        def x_slot(g, t):
            return t if g == 0 else t % 2

        def x_stage(g, t):
            s = x_slot(g, t)
            return xs[:, s, :] if s < 2 else conv_flat[:, (s - 2) * D:(s - 1) * D]

        def h_wide(g, t):
            return x_stage(g, t).rearrange("p (k t) -> p k t", t=P)

        def x_dump(g):
            return conv_flat[:, 0:D] if g else h_lo[:, :, :].rearrange("p k t -> p (k t)")[:, 0:D]

        XUSE = {(g, t): sum(1 for gg, tt, _ in XT[:n] if x_slot(gg, tt) == x_slot(g, t)) for n, (g, t, _) in enumerate(XT)}
        xs_s = conv_flat[0:SMP, :]


        rt_const, tab_out = sem("rt_const"), sem("tab_out")
        rt_m = sem("rt_m")
        rt_e = sem("rt_e")
        oh_ok, wk_ok = sem("oh_ok"), sem("wk_ok")
        dst_ok, tab_sc = sem("dst_ok"), sem("tab_sc")
        ohr_ok, tok_ok = sem("ohr_ok"), sem("tok_ok")
        row_ok, xls_ok, xrow_ok = sem("row_ok"), sem("xls_ok"), sem("xrow_ok")
        xg0_ok, gcol_ok, scol_ok = sem("xg0_ok"), sem("gcol_ok"), sem("scol_ok")
        m_w13, m_w2, m_xg, m_sc = ([sem(f"{n}{s}") for s in range(2)] for n in ("m_w13", "m_w2", "m_xg", "m_sc"))
        m_T, m_xT, m_H, m_sg, m_g, m_G, m_gT, m_Y, m_y = (
            sem(n) for n in ("m_T", "m_xT", "m_H", "m_sg", "m_g", "m_G", "m_gT", "m_Y", "m_y"))
        o_i, o_w, o_c, o_x, o_sc = (sem(n) for n in ("o_i", "o_w", "o_c", "o_x", "o_sc"))
        f_in = [sem(f"f_in{s}") for s in range(YS)]
        f_par, f_a, f_c, f_g, f_sum, f_sq, f_y, f_out = (
            sem(n) for n in ("f_par", "f_a", "f_c", "f_g", "f_sum", "f_sq", "f_y", "f_out"))
        pairs_of = [range(0, 2), range(2, 4), range(4, 6), range(6, 8), range(8, 9)]
        assert NT == 9
        f_rows = [P] * (NT - 1) + [SMP]

        def dense_done(eng):
            eng.wait_ge(item_mm, 2 * NI)
            eng.wait_ge(h2_last[0], 16 * ((PT + 2) // 2))
            eng.wait_ge(h2_last[1], 16 * ((PT + 1) // 2))
            eng.wait_ge(x1_out, 16 * NT)
            eng.wait_ge(x1_sq, NT)
            q_wait_read(eng, "lg", 1, PT)

        def expert_rows(w, e):
            return w[0, bass.ds(e, 1)].rearrange("o (p k) f -> p (o k) f", p=P)

        def moe_sync(sp):
            def load13(e, s):
                for j, w in enumerate((w1, w3)):
                    sp.dma_start(w13[s][:, j], expert_rows(w, e)).then_inc(m_w13[s], 16)

            def load2(e, s):
                sp.dma_start(w2s[s][:], expert_rows(w2, e)).then_inc(m_w2[s], 16)

            sp.wait_ge(item_mm, item_no(1, O0 // 2, 0))
            load13(0, 0)
            dense_done(sp)
            load2(0, 0)
            load13(1, 1)
            load2(1, 1)
            with sp.Fori(0, NE // 2 - 1) as r:
                for s in range(2):
                    sp.wait_ge(m_H, r * 2 + (s + 1))
                    load13(r * 2 + (s + 2), s)
                    sp.wait_ge(m_Y, r * 2 + (s + 1))
                    load2(r * 2 + (s + 2), s)
            sp.wait_ge(xrow_ok, 1)
            sp.wait_ge(tab_sc, 16 * 2 * NT)
            sp.wait_ge(m_H, NE - 1)
            sp.wait_ge(m_Y, NE - 1)
            n = sp.value_load(xrow[0:1, 0, MAXX:MAXX + 1], min_val=0, max_val=MAXX)
            with sp.If(n > 0):
                with sp.Fori(0, n) as i:
                    e = sp.value_load(xrow[0:1, 1, bass.ds(i, 1)], min_val=0, max_val=NE - 1)
                    b = sp.value_load(xrow[0:1, 2, bass.ds(i, 1)], min_val=1, max_val=NBLK - 1)
                    sp.dma_start(xcol[:], table[bass.ds(b * (P * NE), P * NE), :].rearrange(
                        "(r e) o -> r e o", e=NE)[:, bass.ds(e, 1), :].rearrange("r e o -> r (e o)"),
                        allow_slow_non_contiguous=True).then_inc(o_i, 16)
                    for j, w in enumerate((w1, w3)):
                        sp.dma_start(w13[0][:, j], expert_rows(w, e)).then_inc(o_w, 16)
                    sp.dma_start(w2s[0][:], expert_rows(w2, e)).then_inc(o_w, 16)
                    n_ = before_wait(sp, i * 16 + 16)
                    sp.wait_ge(o_sc, n_)
            for s in range(2):
                sp.wait_ge(m_sc[s], 16 * (NE // 2))
            sp.wait_ge(m_Y, NE)
            for t in range(NT):
                if t >= YS:
                    sp.wait_ge(f_c, t - YS + 1)
                for k in range(2):
                    r0 = t * P + k * TPAD
                    sp.dma_start(yin[0:f_rows[t], t % YS, k, :], y_dram[r0:r0 + f_rows[t], :]).then_inc(f_in[t % YS], 16)

        def moe_gpsimd(pool):
            dense_done(pool)
            pool.memset(xg[0][:], 0.0).then_inc(xg0_ok, 1)
            pool.drain()
            pool.memset(xg[1][:], 0.0).then_inc(xg0_ok, 1)
            def fill_table():
                pool.wait_ge(dst_ok, 1)
                pool.wait_ge(tab_out, 16)
                for t in range(NT):
                    rows = P if t < NT - 1 else SMP
                    for k in range(2):
                        pool.indirect_dma_start(table, bass.IndirectOffsetOnAxis(ap=dsti[0:rows, k, t:t + 1], axis=0),
                                                vali[0:rows, k, t:t + 1], None, bounds_check=NBLK * P * NE - 1,
                                                oob_is_err=False).then_inc(tab_sc, 16)

            pool.wait_ge(tok_ok, 1)

            def gather_dma(s, col, done):
                pool.indirect_dma_start(xg[s][:], None, h2_dram, bass.IndirectOffsetOnAxis(ap=col[:, 0:1], axis=0),
                                        bounds_check=TOK - 1, oob_is_err=False).then_inc(done, 16)

            def scatter_dma(s, col, done):
                pool.indirect_dma_start(y_dram, bass.IndirectOffsetOnAxis(ap=col[:, 0:1], axis=0), ysb[s][:], None,
                                        bounds_check=2 * TPAD - 1, oob_is_err=False).then_inc(done, 16)

            def gather(e, s):
                if first(e) >= 2:
                    pool.wait_ge(m_T, e - 1)
                pool.tensor_copy(gcol[s][:], tok0[:, bass.ds(e, 1)]).then_inc(gcol_ok, 1)
                n_ = before_wait(pool, e + 1)
                pool.wait_ge(gcol_ok, n_)
                gather_dma(s, gcol[s], m_xg[s])

            def scatter(e, s, r):
                if first(r):
                    pool.wait_ge(m_sc[s], r * 16)
                pool.tensor_copy(scol[s][:], tb0[:, bass.ds(e, 1)]).then_inc(scol_ok, 1)
                n_ = before_wait(pool, e + 1)
                pool.wait_ge(scol_ok, n_)
                pool.wait_ge(m_y, e + 1)
                scatter_dma(s, scol[s], m_sc[s])

            pool.wait_ge(xg0_ok, 2)
            gather(0, 0)
            gather(1, 1)
            fill_table()
            gather(2, 0)
            gather(3, 1)
            scatter(0, 0, 0)
            gather(4, 0)
            scatter(1, 1, 0)
            with pool.Fori(1, NE // 2 - 2) as r:
                gather(r * 2 + 3, 1)
                scatter(r * 2, 0, r)
                gather(r * 2 + 4, 0)
                scatter(r * 2 + 1, 1, r)
            gather(NE - 1, 1)
            for s in range(2):
                scatter(NE - 4 + s, s, NE // 2 - 2)
            for s in range(2):
                scatter(NE - 2 + s, s, NE // 2 - 1)
            pool.wait_ge(xrow_ok, 1)
            n = pool.value_load(xrow[0:1, 0, MAXX:MAXX + 1], min_val=0, max_val=MAXX)
            with pool.If(n > 0):
                with pool.Fori(0, n) as i:
                    n_ = before_wait(pool, i + 1)
                    pool.wait_ge(o_c, n_)
                    gather_dma(0, xtok, o_x)
                    n_ = before_wait(pool, i + (NE + 1))
                    pool.wait_ge(m_y, n_)
                    scatter_dma(0, xcol, o_sc)

            pool.wait_ge(f_par, 16 * (4 + NS))
            for p in range(len(pairs_of) + 2):
                for t in pairs_of[p] if p < len(pairs_of) else ():
                    acc = yacc[0:f_rows[t], t, :]
                    pool.wait_ge(f_c, t + 1)
                    pool.tensor_tensor(acc, acc, g2b[0:f_rows[t], t // (NT - 1), :], ALU.mult).then_inc(f_g, 1)
                    pool.drain()
                for t in pairs_of[p - 2] if p >= 2 else ():
                    dst = y_prompt[0, t * P:(t + 1) * P, :] if t < NT - 1 else y_sample.rearrange("n t d -> (n t) d")
                    pool.wait_ge(f_y, t + 1)
                    pool.dma_start(dst, yacc[0:f_rows[t], t, :]).then_inc(f_out, 16)
            pool.wait_ge(f_out, 16 * NT)
            pool.wait_ge(st_out, 16 * (3 + 2 * NS))

        def step_T(pe, e, s):
            if first(e):
                pe.wait_ge(m_xT, e)
            for k in range(KD):
                last = pe.transpose(q[0][:, k // 4, (k % 4) * P:(k % 4 + 1) * P],
                                    xg[s][:, :].rearrange("p (c k) -> p k c", k=KD)[:, k, :], ident[:])
            last.then_inc(m_T, 1)

        def step_H(pe, e, s):
            pe.wait_ge(m_xT, e + 1)
            if first(e):
                pe.wait_ge(m_g, e)
            for k in range(KD):
                for j in range(2):
                    last = pe.matmul(z[0][:, j, :], xT[s][:, k, :], w13[s][:, j, k, :], start=(k == 0), stop=(k == KD - 1))
            last.then_inc(m_H, 1)

        def step_G(pe, e):
            pe.wait_ge(m_g, e + 1)
            if first(e):
                pe.wait_ge(m_gT, e)
            for k in range(KF):
                last = pe.transpose(q[1][:, 0, k * P:(k + 1) * P], gs[:, :].rearrange("p (c k) -> p k c", k=KF)[:, k, :], ident[:])
            last.then_inc(m_G, 1)

        def step_Y(pe, e, s):
            pe.wait_ge(m_gT, e + 1)
            if first(e):
                pe.wait_ge(m_y, e)
            for k in range(KF):
                for j in range(2):
                    last = pe.matmul(z[1][:, j, :], gT[:, k, :], w2s[s][:, k, j * 512:(j + 1) * 512],
                                     start=(k == 0), stop=(k == KF - 1))
            last.then_inc(m_Y, 1)

        def moe_tensor(pe):
            s = q_wait_free(pe, "rank")
            pe.wait_ge(oh_ok, 1)
            pe.wait_ge(rt_const, N_RT)
            for t in range(NT):
                out = q[s][:, 0, t * NE:(t + 1) * NE]
                for j in range(t):
                    pe.matmul(out, oneb[:], ohs[:, j, :], start=(j == 0), stop=False)
                last = pe.matmul(out, tri[:], ohs[:, t, :], start=(t == 0), stop=True)
            last.then_inc(q_ready[s], 1)
            s = q_wait_free(pe, "cnt")
            for t in range(NT):
                last = pe.matmul(q[s][0:NE, 0, 0:1], ohs[:, t, :], oneb[:, 0:1], start=(t == 0), stop=(t == NT - 1))
            last.then_inc(q_ready[s], 1)
            s = q_wait_free(pe, "tb")
            pe.wait_ge(ohr_ok, 1)
            for t in range(NT):
                rows = P if t < NT - 1 else SMP
                for k in range(2):
                    last = pe.matmul(q[s][:, 0, 0:NE], ohr[0:rows, k, t, :], ohv[0:rows, k, t, :],
                                     start=(t + k == 0), stop=(t == NT - 1 and k == 1))
            last.then_inc(q_ready[s], 1)
            s = q_wait_free(pe, "pos")
            pe.wait_ge(row_ok, 1)
            pe.matmul(q[s][0:NE, 0, 0:1], trif[:], rowc[:], start=True, stop=True).then_inc(q_ready[s], 1)
            s = q_wait_free(pe, "list")
            pe.wait_ge(xls_ok, 1)
            pe.matmul(q[s][0:1, 0, 0:MAXX + 1], onef[:, 0:1], xls[:], start=True, stop=True).then_inc(q_ready[s], 1)
            q_wait_read(pe, "tb")
            q_wait_read(pe, "list")
            for s in range(2):
                pe.wait_ge(z_free[s], NI)

            def T(r, s):
                pe.wait_ge(m_xg[s], r * 16 + 16)
                step_T(pe, r * 2 + s, s)

            def H(r, s):
                pe.wait_ge(m_w13[s], r * 32 + 32)
                step_H(pe, r * 2 + s, s)

            def Y(r, s):
                pe.wait_ge(m_w2[s], r * 16 + 16)
                step_Y(pe, r * 2 + s, s)

            T(0, 0)
            H(0, 0)
            T(0, 1)
            step_G(pe, 0)
            H(0, 1)
            T(1, 0)
            Y(0, 0)
            step_G(pe, 1)
            with pe.Fori(1, NE // 2) as r:
                H(r, 0)
                T(r, 1)
                Y(r - 1, 1)
                step_G(pe, r * 2)
                H(r, 1)
                with pe.If(r < NE // 2 - 1):
                    T(r + 1, 0)
                Y(r, 0)
                step_G(pe, r * 2 + 1)
            Y(NE // 2 - 1, 1)
            pe.wait_ge(xrow_ok, 1)
            n = pe.value_load(xrow[0:1, 0, MAXX:MAXX + 1], min_val=0, max_val=MAXX)
            with pe.If(n > 0):
                with pe.Fori(0, n) as i:
                    pe.wait_ge(o_x, i * 16 + 16)
                    step_T(pe, i + NE, 0)
                    pe.wait_ge(o_w, i * 48 + 48)
                    step_H(pe, i + NE, 0)
                    step_G(pe, i + NE)
                    step_Y(pe, i + NE, 0)

        def moe_scalar(act):
            act.wait_ge(rt_m, 1)
            act.activation(wk[:, 0, :], gif[:], ACT.Sigmoid)
            act.activation(wk[:, 1, :], gif[:], ACT.Sigmoid, scale=-1.0)
            act.activation(gd[:], gd[:], ACT.Exp).then_inc(rt_e, 1)

            def rows_T(e, s):
                act.wait_ge(m_T, e + 1)
                act.activation(xT[s][:], q[0][:, :, :].rearrange("p b (k t) -> p (b k) t", t=P), ACT.Copy).then_inc(m_xT, 1)

            def sigm(e):
                act.wait_ge(m_H, e + 1)
                if first(e):
                    act.wait_ge(m_g, e)
                act.activation(hsg[:], z[0][:, 0, :], ACT.Sigmoid).then_inc(m_sg, 1)

            def hidden_T(e):
                act.wait_ge(m_G, e + 1)
                if first(e):
                    act.wait_ge(m_Y, e)
                act.activation(gT[:], q[1][:, 0, :].rearrange("p (k t) -> p k t", t=P), ACT.Copy).then_inc(m_gT, 1)

            rows_T(0, 0)
            dense_done(act)
            act.dma_start(fgb[:], final_norm_g.rearrange("(o d) -> o d", o=1).to_broadcast([P, D])).then_inc(f_par, 16)
            act.dma_start(g2b[:, 0, :], mod_dram[0:1, 5 * D:6 * D].to_broadcast([P, D])).then_inc(f_par, 16)
            for n_ in range(NS):
                act.dma_start(g2b[n_ * TS:(n_ + 1) * TS, 1, :],
                              mod_dram[1 + n_:2 + n_, 5 * D:6 * D].to_broadcast([TS, D])).then_inc(f_par, 16)
            act.wait_ge(m_xT, 1)
            act.dma_start(x1a[:, 0:NT - 1, :], x1_dram[0:SEQ, :].rearrange("(t p) d -> p t d", p=P)).then_inc(f_par, 16)
            act.dma_start(x1a[0:SMP, NT - 1, :], x1_dram[SEQ:TOK, :]).then_inc(f_par, 16)
            sigm(0)
            rows_T(1, 1)
            hidden_T(0)
            sigm(1)
            rows_T(2, 0)
            hidden_T(1)
            with act.Fori(1, NE // 2 - 1) as r:
                for s in range(2):
                    sigm(r * 2 + s)
                    rows_T(r * 2 + (s + 1), 1 - s)
                    hidden_T(r * 2 + s)
            sigm(NE - 2)
            rows_T(NE - 1, 1)
            hidden_T(NE - 2)
            sigm(NE - 1)
            hidden_T(NE - 1)
            act.wait_ge(xrow_ok, 1)
            n = act.value_load(xrow[0:1, 0, MAXX:MAXX + 1], min_val=0, max_val=MAXX)
            with act.If(n > 0):
                with act.Fori(0, n) as i:
                    rows_T(i + NE, 0)
                    sigm(i + NE)
                    hidden_T(i + NE)
            for p in range(len(pairs_of) + 1):
                for t in pairs_of[p] if p < len(pairs_of) else ():
                    act.wait_ge(f_in[t % YS], 32 * (t // YS + 1))
                    rows = f_rows[t]
                    act.activation(yacc[0:rows, t, :], yin[0:rows, t % YS, 0, :], ACT.Copy,
                                   scale=wk[0:rows, 0, t:t + 1]).then_inc(f_a, 1)
                for t in pairs_of[p - 1] if p else ():
                    act.wait_ge(f_sum, t + 1)
                    if t >= 2:
                        act.wait_ge(f_sq, t - 1)
                    rows = f_rows[t]
                    act.activation(ysb[t % 2][0:rows, :], yacc[0:rows, t, :], ACT.Square,
                                   accum_out=fss[0:rows, t:t + 1]).then_inc(f_sq, 1)

        def moe_vector(dve):
            def tt(out, a, b, op):
                return dve.tensor_tensor(out, a, b, op)

            def rsqrt(y, v, t):
                dve.drain()
                dve.tensor_scalar(y.bitcast(I32), v.bitcast(I32), 1, None, ALU.logical_shift_right)
                dve.drain()
                dve.tensor_scalar(y.bitcast(I32), y.bitcast(I32), -1, MAGIC, ALU.mult, ALU.add)
                for _ in range(3):
                    dve.drain()
                    tt(t, y, y, ALU.mult)
                    dve.drain()
                    dve.scalar_tensor_tensor(t, v, -0.5, t, ALU.mult, ALU.mult)
                    dve.drain()
                    last = dve.scalar_tensor_tensor(y, t, 1.5, y, ALU.add, ALU.mult)
                return last

            dense_done(dve)
            dve.wait_ge(rt_const, N_RT)
            dve.memset(gpad[:], -BIG)
            dve.drain()
            dve.tensor_copy(gpad[:, :, 0:NG], logit[:, :, 0:NG])
            dve.drain()
            for t in range(NT):
                dve.max(m8g[:, t, :], gpad[:, t, :])
            dve.drain()
            for t in range(NT):
                dve.max_index(i8g[:, t, :], m8g[:, t, :], gpad[:, t, :])
            dve.drain()
            dve.tensor_copy(gif[:], i8g[:, :, 0])
            dve.drain()
            tt(ohg[:], io32[:, 0:NG].unsqueeze(1).to_broadcast([P, NT, NG]), gif[:].unsqueeze(2).to_broadcast([P, NT, NG]), ALU.is_equal)
            tt(gd[:], logit[:, :, 0:NG], m8g[:, :, 0:1].to_broadcast([P, NT, NG]), ALU.subtract)
            dve.drain()
            em4 = em[:, :, :].rearrange("p t (g e) -> p (t g) e", e=EG)
            oh4 = ohg[:, :, :].rearrange("p t g -> p (t g)")
            for t in range(NT):
                tt(em[:, t, :].rearrange("p (g e) -> p g e", e=EG), logit[:, t, NG:NR].rearrange("p (g e) -> p g e", e=EG),
                   ohg[:, t, :].unsqueeze(2).to_broadcast([P, NG, EG]), ALU.mult)
            dve.drain()
            dve.tensor_scalar(ohg[:], ohg[:], 1.0, BIG, ALU.subtract, ALU.mult)
            dve.drain()
            tt(em4, em4, oh4.unsqueeze(2).to_broadcast([P, NT * NG, EG]), ALU.add)
            dve.drain()
            for t in range(NT):
                dve.max(m8[:, t, :], em[:, t, :])
            dve.drain()
            for t in range(NT):
                dve.max_index(i8[:, t, :], m8[:, t, :], em[:, t, :])
            tt(gif[:], m8[:, :, 0], m8[:, :, 1], ALU.subtract).then_inc(rt_m, 1)
            dve.drain()
            dve.tensor_copy(ef[:], i8[:, :, 0:2])
            dve.drain()
            for k in range(2):
                tt(oh[:, k], io32[:].unsqueeze(1).to_broadcast([P, NT, NE]), ef[:, :, k:k + 1].to_broadcast([P, NT, NE]), ALU.is_equal)
            dve.drain()
            tt(ohs[:], oh[:, 0], oh[:, 1], ALU.add)
            dve.drain()
            for p0 in range(SMP, P, 32):
                last = dve.memset(ohs[p0:p0 + 32, NT - 1, :], 0.0)
            last.then_inc(oh_ok, 1)
            for k in range(2):
                tt(ohv[:, k], oh[:, k], valf[:, k, :].unsqueeze(2).to_broadcast([P, NT, NE]), ALU.mult)
            dve.drain()
            s = q_wait_ready(dve, "rank")
            rank = q[s][:, 0, 0:NT * NE].rearrange("p (t e) -> p t e", e=NE)
            for k in range(2):
                tt(oh[:, k], oh[:, k], rank, ALU.mult)
            dve.drain()
            for k in range(2):
                last = dve.tensor_reduce(rk[:, k, :], oh[:, k], axis=AX.X, op=ALU.add)
            last.then_inc(q_free[s], 1)
            dve.drain()
            for k in range(2):
                last = dve.scalar_tensor_tensor(dsti[:, k, :], rk[:, k, :], float(NE), ef[:, :, k], ALU.mult, ALU.add)
            last.then_inc(dst_ok, 1)
            for k in range(2):
                last = tt(ohr[:, k], io128[:].unsqueeze(1).to_broadcast([P, NT, P]),
                          rk[:, k, :].unsqueeze(2).to_broadcast([P, NT, P]), ALU.is_equal)
            last.then_inc(ohr_ok, 1)
            s = q_wait_ready(dve, "cnt")
            dve.tensor_copy(cnt[:], q[s][0:NE, 0, 0:1]).then_inc(q_free[s], 1)
            dve.drain()
            dve.tensor_scalar(need[:], thr[:], cnt[:, 0:1], None, ALU.is_lt)
            dve.drain()
            dve.tensor_reduce(rowc[:], need[:], axis=AX.X, op=ALU.add).then_inc(row_ok, 1)
            s = q_wait_ready(dve, "tb")
            dve.tensor_scalar(tb0[:], q[s][:, 0, 0:NE], float(OOB), None, ALU.add).then_inc(q_free[s], 1)
            dve.drain()
            dve.tensor_scalar(tok0[:], tb0[:], TPAD - 1, None, ALU.bitwise_and).then_inc(tok_ok, 1)
            tt(bval[:], bval[:], need[:], ALU.mult)
            s = q_wait_ready(dve, "pos")
            dve.tensor_scalar(posn[:], thr[:], 1.0 / P, q[s][0:NE, 0, 0:1], ALU.mult, ALU.add).then_inc(q_free[s], 1)
            dve.drain()
            dve.tensor_scalar(posn[:], posn[:], 1.0, None, ALU.subtract)
            dve.drain()
            shape = [NE, MAXX, NBLK - 1]
            tt(xeq[:], io16[:].unsqueeze(2).to_broadcast(shape), posn[:].unsqueeze(1).to_broadcast(shape), ALU.is_equal)
            dve.drain()
            tt(xeq[:], xeq[:], bval[:].unsqueeze(1).to_broadcast(shape), ALU.mult)
            dve.drain()
            dve.tensor_reduce(xls[:, 0:MAXX], xeq[:], axis=AX.X, op=ALU.add)
            dve.tensor_copy(xls[:, MAXX:MAXX + 1], rowc[:]).then_inc(xls_ok, 1)
            s = q_wait_ready(dve, "list")
            dve.tensor_copy(xrow[:, 0, :], q[s][0:1, 0, 0:MAXX + 1]).then_inc(q_free[s], 1)
            dve.drain()
            dve.tensor_scalar(xrow[:, 1, :], xrow[:, 0, :], NE - 1, None, ALU.bitwise_and)
            dve.tensor_scalar(xrow[:, 2, :], xrow[:, 0, :], 5, None, ALU.logical_shift_right).then_inc(xrow_ok, 1)
            dve.wait_ge(rt_e, 1)
            dve.tensor_reduce(gsum[:], gd[:], axis=AX.X, op=ALU.add)
            dve.drain()
            dve.reciprocal(gsum[:], gsum[:])
            dve.drain()
            for k in range(2):
                last = tt(wk[:, k, :], wk[:, k, :], gsum[:], ALU.mult)
            last.then_inc(wk_ok, 1)

            def hidden(e):
                dve.wait_ge(m_sg, e + 1)
                if first(e):
                    dve.wait_ge(m_G, e)
                tt(gs[:], hsg[:], z[0][:, 0, :], ALU.mult)
                dve.drain()
                tt(gs[:], gs[:], z[0][:, 1, :], ALU.mult).then_inc(m_g, 1)

            def result(e, s, r=None):
                dve.wait_ge(m_Y, e + 1)
                if r is not None and first(r):
                    dve.wait_ge(m_sc[s], r * 16)
                dve.tensor_copy(ysb[s][:], z[1][:, :, :].rearrange("p b c -> p (b c)")).then_inc(m_y, 1)

            hidden(0)
            hidden(1)
            result(0, 0, 0)
            hidden(2)
            result(1, 1, 0)
            hidden(3)
            result(2, 0, 1)
            with dve.Fori(2, NE // 2) as r:
                hidden(r * 2)
                result(r * 2 - 1, 1, r - 1)
                hidden(r * 2 + 1)
                result(r * 2, 0, r)
            result(NE - 1, 1, NE // 2 - 1)
            n = dve.value_load(xrow[0:1, 0, MAXX:MAXX + 1], min_val=0, max_val=MAXX)
            with dve.If(n > 0):
                with dve.Fori(0, n) as i:
                    dve.wait_ge(o_i, i * 16 + 16)
                    dve.tensor_scalar(xtok[:], xcol[:], TPAD - 1, None, ALU.bitwise_and).then_inc(o_c, 1)
                    hidden(i + NE)
                    dve.wait_ge(m_sc[0], 16 * (NE // 2))
                    result(i + NE, 0)

            dve.wait_ge(f_par, 16 * (4 + NS))
            for p in range(len(pairs_of) + 2):
                for t in pairs_of[p] if p < len(pairs_of) else ():
                    acc = yacc[0:f_rows[t], t, :]
                    dve.wait_ge(f_a, t + 1)
                    dve.scalar_tensor_tensor(acc, yin[0:f_rows[t], t % YS, 1, :], wk[0:f_rows[t], 1, t:t + 1], acc,
                                             ALU.mult, ALU.add).then_inc(f_c, 1)
                for t in pairs_of[p - 1] if 1 <= p <= len(pairs_of) else ():
                    acc = yacc[0:f_rows[t], t, :]
                    dve.wait_ge(f_g, t + 1)
                    tt(acc, acc, x1a[0:f_rows[t], t, :], ALU.add).then_inc(f_sum, 1)
                if p >= 2:
                    ts = pairs_of[p - 2]
                    rows, a, b = f_rows[ts[0]], ts[0], ts[-1] + 1
                    dve.wait_ge(f_sq, b)
                    dve.tensor_scalar(fv[0:rows, a:b], fss[0:rows, a:b], 1.0 / D, EPS, ALU.mult, ALU.add)
                    rsqrt(fy[0:rows, a:b], fv[0:rows, a:b], ft[0:rows, a:b])
                    dve.drain()
                    for t in ts:
                        acc = yacc[0:rows, t, :]
                        dve.scalar_tensor_tensor(acc, acc, fy[0:rows, t:t + 1], fgb[0:rows, :], ALU.mult, ALU.mult).then_inc(f_y, 1)

        w_in_v = w_in[0].rearrange("(k p) c -> p k c", p=P)
        w_br_v = w_branch[0].rearrange("b (k p) c -> p b k c", p=P)
        w_out_v = w_out[0].rearrange("(k p) c -> p k c", p=P)
        ada_v = w_ada[0].rearrange("(k p) c -> p k c", p=P)

        @block.sync
        def _(sp):
            def load(g, u, s, src, kn=KD):
                if first(u) == 0 or first(u) > O0 // 2:
                    if g or first(u):
                        sp.wait_ge(item_mm, item_no(g, u, s) - 1)
                else:
                    n_ = before_wait(sp, split_no(g, u, s) - 1)
                    sp.wait_ge(wlo_ok, n_)
                sp.dma_start(w_raw[s][:, 0:kn, :], src).then_inc(w_in_sem[s], 16)

            def cols_of(name, i):
                return w_in_v[:, :, bass.ds(i * P + COL[name], P)]

            def load_ada(j):
                s = j % 2
                if j >= 2:
                    q_wait_ready(sp, "ada", j - 2)
                sp.dma_start(ada[:, s, :, :], ada_v[:, :, j * 512:(j + 1) * 512]).then_inc(ada_in[s], 16)
                if j >= 2:
                    sp.wait_ge(modr_ok, j - 1)
                sp.dma_start(badar[:, s, :], b_ada[0:1, j * 512:(j + 1) * 512].to_broadcast([9, 512])
                             ).then_inc(bada_in[s], 16)

            for j in range(4):
                load_ada(j)
            for g in range(2):
                load(g, 0, 0, cols_of("a_gt", 0))
                load(g, 0, 1, cols_of("a_val", 0))
                with sp.Fori(1, CW) as i:
                    load(g, i, 0, cols_of("a_gt", i))
                    load(g, i, 1, cols_of("a_val", i))
                for n in range(3 * CW):
                    if g == 0 and n == 2:
                        for j in range(4, 12):
                            load_ada(j)
                    load(g, (C0 + n) // 2, n % 2, cols_of(("c_h", "c_c", "c_b")[n % 3], n // 3))
                with sp.Fori(0, CW) as i:
                    load(g, i + B0 // 2, 0, cols_of("b_v", i))
                    load(g, i + B0 // 2, 1, cols_of("b_u", i))
                for b, n0 in ((NB_C, GC0), (NB_B, GB0), (NB_A, GA0)):
                    with sp.Fori(0, KD) as i:
                        load(g, i + n0 // 2, 0, cols_of("gates", i + b * KD))
                        load(g, i + n0 // 2, 1, w_br_v[:, b, :, bass.ds(i * P, P)], CW)
                load(g, O0 // 2, 0, w_out_v[:, :, 0:P])
                load(g, O0 // 2, 1, w_out_v[:, :, P:2 * P])
                with sp.Fori(1, KD // 2) as i:
                    for s in range(2):
                        load(g, i + O0 // 2, s, w_out_v[:, :, bass.ds(i * (2 * P) + s * P, P)])
            moe_sync(sp)

        @block.gpsimd
        def _(pool):
            def x_load(g, t):
                s, rows = x_slot(g, t), dict(tiles(g))[t]
                if XUSE[g, t]:
                    gl, tl, _ = [k for k in XT if x_slot(*k[:2]) == s][XUSE[g, t] - 1]
                    pool.wait_ge(hlo_ok, XN[gl, tl] + 1)
                pool.dma_start(x_stage(g, t)[0:rows, :], x_rows(g, t)).then_inc(x_in[s], 16)

            pool.memset(ident[:], 0.0).then_inc(consts, 1)
            pool.drain()
            pool.memset(blk64[:], 0.0).then_inc(consts, 1)
            pool.drain()
            pool.memset(blk2[:], 0.0).then_inc(consts, 1)
            pool.drain()
            pool.wait_ge(consts, 3)
            pool.affine_select(out=ident[:], in_=ident[:], compare_op=ALU.not_equal, fill=1.0, base=0,
                               pattern=[[-1, P]], channel_multiplier=1).then_inc(consts, 1)
            pool.drain()
            for h in range(2):
                pool.memset(blk64[64 * h:64 * h + 64, 64 * h:64 * h + 64], 1.0 / 64).then_inc(consts, 1)
                pool.drain()
                pool.memset(blk2[64 * h:64 * h + 64, h:h + 1], 1.0 / 64).then_inc(consts, 1)
                pool.drain()
            pool.memset(a_in[:, :, 0:HA], 0.0).then_inc(consts, 1)
            pool.drain()
            pool.memset(p_in[:, 0:HC], 0.0).then_inc(consts, 1)
            pool.drain()
            pool.memset(wsS[:], 0.0).then_inc(consts, 1)
            pool.drain()
            for t_ in (rs_v, ssq, ssq2, mv, logit):
                pool.memset(t_[:], 1.0).then_inc(consts, 1)
                pool.drain()
            for t in range(PT):
                x_load(0, t)

            def mod_store(j):
                pool.wait_ge(modr_ok, j + 1)
                pool.dma_start(mod_dram[:, j * 512:(j + 1) * 512], modr[:, j % 2, :]).then_inc(mod_out[j % 2], 16)

            mod_store(0)
            mod_store(1)
            pool.wait_ge(par_in, 16 * N_PAR)
            pool.affine_select(out=wsr[:], in_=wsr[:], compare_op=ALU.is_ge, fill=0.0, base=0,
                               pattern=[[0, HEADS], [-1, P]], channel_multiplier=1).then_inc(consts, 1)
            pool.drain()
            pool.memset(tinit[:], OOB).then_inc(rt_const, 1)
            pool.drain()
            pool.memset(tri[:], 1.0).then_inc(rt_const, 1)
            pool.drain()
            pool.memset(oneb[:], 1.0).then_inc(rt_const, 1)
            pool.drain()
            pool.memset(trif[:], 1.0).then_inc(rt_const, 1)
            pool.drain()
            pool.memset(onef[:], 1.0).then_inc(rt_const, 1)
            pool.drain()
            pool.wait_ge(rt_const, 5)
            pool.dma_start(table.rearrange("(p n) o -> p (n o)", p=P), tinit[:]).then_inc(tab_out, 16)
            for m, n in ((tri, P), (trif, NE)):
                pool.affine_select(out=m[:], in_=m[:], compare_op=ALU.is_gt, fill=0.0, base=0,
                                   pattern=[[1, n]], channel_multiplier=-1).then_inc(rt_const, 1)
                pool.drain()
            pool.iota(io32[:], pattern=[[1, NE]], base=0, channel_multiplier=0,
                      allow_small_or_imprecise_dtypes=True).then_inc(rt_const, 1)
            pool.drain()
            pool.iota(io16[:], pattern=[[1, MAXX]], base=0, channel_multiplier=0,
                      allow_small_or_imprecise_dtypes=True).then_inc(rt_const, 1)
            pool.drain()
            pool.iota(thr[:], pattern=[[P, NBLK - 1]], base=P, channel_multiplier=0,
                      allow_small_or_imprecise_dtypes=True).then_inc(rt_const, 1)
            pool.drain()
            pool.iota(bval[:], pattern=[[NE, NBLK - 1]], base=NE, channel_multiplier=1,
                      allow_small_or_imprecise_dtypes=True).then_inc(rt_const, 1)
            pool.drain()
            pool.iota(io128[:], pattern=[[1, P]], base=0, channel_multiplier=0,
                      allow_small_or_imprecise_dtypes=True).then_inc(rt_const, 1)
            pool.drain()
            pool.iota(valf[:], pattern=[[TPAD, 2], [P, NT]], base=-OOB, channel_multiplier=1,
                      allow_small_or_imprecise_dtypes=True).then_inc(rt_const, 1)
            pool.drain()
            pool.iota(vali[:], pattern=[[TPAD, 2], [P, NT]], base=0, channel_multiplier=1).then_inc(rt_const, 1)
            pool.drain()
            for j in range(2, 12):
                mod_store(j)
                if j == 3:
                    pool.wait_ge(aux_ok, 1)
                    pool.wait_ge(consts, N_CONST)
                    for n in range(NS):
                        pool.dma_start(wsS[n * TS:(n + 1) * TS, :, n * TS:(n + 1) * TS],
                                       wsT[0:TS, :, 0:TS]).then_inc(bd_in, 16)

            def tail_out(g, t, rows, s=0):
                r0 = t * P + g * PT * P
                pool.dma_start(x1_dram[bass.ds(r0, rows), :], chunk(xres, t)[0:rows, :]).then_inc(x1_out, 16)
                n_ = before_wait(pool, PT * g + t + 1)
                pool.wait_ge(h2_ok, n_)
                pool.dma_start(h2_dram[bass.ds(r0, rows), :], h2s[s][0:rows, :]
                               ).then_inc(h2_last[s] if g else h2_out, 16)

            def conv_taps(g):
                q_wait_read(pool, "par")
                q_wait_read(pool, "hist")
                pool.wait_ge(z_free[1], slot_use(g, CW - 1) + 1)
                pool.wait_ge(x_sq, (PT, 2 * PT + 1)[g])
                if g:
                    pool.wait_ge(alo_ok, CW)
                pool.wait_ge(hlo_ok, (PT, 2 * PT + 1)[g])
                samples = a_in[:, 2:4, HA + HALF:].rearrange("p c (n t) -> p c n t", t=AS)

                def product(k):
                    for c in range(2):
                        wt, bias = parT[:, 2 + c, k:k + 1], parT[:, 2 + c, PAR_B:PAR_B + 1]
                        parts = [(a_in[:, 2 + c, k:k + HALF], conv[:, 2 + c, 0:HALF] if k == 0 else
                                  xs[:, k % 2, c * HALF:(c + 1) * HALF])]
                        if g:
                            parts.append((samples[:, c, :, k:k + TS], seqs(conv[:, 2 + c, HALF:TM]) if k == 0 else
                                          seqs(tap_s[:, k % 2, c, :])))
                        for x, out in parts:
                            if k == 0:
                                pool.tensor_scalar(out, x, wt, bias, ALU.mult, ALU.add)
                            else:
                                pool.tensor_scalar(out, x, wt, None, ALU.mult)

                product(0)
                product(1)
                for k in range(1, KA):
                    pool.drain()
                    if k + 1 < KA:
                        product(k + 1)
                    if g:
                        sums = conv[:, 2:4, HALF:TM]
                        pool.tensor_tensor(sums, tap_s[:, k % 2, :, :], sums, ALU.add)
                    sums = conv[:, 2:4, 0:HALF]
                    last = pool.tensor_tensor(sums, xs[:, k % 2, :].rearrange("p (c t) -> p c t", c=2), sums, ALU.add)
                last.then_inc(cnvp_ok, 1)
                pool.drain()

            for g in range(2):
                conv_taps(g)
                if g == 1:
                    pool.wait_ge(vn_ok, 2 * PT + 1)
                    pool.dma_start(new_v_sample[0].rearrange("n t c -> (n t) c"), v_tok[0:SMP, PT, :]).then_inc(v_out, 16)
                    pool.dma_start(new_a_sample[0, :, 0:HA - TS, :], state_conv_a[0, :, TS:HA, :]).then_inc(st_out, 16)
                    q_wait_read(pool, "stA")
                    q_wait_read(pool, "stC")
                    pool.dma_start(new_a_prompt[0, 0], xs[0:HA, 0, 0:W]).then_inc(st_out, 16)
                    pool.dma_start(new_c_prompt[0, 0], xs[0:HC, 1, 0:W]).then_inc(st_out, 16)
                    for n in range(NS):
                        pool.dma_start(new_a_sample[0, n, HA - TS:HA, :], xs[n * TS:(n + 1) * TS, 0, W:D]).then_inc(st_out, 16)
                        pool.dma_start(new_c_sample[0, n], xs[n * TS + TS - HC:(n + 1) * TS, 1, W:D]).then_inc(st_out, 16)
                    pool.wait_ge(v_out, 16)
                pool.wait_ge(blo_ok, CW * (g + 1))
                for t, rows in tiles(g):
                    pool.dma_start(xres[0:rows, t, :], x_rows(g, t)).then_inc(xres_in, 16)
                if g == 0:
                    for t, _ in tiles(1):
                        x_load(1, t)
                    for s in range(2):
                        pool.wait_ge(mod_out[s], 16 * 6)
                pool.wait_ge(item_mm, item_no(g, GA0 // 2, 0))
                pool.dma_start(B2[:], mod_dram[0:1, 3 * D:4 * D].to_broadcast([P, D])).then_inc(ab_in, 16)
                pool.dma_start(A2[:], mod_dram[0:1, 4 * D:5 * D].to_broadcast([P, D])).then_inc(ab_in, 16)
                if g:
                    pool.wait_ge(alo_ok, 2 * CW)
                    for k, off in enumerate((3, 4)):
                        for n in range(NS):
                            pool.dma_start(xs_s[n * TS:(n + 1) * TS, k * D:(k + 1) * D],
                                           mod_dram[1 + n:2 + n, off * D:(off + 1) * D].to_broadcast([TS, D])
                                           ).then_inc(abs_in, 16)
                q_wait_read(pool, "oT", g, KD - 1)
                if g == 0:
                    with pool.Fori(0, PT) as t:
                        tail_out(0, t, P)
            for t, rows in tiles(1):
                tail_out(1, t, rows, t % 2)
            moe_gpsimd(pool)

        @block.scalar
        def _(act):
            act.dma_start(crow[0:1, :], c_prompt).then_inc(c_in, 16)
            act.dma_start(crow[1:9, :], c_sample).then_inc(c_in, 16)

            def par(dst, src):
                act.dma_start(dst, src).then_inc(par_in, 16)

            par(parr[0:KA, :], a_dw_w[0])
            par(parr[KA:PAR_B, :], c_conv_w[0])
            for r, v in ((PAR_B, a_dw_b), (PAR_G, a_norm_g), (PAR_S, a_norm_b)):
                par(parr[r:r + 1, :], v)
            par(parr[PAR_H:NPAR, :], state_conv_c[0].rearrange("n h c -> (n h) c"))
            par(n1r[:], norm1_g[0].rearrange("(k p) -> k p", p=P))
            for a in range(2):
                par(hist[:, a, :], state_conv_a[0, a * TS:(a + 1) * TS].rearrange("n h c -> (n h) c"))
            par(wsr[:], b_spatial_w[0].rearrange("h t s -> t h s"))
            for h in range(HEADS):
                par(s_bias[64 * (h % 2):64 * (h % 2) + 64, h // 2, :], b_spatial_b[0, h:h + 1, :].to_broadcast([64, P]))
            par(bn_g[:], b_norm_g.to_broadcast([P, W]))
            par(bn_b[:], b_norm_b.to_broadcast([P, W]))
            par(n2_b[:], norm2_g.to_broadcast([P, D]))
            par(rb[:, 0:NG], b_router_g.to_broadcast([P, NG]))
            par(rb[:, NG:NR], b_router_e.to_broadcast([P, NE]))
            par(rw[:, :, 0:NG], w_router_g[0].rearrange("(k p) c -> p k c", p=P))
            par(rw[:, :, NG:NR], w_router_e[0].rearrange("(k p) c -> p k c", p=P))

            act.wait_ge(c_in, 32)
            act.activation(csig[:], crow[:], ACT.Sigmoid).then_inc(csig_ok, 1)
            def x_square(g, t):
                n, rows = XN[g, t], dict(tiles(g))[t]
                act.wait_ge(x_in[x_slot(g, t)], 16 * (XUSE[g, t] + 1))
                if n == 0:
                    act.wait_ge(consts, N_CONST - 1)
                if n:
                    act.wait_ge(x_sq, n)
                act.activation(x_dump(g)[0:rows, :], x_stage(g, t)[0:rows, :], ACT.Square,
                               accum_out=ssq[0:rows, n:n + 1]).then_inc(x_sq, 1)

            def h_round(g, t):
                rows = dict(tiles(g))[t]
                q_wait_read(act, "xT", g, t)
                if g and t == 0:
                    act.wait_ge(item_mm, item_no(0, O0 // 2, 0))
                act.activation(h_hi[:, :, t * P:t * P + rows], h_wide(g, t)[:, :, 0:rows], ACT.Copy).then_inc(hhi_ok, 1)

            def w_round(g, u, s, kn=KD):
                act.wait_ge(w_in_sem[s], slot_use(g, u) * 16 + 16)
                if g or first(u):
                    act.wait_ge(item_mm, item_no(g, u, s) - 1)
                act.activation(w_hi[s][:, 0:kn, :], w_raw[s][:, 0:kn, :], ACT.Copy).then_inc(whi_ok, 1)

            for t in range(PT):
                x_square(0, t)
            s = q_wait_ready(act, "par")
            act.activation(parT[:], q[s][:, 0, 0:CW * 64].rearrange("p (c n) -> p c n", n=64)[:, :, 0:NPAR],
                           ACT.Copy).then_inc(q_free[s], 1)
            s = q_wait_ready(act, "n1")
            act.activation(n1T[:], q[s][:, 0, 0:KD], ACT.Copy).then_inc(q_free[s], 1)
            s = q_wait_ready(act, "hist")
            for c in range(CW):
                last = act.activation(
                    a_in[:, c, HA + HALF:].rearrange("p (n t) -> p n t", t=AS)[:, :, 0:HA],
                    q[s][:, c // 2, (c % 2) * 240:(c % 2) * 240 + 240].rearrange("p (n h) -> p n h", h=HA), ACT.Copy)
            last.then_inc(q_free[s], 1)
            s = q_wait_ready(act, "ws")
            act.activation(wsT[:], q[s][:, :, :].rearrange("p b (h t) -> p (b h) t", t=P), ACT.Copy).then_inc(q_free[s], 1)
            q_wait_read(act, "par")
            q_wait_read(act, "ws")
            act.activation(p_hist[:], parT[:, :, PAR_H:NPAR], ACT.Copy).then_inc(aux_ok, 1)
            w_round(0, 0, 0)
            w_round(0, 0, 1)
            for t in range(PT):
                h_round(0, t)

            def tail_squares(g):
                q_wait_read(act, "oT", g, KD - 1)
                if g:
                    q_wait_read(act, "lg", 0, PT - 1)
                for t, rows in tiles(g):
                    if t:
                        act.wait_ge(x1_sq, PT * g + t)
                    act.activation(junk[0:rows, :], xres[0:rows, t, :], ACT.Square,
                                   accum_out=ssq2[0:rows, t:t + 1]).then_inc(x1_sq, 1)

            def tail_tile(g, t, rows=P):
                s = q_wait_ready(act, "h2T", g, 0, more=t)
                act.activation(h2T[:, :, 0:rows], q[s][:, :, :].rearrange("p b (k t) -> p (b k) t", t=P)[:, :, 0:rows],
                               ACT.Copy).then_inc(q_free[s], 1)

            for g in range(2):
                T = TG[g]

                def a_chunk(i):
                    act.wait_ge(item_mm, item_no(g, i, 0) + 1)
                    if g or first(i):
                        act.wait_ge(z_free[1], slot_use(g, i))
                    act.activation(tv(sig, g), zv(0, g), ACT.Sigmoid).then_inc(z_free[0], 1)
                    w_round(g, i + 1, 0)
                    if g:
                        tail_tile(0, i)
                    w_round(g, i + 1, 1)

                if g:
                    tail_squares(0)
                a_chunk(0)
                with act.Fori(1, CW) as i:
                    a_chunk(i)

                def c_chunk(i, u, s0):
                    for k in range(3):
                        uk, s = u + (s0 + k) // 2, (s0 + k) % 2
                        if k == 0:
                            act.wait_ge(item_mm, item_no(g, uk, s) + 1)
                            act.activation(tv(chb, g), zv(s, g), ACT.Copy).then_inc(z_free[s], 1)
                        w_round(g, uk + 1, s)
                        if k == 2:
                            act.wait_ge(z_free[s], slot_use(g, uk) + 1)
                            act.activation(chunk(act0_hi, i)[:, 0:T], cv[:, 0:T], ACT.Copy).then_inc(chi_ok, 1)

                if g == 0:
                    q_wait_ready(act, "ada", 11)
                else:
                    act.wait_ge(x1_sq, PT)
                with act.Fori(0, CW // 2) as i:
                    c_chunk(i * 2, i * 3 + C0 // 2, 0)
                    c_chunk(i * 2 + 1, i * 3 + (C0 // 2 + 1), 1)

                def b_item(i, s):
                    n = i * 2 + (2 * CW * g + s)
                    u = i + B0 // 2
                    act.wait_ge(item_mm, item_no(g, u, s) + 1)
                    act.wait_ge(z_free[1 - s], slot_use(g, u) + s)
                    act.activation(tv(gq, g), zv(s, g), ACT.Square).then_inc(gq_ok, 1)
                    act.wait_ge(gt_ok, n + 1)
                    act.activation(gq[:, 0:T], gt[:, 0:T], ACT.Sigmoid).then_inc(gs_ok, 1)

                def b_chunk(i, kn=KD):
                    b_item(i, 0)
                    w_round(g, i + (B0 // 2 + 1), 0)
                    b_item(i, 1)
                    w_round(g, i + (B0 // 2 + 1), 1, kn)
                    s = q_wait_ready(act, "vT", g, 0, more=i)
                    if g:
                        act.activation(v_tok[0:SMP, PT, bass.ds(i * P, P)], q[s][0:SMP, 1, 0:P], ACT.Copy)
                    act.activation(v_tok[:, 0:PT, bass.ds(i * P, P)],
                                   q[s][:, 0, :].rearrange("p (t c) -> p t c", c=P), ACT.Copy).then_inc(q_free[s], 1)

                if g:
                    act.wait_ge(x1_out, 16 * PT)
                with act.Fori(0, CW - 1) as i:
                    b_chunk(i)
                b_chunk(CW - 1, CW)

                def gate(n0, i, k0=KD, k1=CW):
                    u = i + n0 // 2
                    act.wait_ge(item_mm, item_no(g, u, 0) + 1)
                    act.wait_ge(z_free[1], slot_use(g, u))
                    act.activation(tv(sig, g), zv(0, g), ACT.Sigmoid).then_inc(z_free[0], 1)
                    if k0:
                        w_round(g, u + 1, 0, k0)
                        w_round(g, u + 1, 1, k1)

                with act.Fori(0, KD) as i:
                    gate(GC0, i)
                if g == 0:
                    for s in range(2):
                        act.wait_ge(mod_out[s], 16 * 6)
                else:
                    act.wait_ge(h2_out, 16 * PT)
                    q_wait_read(act, "lg", 0, PT - 1)
                act.wait_ge(bb_ok, PT + g * (PT + 1))
                for c in range(CW):
                    act.activation(act1_hi[:, c, 0:T], u_sb[:, c, 0:T], ACT.Copy).then_inc(bhi_ok, 1)
                if g:
                    act.wait_ge(cnvp_ok, 2)
                    for k, rows in ((0, HA), (1, HC)):
                        s = q_wait_ready(act, ("stA", "stC")[k])
                        act.activation(xs[0:rows, k, 0:W], q[s][0:rows, 0, :], ACT.Copy)
                        act.activation(xs[0:SMP, k, W:D], q[s][0:SMP, 1, :], ACT.Copy).then_inc(q_free[s], 1)

                def squares(cs):
                    for c in cs:
                        q_wait_read(act, "mu", g, c)
                        act.activation(a_in[:, c, 0:T], conv[:, c, 0:T], ACT.Square).then_inc(asq_ok, 1)

                def silus(cs):
                    for c in cs:
                        n = CW * g + c
                        q_wait_read(act, "bc", g, c)
                        if n:
                            act.wait_ge(af_ok, n)
                        gain, shift = parT[:, c, PAR_G:PAR_G + 1], parT[:, c, PAR_S:PAR_S + 1]
                        act.activation(gq[:, 0:T], conv[:, c, 0:T], ACT.Sigmoid, bias=shift, scale=gain)
                        act.activation(gt[:, 0:T], conv[:, c, 0:T], ACT.Identity, bias=shift, scale=gain).then_inc(ay_ok, 1)
                        act.wait_ge(af_ok, n + 1)
                        act.activation(act0_hi[:, c, 0:T], conv[:, c, 0:T], ACT.Copy).then_inc(ahi_ok, 1)

                squares(range(CW))
                gate(GB0, 0)
                silus([0, 1])
                gate(GB0, 1)
                silus([2, 3])
                with act.Fori(2, KD) as i:
                    gate(GB0, i)
                with act.Fori(0, KD - 1) as i:
                    gate(GA0, i)
                if g == 0:
                    act.wait_ge(alo_ok, CW)
                    x_square(1, 0)
                    x_square(1, 1)
                gate(GA0, KD - 1, None)

                def out_item(j, s, ready=None):
                    u = j + O0 // 2
                    act.wait_ge(item_mm, item_no(g, u, s) + 1)
                    if first(j) or g:
                        if isinstance(j, int):
                            q_wait_ready(act, "oT", g if j else 0, 2 * j - 2 + s if j else KD - 2 + s)
                        else:
                            q_wait_ready(act, "oT", g, 2 + s, more=j - 2)
                    n = j * 2 + (2 * KD + s)
                    g1 = modT[:, n, 0:1] if isinstance(n, int) else \
                        modT[:, bass.ds(n, 1), 0:1].rearrange("p a b -> p (a b)")
                    for src, t0, t1 in zparts(s, g):
                        last = act.activation(ot[s][:, t0:t1], src, ACT.Copy, scale=g1)
                    last.then_inc(ot_ok if g else z_free[s], 1)

                if g == 0:
                    h_round(1, 0)
                    h_round(1, 1)
                    x_square(1, 2)
                    x_square(1, 3)
                out_item(0, 0)
                out_item(0, 1)
                if g == 0:
                    h_round(1, 2)
                    h_round(1, 3)
                    x_square(1, 4)
                out_item(1, 0)
                out_item(1, 1)
                if g == 0:
                    h_round(1, 4)
                with act.Fori(2, KD // 2) as j:
                    out_item(j, 0)
                    out_item(j, 1)
                if g == 0:
                    w_round(1, 0, 0)
                    w_round(1, 0, 1)
            tail_squares(1)
            for t, rows in tiles(1):
                tail_tile(1, t, rows)
            moe_scalar(act)

        @block.vector
        def _(dve):
            def tt(out, a, b, op):
                return dve.tensor_tensor(out, a, b, op)

            def rsqrt(y, v, t):
                dve.drain()
                dve.tensor_scalar(y.bitcast(I32), v.bitcast(I32), 1, None, ALU.logical_shift_right)
                dve.drain()
                dve.tensor_scalar(y.bitcast(I32), y.bitcast(I32), -1, MAGIC, ALU.mult, ALU.add)
                for _ in range(3):
                    dve.drain()
                    tt(t, y, y, ALU.mult)
                    dve.drain()
                    dve.scalar_tensor_tensor(t, v, -0.5, t, ALU.mult, ALU.mult)
                    dve.drain()
                    last = dve.scalar_tensor_tensor(y, t, 1.5, y, ALU.add, ALU.mult)
                return last

            def w_low(g, u, s, kn=KD):
                dve.wait_ge(whi_ok, split_no(g, u, s) + 1)
                tt(w_lo[s][:, 0:kn, :], w_raw[s][:, 0:kn, :], w_hi[s][:, 0:kn, :].bitcast(F32),
                   ALU.subtract).then_inc(wlo_ok, 1)

            def x_norm(g, t):
                n, rows = XN[g, t], dict(tiles(g))[t]
                dve.wait_ge(x_sq, n + 1)
                v, y, tm = (a[0:rows, n:n + 1] for a in (nv, ny, nt_))
                dve.tensor_scalar(v, ssq[0:rows, n:n + 1], 1.0 / D, EPS, ALU.mult, ALU.add)
                rsqrt(y, v, tm)
                dve.drain()
                x = x_stage(g, t)[0:rows, :]
                dve.tensor_scalar(x, x, y, None, ALU.mult).then_inc(x_n, 1)

            def x_mod(g, t):
                h = h_wide(g, t)
                s = q_wait_ready(dve, "xT", g, t)
                ps = q[s][:, :, :].rearrange("p b (k t) -> p (b k) t", t=P)
                if t < PT:
                    for k in range(KD):
                        last = dve.tensor_scalar(h[:, k, :], ps[:, k, :], modT[:, KD + k, 0:1], modT[:, k, 0:1],
                                                 ALU.mult, ALU.add)
                else:
                    for k in range(KD):
                        dve.tensor_tensor(seqs(h[:, k, 0:SMP]), seqs(ps[:, k, 0:SMP]),
                                          modT[:, KD + k, 1:9].unsqueeze(2).to_broadcast([P, NS, TS]), ALU.mult)
                    dve.drain()
                    for k in range(KD):
                        last = dve.tensor_tensor(seqs(h[:, k, 0:SMP]), seqs(h[:, k, 0:SMP]),
                                                 modT[:, k, 1:9].unsqueeze(2).to_broadcast([P, NS, TS]), ALU.add)
                last.then_inc(q_free[s], 1)

            def x_low(g, t):
                rows = dict(tiles(g))[t]
                dve.wait_ge(hhi_ok, XN[g, t] + 1)
                if g and t == 0:
                    dve.wait_ge(item_mm, item_no(0, O0 // 2, 0))
                tt(h_lo[:, :, t * P:t * P + rows], h_wide(g, t)[:, :, 0:rows],
                   h_hi[:, :, t * P:t * P + rows].bitcast(F32), ALU.subtract).then_inc(hlo_ok, 1)

            dve.wait_ge(csig_ok, 1)
            tt(crow[:], crow[:], csig[:], ALU.mult).then_inc(sic_ok, 1)
            s = q_wait_ready(dve, "sic")
            dve.tensor_copy(sicT[:], q[s][:, 0, 0:KD * 9].rearrange("p (k n) -> p k n", n=9)).then_inc(q_free[s], 1)

            def ada_piece(j):
                dve.wait_ge(bada_in[j % 2], 16 * (j // 2 + 1))
                if j >= 2:
                    dve.wait_ge(mod_out[j % 2], 16 * (j // 2))
                    if j - 2 < 6:
                        q_wait_ready(dve, "modT", j - 2)
                s = q_wait_ready(dve, "ada", j)
                tt(modr[:, j % 2, :], q[s][0:9, 0, :], badar[:, j % 2, :], ALU.add).then_inc(modr_ok, 1)
                if j < 6:
                    s = q_wait_ready(dve, "modT", j)
                    dve.tensor_copy(modT[:, 4 * j:4 * j + 4, :], q[s][:, 0, 0:36].rearrange("p (k n) -> p k n", n=9)
                                    ).then_inc(q_free[s], 1)

            ada_piece(0)
            x_norm(0, 0)
            x_norm(0, 1)
            ada_piece(1)
            x_norm(0, 2)
            x_norm(0, 3)
            ada_piece(2)
            ada_piece(3)
            q_wait_read(dve, "n1")
            dve.drain()
            for k in range(KD):
                dve.tensor_scalar(modT[:, KD + k, :], modT[:, KD + k, :], 1.0, n1T[:, k:k + 1], ALU.add, ALU.mult)
            dve.drain()
            w_low(0, 0, 0)
            w_low(0, 0, 1)
            x_mod(0, 0)
            for t in range(PT):
                if t + 1 < PT:
                    x_mod(0, t + 1)
                x_low(0, t)

            def smp_in(ap, seq, h):
                return ap.rearrange("p (n t) -> p n t", t=seq)[:, :, h:seq]

            def conv_taps(g, c, k, first_tap=False):
                src = chunk(a_in, c)
                wt = parT[:, c, k:k + 1] if isinstance(k, int) else parT[:, c, bass.ds(k, 1)]
                parts = [(conv[:, c, 0:HALF], src[:, bass.ds(k, HALF)])]
                if g:
                    parts.append((seqs(conv[:, c, HALF:TM]),
                                  src[:, HA + HALF:].rearrange("p (n t) -> p n t", t=AS)[:, :, bass.ds(k, TS)]))
                dve.drain()
                for out, x in parts:
                    if first_tap:
                        last = dve.tensor_scalar(out, x, wt, parT[:, c, PAR_B:PAR_B + 1], ALU.mult, ALU.add)
                    else:
                        last = dve.scalar_tensor_tensor(out, x, wt, out, ALU.mult, ALU.add)
                return last

            def tail_h2(g, t, rows=P, factors=None):
                scale, shift = factors or (A2, B2)
                if g == 0:
                    if first(t):
                        dve.wait_ge(h2_out, t * 16)
                        q_wait_ready(dve, "h2T", g, 0, more=t - 1)
                elif t < 2:
                    dve.wait_ge(h2_out, PT * 16)
                    q_wait_ready(dve, "h2T", 0, PT - 1)
                else:
                    dve.wait_ge(h2_last[t % 2], t // 2 * 16)
                    q_wait_ready(dve, "h2T", 1, t - 2)
                h = h2s[t % 2 if g else 0][0:rows, :]
                y = r2y[0:rows, t:t + 1] if isinstance(t, int) else r2y[0:rows, bass.ds(t, 1)]
                dve.scalar_tensor_tensor(h, chunk(xres, t)[0:rows, :], y, scale[0:rows, :], ALU.mult, ALU.mult)
                dve.drain()
                tt(h, h, shift[0:rows, :], ALU.add).then_inc(h2_ok, 1)

            def tail_logits(g, t, rows=P):
                s = q_wait_ready(dve, "lg", g, 0, more=t)
                dst = logit[0:rows, t + PT * g, :] if isinstance(t, int) else \
                    logit[0:rows, bass.ds(t, 1), :].rearrange("p o r -> p (o r)")
                tt(dst, q[s][0:rows, 0, 0:NR], rb[0:rows, :], ALU.add).then_inc(q_free[s], 1)

            def tail_start(g):
                nt = PT + g
                dve.wait_ge(x1_sq, PT + g * (PT + 1))
                dve.tensor_scalar(nv[:, 0:nt], ssq2[:, 0:nt], 1.0 / D, EPS, ALU.mult, ALU.add)
                rsqrt(r2y[:, 0:nt], nv[:, 0:nt], nt_[:, 0:nt])
                dve.wait_ge(ab_in, 32 * (g + 1))
                dve.scalar_tensor_tensor(A2[:], A2[:], 1.0, n2_b[:], ALU.add, ALU.mult)
                dve.drain()

            for g in range(2):
                T = TG[g]

                def a_chunk(i):
                    w_low(g, i + 1, 0)
                    s = 1
                    dve.wait_ge(z_free[0], slot_use(g, i) + 1)
                    dve.wait_ge(item_mm, item_no(g, i, 1) + 1)
                    dst = chunk(a_in, i)
                    if g:
                        tt(smp_in(dst[:, HA + HALF:], AS, HA), seqs(zsample(s)), seqs(sig[:, HALF:TM]), ALU.mult)
                    for src, t0, t1 in zparts(s, g):
                        last = tt(dst[:, HA + t0:HA + t1], src, sig[:, t0:t1], ALU.mult)
                    last.then_inc(z_free[1], 1)
                    w_low(g, i + 1, 1)
                    dve.drain()
                    tail = chunk(a_tail, i)
                    dve.tensor_copy(tail[:, 0:HA], dst[:, HALF:HALF + HA])
                    if g:
                        dve.tensor_copy(seqs(tail[:, HA:]), smp_in(dst[:, HA + HALF:], AS, HA))

                if g == 0:
                    dve.wait_ge(consts, N_CONST)
                    q_wait_read(dve, "hist")
                    dve.wait_ge(aux_ok, 1)
                    a_chunk(0)
                    with dve.Fori(1, CW) as i:
                        a_chunk(i)
                    for j in range(4, 12):
                        ada_piece(j)
                else:
                    dve.tensor_copy(a_in[:, :, 0:HA], a_tail[:, :, 0:HA])
                    tail_start(0)
                    tail_h2(0, 0)
                    a_chunk(0)
                    tail_logits(0, 0)
                    with dve.Fori(1, CW) as i:
                        tail_h2(0, i)
                        a_chunk(i)
                        tail_logits(0, i)

                def c_chunk(i, u, s0, taps):
                    (uh, sh), (uc, sc), (ub, sb_) = ((u + (s0 + k) // 2, (s0 + k) % 2) for k in range(3))
                    w_low(g, uh + 1, sh)
                    if g:
                        dve.tensor_copy(p_in[:, 0:HC], chunk(p_tail, i)[:, 0:HC])
                        dve.tensor_copy(p_in[:, HC + HALF:].rearrange("p (n t) -> p n t", t=CS)[:, :, 0:HC],
                                        chunk(p_hist, i).rearrange("p (n h) -> p n h", h=HC))
                    for k in taps[:len(taps) // 2]:
                        conv_taps(g, 0, k)
                    dve.wait_ge(z_free[sh], slot_use(g, uh) + 1)
                    dve.wait_ge(item_mm, item_no(g, uc, sc) + 1)
                    if g:
                        tt(smp_in(p_in[:, HC + HALF:], CS, HC), seqs(zsample(sc)), seqs(chb[:, HALF:TM]), ALU.mult)
                    for src, t0, t1 in zparts(sc, g):
                        last = tt(p_in[:, HC + t0:HC + t1], src, chb[:, t0:t1], ALU.mult)
                    last.then_inc(z_free[sc], 1)
                    w_low(g, uc + 1, sc)
                    dve.drain()
                    tail = chunk(p_tail, i)
                    dve.tensor_copy(tail[:, 0:HC], p_in[:, HALF:HALF + HC])
                    if g:
                        dve.tensor_copy(seqs(tail[:, HC:]), smp_in(p_in[:, HC + HALF:], CS, HC))
                    for k in range(KC):
                        dve.drain()
                        wt = parT[:, i, KA + k:KA + k + 1] if isinstance(i, int) else \
                            parT[:, bass.ds(i, 1), KA + k:KA + k + 1].rearrange("p a b -> p (a b)")
                        parts = [(cv[:, 0:HALF], p_in[:, k:k + HALF])]
                        if g:
                            parts.append((seqs(cv[:, HALF:TM]),
                                          p_in[:, HC + HALF:].rearrange("p (n t) -> p n t", t=CS)[:, :, k:k + TS]))
                        for out, x in parts:
                            if k == 0:
                                dve.tensor_scalar(out, x, wt, None, ALU.mult)
                            else:
                                dve.scalar_tensor_tensor(out, x, wt, out, ALU.mult, ALU.add)
                    for k in taps[len(taps) // 2:]:
                        conv_taps(g, 0, k)
                    dve.drain()
                    dve.wait_ge(item_mm, item_no(g, ub, sb_) + 1)
                    tt(tv(cv, g), zv(sb_, g), tv(cv, g), ALU.mult).then_inc(z_free[sb_], 1)
                    w_low(g, ub + 1, sb_)
                    n = i + CW * g
                    dve.wait_ge(chi_ok, n + 1)
                    tt(chunk(act0_lo, i)[:, 0:T], cv[:, 0:T], chunk(act0_hi, i)[:, 0:T].bitcast(F32),
                       ALU.subtract).then_inc(clo_ok, 1)

                conv_taps(g, 0, 0, True)
                with dve.Fori(0, CW // 2) as i:
                    c_chunk(i * 2, i * 3 + C0 // 2, 0, [i * 15 + (1 + k) for k in range(8)])
                    c_chunk(i * 2 + 1, i * 3 + (C0 // 2 + 1), 1, [i * 15 + (9 + k) for k in range(7)])

                def b_item(i, s):
                    n = i * 2 + (2 * CW * g + s)
                    u = i + B0 // 2
                    dve.wait_ge(gq_ok, n + 1)
                    dve.tensor_scalar(gt[:, 0:T], gq[:, 0:T], GELU1, GELU0, ALU.mult, ALU.add)
                    dve.drain()
                    tt(tv(gt, g), tv(gt, g), zv(s, g), ALU.mult).then_inc(gt_ok, 1)
                    dst = vT
                    if s == 0:
                        if first(i):
                            q_wait_ready(dve, "vT", g, 0, more=i - 1)
                        out = tv(vT, g)
                    else:
                        out = tv(chunk(u_sb, i), g)
                    dve.wait_ge(gs_ok, n + 1)
                    tt(out, tv(gq, g), zv(s, g), ALU.mult).then_inc(z_free[s], 1)

                def b_chunk(i, taps, kn=KD):
                    b_item(i, 0)
                    w_low(g, i + (B0 // 2 + 1), 0)
                    for k in taps[:1]:
                        conv_taps(g, 1, k)
                    b_item(i, 1)
                    w_low(g, i + (B0 // 2 + 1), 1, kn)
                    for k in taps[1:]:
                        conv_taps(g, 1, k)

                if g:
                    dve.wait_ge(x1_out, 16 * PT)
                conv_taps(g, 1, 0, True)
                b_chunk(0, range(1, 3))
                with dve.Fori(1, CW - 1) as i:
                    b_chunk(i, [i * 2 + (k + 1) for k in range(2)])
                b_chunk(CW - 1, range(7, 9), CW)

                def gated(b, n0, i, k0=KD, k1=CW):
                    u = i + n0 // 2
                    if k0:
                        w_low(g, u + 1, 0, k0)
                    dve.wait_ge(z_free[0], slot_use(g, u) + 1)
                    dve.wait_ge(item_mm, item_no(g, u, 1) + 1)
                    m = chunk(macc, i)
                    if b == NB_C:
                        tt(tv(m, g), zv(1, g), tv(sig, g), ALU.mult).then_inc(z_free[1], 1)
                    else:
                        tt(tv(chb, g), zv(1, g), tv(sig, g), ALU.mult).then_inc(z_free[1], 1)
                        dve.drain()
                        last = tt(m[:, 0:T], m[:, 0:T], chb[:, 0:T], ALU.add)
                        if b == NB_A:
                            last.then_inc(macc_ok, 1)
                    if k0:
                        w_low(g, u + 1, 1, k1)

                def v_stats():
                    nt = PT + g
                    for t, rows in tiles(g):
                        dve.bn_stats(bn6[0:rows, t, :], v_tok[0:rows, t, :])
                    dve.drain()
                    for t, rows in tiles(g):
                        dve.bn_aggr(mv[0:rows, t, :], bn6[0:rows, t, :])
                    dve.drain()
                    dve.tensor_scalar(nv[:, 0:nt], mv[:, 0:nt, 1:2].rearrange("p t o -> p (t o)"), EPS, None, ALU.add)
                    rsqrt(ny[:, 0:nt], nv[:, 0:nt], nt_[:, 0:nt])

                def v_norm(ts):
                    vs = [(t, r, v_tok[0:r, t, :]) for t, r in tiles(g) if t in ts]
                    dve.drain()
                    for t, r, v in vs:
                        dve.tensor_scalar(v, v, mv[0:r, t, 0:1], ny[0:r, t:t + 1], ALU.subtract, ALU.mult)
                    dve.drain()
                    for t, r, v in vs:
                        tt(v, v, bn_g[0:r, :], ALU.mult)
                    dve.drain()
                    for t, r, v in vs:
                        tt(v, v, bn_b[0:r, :], ALU.add).then_inc(vn_ok, 1)

                def spatial(t, rows=P):
                    s = q_wait_ready(dve, "sp", g, t)
                    tmp = gt[:, 0:CW * rows].rearrange("p (c t) -> p c t", t=rows)
                    src = q[s][:, 0, 0:CW * rows].rearrange("p (c t) -> p c t", t=rows)
                    ut = u_sb[:, :, t * P:t * P + rows]
                    dve.drain()
                    if rows == P:
                        tt(tmp, src, s_bias[:], ALU.add).then_inc(q_free[s], 1)
                    else:
                        for c in range(CW):
                            last = tt(seqs(tmp[:, c, :]), seqs(src[:, c, :]),
                                      s_bias[:, c:c + 1, 0:TS].to_broadcast([P, NS, TS]), ALU.add)
                        last.then_inc(q_free[s], 1)
                    dve.drain()
                    tt(ut, tmp, ut, ALU.mult).then_inc(bb_ok, 1)

                q_wait_read(dve, "vT", g, CW - 1)
                k = 9
                for i in range(KD):
                    gated(NB_C, GC0, i)
                    if i == 0:
                        v_stats()
                    elif i < 3:
                        v_norm((2 * i - 2, 2 * i - 1))
                    elif i == 3:
                        if g:
                            v_norm((PT,))
                    else:
                        spatial(i - PT)
                    for _ in range((0, 0, 0, 5, 4, 4, 4, 5)[i]):
                        last = conv_taps(g, 1, k)
                        k += 1
                assert k == KA
                last.then_inc(cnv_ok, 1)
                if g:
                    spatial(PT, SMP)
                for c in range(CW):
                    dve.wait_ge(bhi_ok, CW * g + c + 1)
                    tt(act1_lo[:, c, 0:T], u_sb[:, c, 0:T], act1_hi[:, c, 0:T].bitcast(F32), ALU.subtract).then_inc(blo_ok, 1)

                def parts_of(c, s):
                    p = [(conv[:, c, 0:HALF], q[s][:, 0, :])]
                    return p + [(conv[:, c, HALF:TM], q[s][:, 1, 0:SMP])] if g else p

                def centre(cs):
                    for c in cs:
                        s = q_wait_ready(dve, "mu", g, c)
                        for x, m in parts_of(c, s):
                            last = tt(x, x, m, ALU.subtract)
                        last.then_inc(q_free[s], 1)

                def inverse(cs):
                    c0, n = cs[0], len(cs)
                    s = q_wait_ready(dve, "var", g)
                    src = q[s][:, 0, 0:CW * (PT + 1) * 2].rearrange("p (c t j) -> p c t j", c=CW, j=2)
                    cc = slice(c0, c0 + n)
                    for t, rows in tiles(g):
                        last = dve.tensor_scalar(rs_v[0:rows, cc, t, :], src[0:rows, cc, t, :], EPS, None, ALU.add)
                    last.then_inc(q_free[s], 1)
                    a, b, c = (x[:, cc, :, :].rearrange("p c t j -> p (c t j)") for x in (rs_y, rs_v, rs_t))
                    rsqrt(a, b, c).then_inc(rs_ok, 1)

                def normed(c):
                    s = q_wait_ready(dve, "bc", g, c)
                    for x, m in parts_of(c, s):
                        last = tt(x, x, m, ALU.mult)
                    last.then_inc(q_free[s], 1)

                def silus(cs):
                    normed(cs[0])
                    for c in cs:
                        n = CW * g + c
                        if c + 1 in cs:
                            normed(c + 1)
                        dve.wait_ge(ay_ok, n + 1)
                        tt(conv[:, c, 0:T], gq[:, 0:T], gt[:, 0:T], ALU.mult).then_inc(af_ok, 1)
                        dve.wait_ge(ahi_ok, n + 1)
                        tt(act0_lo[:, c, 0:T], conv[:, c, 0:T], act0_hi[:, c, 0:T].bitcast(F32), ALU.subtract).then_inc(alo_ok, 1)

                centre(range(CW))
                gated(NB_B, GB0, 0)
                inverse(range(CW))
                silus([0, 1])
                gated(NB_B, GB0, 1)
                silus([2, 3])
                with dve.Fori(2, KD) as i:
                    gated(NB_B, GB0, i)
                with dve.Fori(0, KD - 1) as i:
                    gated(NB_A, GA0, i)
                if g == 0:
                    x_norm(1, 0)
                    x_norm(1, 1)
                gated(NB_A, GA0, KD - 1, None)

                def out_smp(j, s):
                    if not g:
                        return
                    n = j * 2 + (2 * KD + s)
                    g1 = modT[:, n, 1:9] if isinstance(n, int) else modT[:, bass.ds(n, 1), 1:9].rearrange("p a b -> p (a b)")
                    dve.wait_ge(ot_ok, j * 2 + (s + 1))
                    tt(seqs(ot[s][:, HALF:TM]), seqs(zsample(s)), g1.unsqueeze(2).to_broadcast([P, NS, TS]),
                       ALU.mult).then_inc(z_free[s], 1)

                def out_add(j, s):
                    if isinstance(j, int):
                        q_wait_ready(dve, "oT", g, 2 * j + s)
                    else:
                        q_wait_ready(dve, "oT", g, 2 + s, more=j - 1)
                    lo = j * (2 * P) + s * P
                    x = xres[:, 0:PT, bass.ds(lo, P)]
                    if g:
                        xx = xres[0:SMP, PT, bass.ds(lo, P)]
                        tt(xx, q[s][0:SMP, 1, 0:P], xx, ALU.add)
                    tt(x, q[s][:, 0, :].rearrange("p (t c) -> p t c", c=P), x, ALU.add).then_inc(q_free[s], 1)

                if g == 0:
                    x_mod(1, 0)
                    x_mod(1, 1)
                    x_low(1, 0)
                    x_low(1, 1)
                    x_norm(1, 2)
                    x_norm(1, 3)
                    x_mod(1, 2)
                    x_mod(1, 3)
                    x_low(1, 2)
                    x_low(1, 3)
                    x_norm(1, 4)
                out_smp(0, 0)
                out_smp(0, 1)
                dve.wait_ge(xres_in, 16 * (PT + g * (PT + 1)))
                out_add(0, 0)
                out_smp(1, 0)
                out_add(0, 1)
                out_smp(1, 1)
                if g == 0:
                    x_mod(1, 4)
                    x_low(1, 4)
                with dve.Fori(2, KD // 2) as j:
                    out_add(j - 1, 0)
                    out_smp(j, 0)
                    out_add(j - 1, 1)
                    out_smp(j, 1)
                out_add(KD // 2 - 1, 0)
                out_add(KD // 2 - 1, 1)
                if g == 0:
                    w_low(1, 0, 0)
                    w_low(1, 0, 1)
            tail_start(1)
            for t in range(PT):
                tail_h2(1, t)
                if t:
                    tail_logits(1, t - 1)
            dve.wait_ge(abs_in, 16 * 2 * NS)
            scale = xs_s[:, D:2 * D]
            dve.scalar_tensor_tensor(scale, scale, 1.0, n2_b[0:SMP, :], ALU.add, ALU.mult)
            dve.drain()
            tail_h2(1, PT, SMP, (scale, xs_s[:, 0:D]))
            tail_logits(1, PT - 1)
            tail_logits(1, PT, SMP)
            moe_vector(dve)

        @block.tensor
        def _(pe):
            def transposed(out, src):
                n = src.shape[0]
                return pe.transpose(out, src, ident[0:n, 0:n])

            pe.wait_ge(consts, N_CONST - 1)
            s = q_wait_free(pe, "sic")
            pe.wait_ge(sic_ok, 1)
            for k in range(KD):
                last = transposed(q[s][:, 0, 9 * k:9 * k + 9], crow[:, k * P:(k + 1) * P])
            last.then_inc(q_ready[s], 1)
            q_wait_read(pe, "sic")

            def ada_piece(j):
                if j:
                    pe.wait_ge(modr_ok, j)
                pe.wait_ge(ada_in[j % 2], 16 * (j // 2 + 1))
                for k in range(KD):
                    last = pe.matmul(q[0][0:9, 0, :], sicT[:, k, :], ada[:, j % 2, k, :], start=(k == 0), stop=(k == KD - 1))
                last.then_inc(q_ready[0], 1)
                if j < 6:
                    s = q_wait_free(pe, "modT", j)
                    pe.wait_ge(modr_ok, j + 1)
                    for c in range(4):
                        last = transposed(q[s][:, 0, 9 * c:9 * c + 9], modr[:, j % 2, c * P:(c + 1) * P])
                    last.then_inc(q_ready[s], 1)

            for j in range(4):
                ada_piece(j)
            pe.wait_ge(par_in, 16 * N_PAR)
            pe.wait_ge(consts, N_CONST)
            s = q_wait_free(pe, "par")
            pe.wait_ge(modr_ok, 4)
            for c in range(CW):
                last = transposed(q[s][:, 0, c * 64:c * 64 + NPAR], parr[:, c * P:(c + 1) * P])
            last.then_inc(q_ready[s], 1)
            s = q_wait_free(pe, "n1")
            transposed(q[s][:, 0, 0:KD], n1r[:]).then_inc(q_ready[s], 1)
            s = q_wait_free(pe, "hist")
            for c in range(CW):
                for a in range(2):
                    o = (c % 2) * 240 + a * HA * TS
                    last = transposed(q[s][:, c // 2, o:o + HA * TS], hist[:, a, c * P:(c + 1) * P])
            last.then_inc(q_ready[s], 1)
            s = q_wait_free(pe, "ws")
            for h in range(HEADS):
                last = transposed(q[s][:, h // 4, (h % 4) * P:(h % 4 + 1) * P], wsr[:, h, :])
            last.then_inc(q_ready[s], 1)

            def x_transpose(g, t):
                s, rows = q_wait_free(pe, "xT", g, t), dict(tiles(g))[t]
                pe.wait_ge(x_n, XN[g, t] + 1)
                for k in range(KD):
                    last = transposed(q[s][:, k // 4, (k % 4) * P:(k % 4) * P + rows], x_stage(g, t)[0:rows, k * P:(k + 1) * P])
                last.then_inc(q_ready[s], 1)

            pe.wait_ge(modr_ok, 4)
            for t in range(PT):
                x_transpose(0, t)

            def item(g, u, s, hi, lo, kn=KD):
                pe.wait_ge(wlo_ok, split_no(g, u, s) + 1)
                if g or first(u):
                    pe.wait_ge(z_free[s], slot_use(g, u))
                for b, t0, t1 in halves(g):
                    for k in range(kn):
                        out = z[s][:, b, 0:t1 - t0]
                        pe.matmul(out, w_hi[s][:, k, :], hi[:, k, t0:t1], start=(k == 0), stop=False)
                        pe.matmul(out, w_hi[s][:, k, :], lo[:, k, t0:t1], start=False, stop=False)
                        last = pe.matmul(out, w_lo[s][:, k, :], hi[:, k, t0:t1], start=False, stop=(k == kn - 1))
                last.then_inc(item_mm, 1)

            def h2_transpose(g, t, rows=P):
                s, n0 = QUSE["h2T", g, 0]
                pe.wait_ge(q_free[s], n0 + t)
                pe.wait_ge(h2_ok, t + (PT * g + 1))
                for k in range(KD):
                    last = transposed(q[s][:, k // 4, (k % 4) * P:(k % 4) * P + rows],
                                      h2s[t % 2 if g else 0][0:rows, k * P:(k + 1) * P])
                last.then_inc(q_ready[s], 1)

            def logits(g, t, rows=P):
                q_wait_read(pe, "h2T", g, 0, more=t)
                s, n0 = QUSE["lg", g, 0]
                pe.wait_ge(q_free[s], n0 + t)
                for k in range(KD):
                    last = pe.matmul(q[s][0:rows, 0, 0:NR], h2T[:, k, 0:rows], rw[:, k, :], start=(k == 0), stop=(k == KD - 1))
                last.then_inc(q_ready[s], 1)

            for g in range(2):
                T = TG[g]
                pe.wait_ge(hlo_ok, PT + g * (PT + 1))
                item(g, 0, 0, h_hi, h_lo)
                if g:
                    h2_transpose(0, 0)
                item(g, 0, 1, h_hi, h_lo)
                if g:
                    logits(0, 0)
                with pe.Fori(1, CW) as i:
                    item(g, i, 0, h_hi, h_lo)
                    if g:
                        h2_transpose(0, i)
                    item(g, i, 1, h_hi, h_lo)
                    if g:
                        logits(0, i)
                if g == 0:
                    for j in range(4, 12):
                        if j == 4:
                            q_wait_free(pe, "ada", 4)
                        ada_piece(j)
                    pe.wait_ge(modr_ok, 12)
                with pe.Fori(0, CW // 2) as i:
                    for k in range(6):
                        item(g, i * 3 + (C0 // 2 + k // 2), k % 2, h_hi, h_lo)

                def v_chunk(i):
                    item(g, i + B0 // 2, 0, h_hi, h_lo)
                    item(g, i + B0 // 2, 1, h_hi, h_lo)
                    s, n0 = QUSE["vT", g, 0]
                    pe.wait_ge(q_free[s], i + n0)
                    pe.wait_ge(z_free[0], slot_use(g, i + B0 // 2) + 1)
                    for t, rows in tiles(g):
                        last = transposed(q[s][0:rows, t // PT, (t % PT) * P:(t % PT) * P + P], vT[:, t * P:t * P + rows])
                    last.then_inc(q_ready[s], 1)

                with pe.Fori(0, CW) as i:
                    v_chunk(i)

                def pairs(n0, lo, hi_, xh, xl):
                    if hi_ == lo + 1:
                        item(g, lo + n0 // 2, 0, h_hi, h_lo)
                        item(g, lo + n0 // 2, 1, xh, xl, CW)
                        return
                    with pe.Fori(lo, hi_) as i:
                        item(g, i + n0 // 2, 0, h_hi, h_lo)
                        item(g, i + n0 // 2, 1, xh, xl, CW)

                pe.wait_ge(clo_ok, CW * (g + 1))
                pairs(GC0, 0, PT, act0_hi, act0_lo)
                def spatial(t, rows=P):
                    s = q_wait_free(pe, "sp", g, t)
                    pe.wait_ge(vn_ok, PT + g * (PT + 1))
                    if t == PT:
                        pe.wait_ge(bd_in, 16 * NS)
                    for h in range(HEADS):
                        ws = wsT[:, h, :] if t < PT else wsS[:, h, :]
                        last = pe.matmul(q[s][64 * (h % 2):64 * (h % 2) + 64, 0, (h // 2) * rows:(h // 2 + 1) * rows],
                                         v_tok[0:rows, t, 64 * h:64 * h + 64], ws, start=True, stop=True)
                    last.then_inc(q_ready[s], 1)

                spatial(0)
                for i in range(PT, KD):
                    if i - PT + 1 < PT:
                        spatial(i - PT + 1)
                    elif g:
                        spatial(PT, SMP)
                    pairs(GC0, i, i + 1, act0_hi, act0_lo)
                if g:
                    for name, src, n in (("stA", a_tail, HA), ("stC", p_tail, HC)):
                        s = q_wait_free(pe, name)
                        for c in range(CW):
                            transposed(q[s][0:n, 0, c * P:(c + 1) * P], src[:, c, 0:n])
                            last = transposed(q[s][0:SMP, 1, c * P:(c + 1) * P], src[:, c, n:n + SMP])
                        last.then_inc(q_ready[s], 1)

                def mean(c):
                    s = q_wait_free(pe, "mu", g, c)
                    pe.wait_ge(cnv_ok if c < 2 else cnvp_ok, g + 1)
                    last = pe.matmul(q[s][:, 0, :], blk64[:], conv[:, c, 0:HALF], start=True, stop=True)
                    if g:
                        last = pe.matmul(q[s][:, 1, 0:SMP], blk64[:], conv[:, c, HALF:TM], start=True, stop=True)
                    last.then_inc(q_ready[s], 1)

                def variance(cs):
                    s = q_wait_free(pe, "var", g)
                    for c in cs:
                        pe.wait_ge(asq_ok, CW * g + c + 1)
                        for t, rows in tiles(g):
                            o = (c * (PT + 1) + t) * 2
                            last = pe.matmul(q[s][0:rows, 0, o:o + 2], a_in[:, c, t * P:t * P + rows], blk2[:], start=True, stop=True)
                    last.then_inc(q_ready[s], 1)

                def spread(c):
                    s = q_wait_free(pe, "bc", g, c)
                    pe.wait_ge(rs_ok, g + 1)
                    for t, rows in tiles(g):
                        for j in range(2):
                            last = pe.matmul(q[s][64 * j:64 * j + 64, t // PT, (t % PT) * P:(t % PT) * P + rows],
                                             rs_y[0:rows, c, t, j:j + 1].to_broadcast([rows, 64]),
                                             ident[0:rows, 0:rows], start=True, stop=True)
                    last.then_inc(q_ready[s], 1)

                for c in range(CW):
                    mean(c)
                item(g, GB0 // 2, 0, h_hi, h_lo)
                variance(range(CW))
                pe.wait_ge(blo_ok, CW * (g + 1))
                item(g, GB0 // 2, 1, act1_hi, act1_lo, CW)
                spread(0)
                spread(1)
                pairs(GB0, 1, 2, act1_hi, act1_lo)
                spread(2)
                spread(3)
                pairs(GB0, 2, KD, act1_hi, act1_lo)
                item(g, GA0 // 2, 0, h_hi, h_lo)
                pe.wait_ge(alo_ok, CW * (g + 1))
                item(g, GA0 // 2, 1, act0_hi, act0_lo, CW)
                pairs(GA0, 1, KD, act0_hi, act0_lo)

                def out_item(j, s):
                    u = j + O0 // 2
                    pe.wait_ge(w_in_sem[s], slot_use(g, u) * 16 + 16)
                    pe.wait_ge(z_free[s], slot_use(g, u))
                    for b, t0, t1 in halves(g):
                        for k in range(KD):
                            last = pe.matmul(z[s][:, b, 0:t1 - t0], w_raw[s][:, k, :], macc[:, k, t0:t1],
                                             start=(k == 0), stop=(k == KD - 1))
                    last.then_inc(item_mm, 1)

                def out_transpose(j, s):
                    if isinstance(j, int):
                        q_wait_free(pe, "oT", g, 2 * j + s)
                    else:
                        pe.wait_ge(q_free[s], QUSE["oT", g, 2 + s][1] + (j - 1))
                    pe.wait_ge(z_free[s], slot_use(g, j + O0 // 2) + 1)
                    for t, rows in tiles(g):
                        last = transposed(q[s][0:rows, t // PT, (t % PT) * P:(t % PT) * P + P], ot[s][:, t * P:t * P + rows])
                    last.then_inc(q_ready[s], 1)

                if g == 0:
                    x_transpose(1, 0)
                    x_transpose(1, 1)
                pe.wait_ge(macc_ok, KD * (g + 1))
                out_item(0, 0)
                out_item(0, 1)
                if g == 0:
                    x_transpose(1, 2)
                    x_transpose(1, 3)
                out_transpose(0, 0)
                out_item(1, 0)
                out_transpose(0, 1)
                out_item(1, 1)
                if g == 0:
                    x_transpose(1, 4)
                with pe.Fori(2, KD // 2) as j:
                    out_transpose(j - 1, 0)
                    out_item(j, 0)
                    out_transpose(j - 1, 1)
                    out_item(j, 1)
                out_transpose(KD // 2 - 1, 0)
                out_transpose(KD // 2 - 1, 1)
            for t, rows in tiles(1):
                h2_transpose(1, t, rows)
                logits(1, t, rows)
            moe_tensor(pe)


_INS = ["x_prompt", "x_sample", "c_prompt", "c_sample", "state_conv_a", "state_conv_c", "norm1_g", "norm2_g",
        "w_ada", "b_ada", "w_in", "a_dw_w", "a_dw_b", "a_norm_g", "a_norm_b", "b_norm_g", "b_norm_b",
        "b_spatial_w", "b_spatial_b", "c_conv_w", "w_branch", "w_out", "w_router_g", "b_router_g",
        "w_router_e", "b_router_e", "w1", "w3", "w2", "final_norm_g"]
_OUTS = [(1, SEQ, D), (NS, TS, D), (1, 1, HA, W), (1, 1, HC, W), (1, NS, HA, W), (1, NS, HC, W), (1, NS, TS, W)]


def kernel(**inputs):
    import concourse.bacc as _bacc
    from concourse.bass_utils import run_bass_kernel_spmd as _run

    nc = _bacc.Bacc("TRN2", target_bir_lowering=False, num_devices=1)
    arrays, args = {}, []
    for name in _INS:
        a = np.ascontiguousarray(inputs[name])
        arrays[f"in_{name}_dram"] = a
        args.append(nc.dram_tensor(f"in_{name}_dram", a.shape, mybir.dt.from_np(a.dtype), kind="ExternalInput").ap())
    for i, shape in enumerate(_OUTS):
        args.append(nc.dram_tensor(f"out_{i}_dram", shape, F32, kind="ExternalOutput").ap())
    build(nc, *args)
    r = _run(nc, [arrays], core_ids=[0])
    return tuple(r.results[0][f"out_{i}_dram"] for i in range(len(_OUTS)))
```
